# Optimizing a Trainium2 kernel written in Bass

```python
import jax, jax.numpy as jnp
from jax import lax
import numpy as np
import math

D_MODEL = 1024
BATCH = 1
SEQ = 256
DEPTH = 1

HEAD_DIM = 64
D_MIX = D_MODEL
N_HEADS_A = (D_MIX // 2) // HEAD_DIM
N_KV_A = 2
N_HEADS_B = (D_MIX // 2) // HEAD_DIM
DILATED_CONFIGS = ((128, 1), (512, 4), (2048, 16))
Q_BLOCK = 128
GRID_W = 64
ROPE_THETA = 10000.0
D_FF = 2816
EPS = 1e-6
NEG_INF = -1e30

A_Q = N_HEADS_A * HEAD_DIM
A_KV = N_KV_A * HEAD_DIM
B_QKV = N_HEADS_B * HEAD_DIM
QKV_COLS = A_Q + 2 * A_KV + 3 * B_QKV
QKV_SPLITS = (A_Q, A_Q + A_KV, A_Q + 2 * A_KV, A_Q + 2 * A_KV + B_QKV, A_Q + 2 * A_KV + 2 * B_QKV)


def _rmsnorm(x, g):
    xf = x.astype(jnp.float32)
    r = lax.rsqrt(jnp.mean(xf * xf, axis=-1, keepdims=True) + EPS)
    return (xf * r * g.astype(jnp.float32)).astype(x.dtype)

def _rope_angles(pos, dim):
    freqs = ROPE_THETA ** (-jnp.arange(0, dim, 2, dtype=jnp.float32) / dim)
    return pos.astype(jnp.float32)[:, None] * freqs[None, :]

def _apply_rope(x, ang):
    xf = x.astype(jnp.float32)
    x1, x2 = jnp.split(xf, 2, axis=-1)
    cos = jnp.cos(ang)[None, :, None, :]
    sin = jnp.sin(ang)[None, :, None, :]
    return jnp.concatenate([x1 * cos - x2 * sin, x2 * cos + x1 * sin], axis=-1).astype(x.dtype)

def _apply_axial_rope(x, ang_row, ang_col):
    xr, xc = jnp.split(x, 2, axis=-1)
    return jnp.concatenate([_apply_rope(xr, ang_row), _apply_rope(xc, ang_col)], axis=-1)

def _swiglu(x, w_gate, w_up, w_down):
    return (jax.nn.silu(x @ w_gate) * (x @ w_up)) @ w_down

def _gqa_dense_blocked(q, k, v):
    B, S, Hq, D = q.shape
    Hkv = k.shape[2]
    G = Hq // Hkv
    nq = S // Q_BLOCK
    scale = D ** -0.5
    qb = q.reshape(B, nq, Q_BLOCK, Hkv, G, D).transpose(1, 0, 2, 3, 4, 5)

    def block(qi):
        s = jnp.einsum('bqkgd,bskd->bkgqs', qi, k, preferred_element_type=jnp.float32) * scale
        p = jax.nn.softmax(s, axis=-1)
        o = jnp.einsum('bkgqs,bskd->bqkgd', p.astype(v.dtype), v, preferred_element_type=jnp.float32)
        return o.astype(v.dtype)

    o = lax.map(block, qb)
    return o.transpose(1, 0, 2, 3, 4, 5).reshape(B, S, Hq, D)

def _dilated_window_partial(q, k, v, window, dilation):
    B, S, H, D = q.shape
    span = (window // 2) // dilation
    L = S // dilation
    blk = span
    nb = -(-L // blk)
    Lp = nb * blk
    scale = D ** -0.5

    def strided(x):
        return x.reshape(B, L, dilation, H, D).transpose(0, 2, 1, 3, 4)

    qs = jnp.pad(strided(q), ((0, 0), (0, 0), (0, Lp - L), (0, 0), (0, 0)))
    kv_pad = ((0, 0), (0, 0), (blk, Lp - L + blk), (0, 0), (0, 0))
    ks = jnp.pad(strided(k), kv_pad).reshape(B, dilation, nb + 2, blk, H, D)
    vs = jnp.pad(strided(v), kv_pad).reshape(B, dilation, nb + 2, blk, H, D)
    qb = qs.reshape(B, dilation, nb, blk, H, D)
    kw = jnp.concatenate([ks[:, :, :-2], ks[:, :, 1:-1], ks[:, :, 2:]], axis=3)
    vw = jnp.concatenate([vs[:, :, :-2], vs[:, :, 1:-1], vs[:, :, 2:]], axis=3)

    qpos = jnp.arange(nb)[:, None] * blk + jnp.arange(blk)[None, :]
    kpos = jnp.arange(nb)[:, None] * blk + jnp.arange(3 * blk)[None, :] - blk
    diff = kpos[:, None, :] - qpos[:, :, None]
    valid = (jnp.abs(diff) <= span) & (kpos[:, None, :] >= 0) & (kpos[:, None, :] < L)

    s = jnp.einsum('brcihe,brcjhe->brchij', qb, kw, preferred_element_type=jnp.float32) * scale
    s = jnp.where(valid[None, None, :, None], s, NEG_INF)
    m = jnp.max(s, axis=-1)
    p = jnp.exp(s - m[..., None])
    l = jnp.sum(p, axis=-1)
    o = jnp.einsum('brchij,brcjhe->brcihe', p.astype(vw.dtype), vw, preferred_element_type=jnp.float32)

    o = o.reshape(B, dilation, Lp, H, D)[:, :, :L].transpose(0, 2, 1, 3, 4).reshape(B, S, H, D)

    def unstride_stat(a):
        a = a.transpose(0, 1, 2, 4, 3).reshape(B, dilation, Lp, H)[:, :, :L]
        return a.transpose(0, 2, 1, 3).reshape(B, S, H)

    return o, unstride_stat(m), unstride_stat(l)

def _dilated_mixture(q, k, v):
    parts = [_dilated_window_partial(q, k, v, w, d) for (w, d) in DILATED_CONFIGS]
    m_all = jnp.max(jnp.stack([p[1] for p in parts], axis=0), axis=0)
    num = jnp.zeros(q.shape, jnp.float32)
    den = jnp.zeros(q.shape[:3], jnp.float32)
    for o_i, m_i, l_i in parts:
        w_i = jnp.exp(m_i - m_all)
        num = num + w_i[..., None] * o_i
        den = den + w_i * l_i
    return (num / den[..., None]).astype(q.dtype)

def first_inputs(seed: int = 0) -> dict:
    key = jax.random.key(seed)
    ks = jax.random.split(key, 18)
    f32 = jnp.float32

    def w(k, shape, fan_in):
        return jax.random.normal(k, shape, f32) * (fan_in ** -0.5)

    def gain(k, dim):
        return 1.0 + 0.02 * jax.random.normal(k, (DEPTH, dim), f32)

    return {
        "x": jax.random.normal(ks[0], (BATCH, SEQ, D_MODEL), f32),
        "ffn1_pre_g": gain(ks[1], D_MODEL),
        "ffn1_post_g": gain(ks[2], D_MODEL),
        "ffn1_w_gate": w(ks[3], (DEPTH, D_MODEL, D_FF), D_MODEL),
        "ffn1_w_up": w(ks[4], (DEPTH, D_MODEL, D_FF), D_MODEL),
        "ffn1_w_down": w(ks[5], (DEPTH, D_FF, D_MODEL), D_FF),
        "mix_pre_g": gain(ks[6], D_MODEL),
        "mix_post_g": gain(ks[7], D_MODEL),
        "w_qkv": w(ks[8], (DEPTH, D_MODEL, QKV_COLS), D_MODEL),
        "q_norm_g": gain(ks[9], HEAD_DIM),
        "k_norm_g": gain(ks[10], HEAD_DIM),
        "w_out": w(ks[11], (DEPTH, D_MIX, D_MODEL), D_MIX),
        "ffn2_pre_g": gain(ks[12], D_MODEL),
        "ffn2_post_g": gain(ks[13], D_MODEL),
        "ffn2_w_gate": w(ks[14], (DEPTH, D_MODEL, D_FF), D_MODEL),
        "ffn2_w_up": w(ks[15], (DEPTH, D_MODEL, D_FF), D_MODEL),
        "ffn2_w_down": w(ks[16], (DEPTH, D_FF, D_MODEL), D_FF),
    }

def first_block(x, ffn1_pre_g, ffn1_post_g, ffn1_w_gate, ffn1_w_up, ffn1_w_down,
              mix_pre_g, mix_post_g, w_qkv, q_norm_g, k_norm_g, w_out,
              ffn2_pre_g, ffn2_post_g, ffn2_w_gate, ffn2_w_up, ffn2_w_down):
    B, S, _ = x.shape
    ROWS = S // GRID_W
    pos = jnp.arange(S, dtype=jnp.int32)
    row = jnp.repeat(jnp.arange(ROWS, dtype=jnp.int32), GRID_W)
    col = jnp.tile(jnp.arange(GRID_W, dtype=jnp.int32), ROWS)
    ang_row = _rope_angles(row, HEAD_DIM // 2)
    ang_col = _rope_angles(col, HEAD_DIM // 2)
    ang_1d = _rope_angles(pos, HEAD_DIM)

    for l in range(DEPTH):
        f = _swiglu(_rmsnorm(x, ffn1_pre_g[l]), ffn1_w_gate[l], ffn1_w_up[l], ffn1_w_down[l])
        x = x + 0.5 * _rmsnorm(f, ffn1_post_g[l])

        h = _rmsnorm(x, mix_pre_g[l])
        qkv = h @ w_qkv[l]
        qa, ka, va, qb, kb, vb = jnp.split(qkv, QKV_SPLITS, axis=-1)

        qa = _rmsnorm(qa.reshape(B, S, N_HEADS_A, HEAD_DIM), q_norm_g[l])
        ka = _rmsnorm(ka.reshape(B, S, N_KV_A, HEAD_DIM), k_norm_g[l])
        va = va.reshape(B, S, N_KV_A, HEAD_DIM)
        qa = _apply_axial_rope(qa, ang_row, ang_col)
        ka = _apply_axial_rope(ka, ang_row, ang_col)
        out_a = _gqa_dense_blocked(qa, ka, va)

        qb = _apply_rope(qb.reshape(B, S, N_HEADS_B, HEAD_DIM), ang_1d)
        kb = _apply_rope(kb.reshape(B, S, N_HEADS_B, HEAD_DIM), ang_1d)
        vb = vb.reshape(B, S, N_HEADS_B, HEAD_DIM)
        out_b = _dilated_mixture(qb, kb, vb)

        heads = jnp.concatenate([out_a.reshape(B, S, A_Q), out_b.reshape(B, S, B_QKV)], axis=-1)
        x = x + _rmsnorm(heads @ w_out[l], mix_post_g[l])

        f = _swiglu(_rmsnorm(x, ffn2_pre_g[l]), ffn2_w_gate[l], ffn2_w_up[l], ffn2_w_down[l])
        x = x + 0.5 * _rmsnorm(f, ffn2_post_g[l])
    return x


DEPTH_2 = 2

RG_WIDTH = 512
RG_HEADS = 8
RG_HEAD_DIM = RG_WIDTH // RG_HEADS
RG_CONV = 4
RG_C = 8.0
SB_HEADS = 8
SB_HEAD_DIM = 64
SB_WIDTH = SB_HEADS * SB_HEAD_DIM
SB_QBLOCK = 128
AB_IN = 2 * RG_WIDTH + 3 * SB_WIDTH
AB_MIX = RG_WIDTH + SB_WIDTH

S5_WIDTH = 512
S5_GROUP = 16
S5_GROUPS = S5_WIDTH // S5_GROUP
S5_STATE = 64
MOBA_HEADS = 4
MOBA_HEAD_DIM = 128
MOBA_WIDTH = MOBA_HEADS * MOBA_HEAD_DIM
MOBA_BLOCK = 256
MOBA_TOPK = 3
MOBA_QCHUNK = 32
CD_IN = S5_WIDTH + 3 * MOBA_WIDTH
CD_MIX = S5_WIDTH + MOBA_WIDTH

FFN_HIDDEN = ((8 * D_MODEL + 3 * 256 - 1) // (3 * 256)) * 256
N_EVEN = (DEPTH_2 + 1) // 2
N_ODD = DEPTH_2 // 2


def rms_norm(x, g):
    xf = x.astype(jnp.float32)
    y = xf * lax.rsqrt(jnp.mean(xf * xf, axis=-1, keepdims=True) + EPS)
    return (y * g.astype(jnp.float32)).astype(x.dtype)

def swiglu(h, w_gate, w_up, w_down):
    return (jax.nn.silu(h @ w_gate) * (h @ w_up)) @ w_down

def alibi_slopes(n_heads):
    return 2.0 ** (-8.0 * jnp.arange(1, n_heads + 1, dtype=jnp.float32) / n_heads)

def rglru_branch(xr, gate, conv_w, conv_b, wa, ba, wx, bx, lam):
    f32 = jnp.float32
    B_, S_, _ = xr.shape
    xc = lax.conv_general_dilated(xr, conv_w, window_strides=(1,), padding=[(RG_CONV - 1, 0)],
                                  dimension_numbers=('NWC', 'WIO', 'NWC'),
                                  feature_group_count=RG_WIDTH) + conv_b
    xh = xc.reshape(B_, S_, RG_HEADS, RG_HEAD_DIM)
    r = jax.nn.sigmoid(jnp.einsum('bshi,hij->bshj', xh, wa) + ba).reshape(B_, S_, RG_WIDTH)
    i = jax.nn.sigmoid(jnp.einsum('bshi,hij->bshj', xh, wx) + bx).reshape(B_, S_, RG_WIDTH)
    log_a = (-RG_C * r.astype(f32)) * jax.nn.softplus(-lam.astype(f32))
    a = jnp.exp(log_a)
    b = jnp.sqrt(-jnp.expm1(2.0 * log_a)) * (i * xc).astype(f32)

    def combine(l, rr):
        a_l, b_l = l
        a_r, b_r = rr
        return a_r * a_l, a_r * b_l + b_r

    _, h = lax.associative_scan(combine, (a, b), axis=1)
    return h.astype(xr.dtype) * jax.nn.gelu(gate)

def stick_breaking_attention(q, k, v):
    f32 = jnp.float32
    S_ = q.shape[2]
    scale = SB_HEAD_DIM ** -0.5
    outs = []
    for blk in range(S_ // SB_QBLOCK):
        q0 = blk * SB_QBLOCK
        kend = q0 + SB_QBLOCK
        z = jnp.einsum('bhqd,bhkd->bhqk', q[:, :, q0:kend], k[:, :, :kend]).astype(f32) * scale
        q_pos = q0 + jnp.arange(SB_QBLOCK)
        k_pos = jnp.arange(kend)
        past = k_pos[None, :] < q_pos[:, None]
        log_keep = jnp.where(past, jax.nn.log_sigmoid(-z), 0.0)
        later = lax.cumsum(log_keep, axis=3, reverse=True) - log_keep
        w = jnp.where(past, jnp.exp(jax.nn.log_sigmoid(z) + later), 0.0)
        outs.append(jnp.einsum('bhqk,bhkd->bhqd', w.astype(v.dtype), v[:, :, :kend]))
    return jnp.concatenate(outs, axis=2)

def s5_branch(u, lam_re, lam_im, log_dt, b_re, b_im, c_re, c_im, d_skip, glu_w, glu_b):
    f32 = jnp.float32
    B_, S_, _ = u.shape
    uf = u.astype(f32).reshape(B_, S_, S5_GROUPS, S5_GROUP)
    dt = jnp.exp(log_dt.astype(f32))[:, None]
    lr, li = lam_re.astype(f32), lam_im.astype(f32)
    mag = jnp.exp(lr * dt)
    ab_re, ab_im = mag * jnp.cos(li * dt), mag * jnp.sin(li * dt)
    den = lr * lr + li * li
    nr, ni = ab_re - 1.0, ab_im
    f_re = (nr * lr + ni * li) / den
    f_im = (ni * lr - nr * li) / den
    br, bi = b_re.astype(f32), b_im.astype(f32)
    bb_re = f_re[..., None] * br - f_im[..., None] * bi
    bb_im = f_re[..., None] * bi + f_im[..., None] * br
    bu_re = jnp.einsum('bsgp,gnp->bsgn', uf, bb_re)
    bu_im = jnp.einsum('bsgp,gnp->bsgn', uf, bb_im)
    a_re = jnp.broadcast_to(ab_re, (1, S_) + ab_re.shape)
    a_im = jnp.broadcast_to(ab_im, (1, S_) + ab_im.shape)

    def combine(l, r):
        ar_l, ai_l, br_l, bi_l = l
        ar_r, ai_r, br_r, bi_r = r
        return (ar_r * ar_l - ai_r * ai_l,
                ar_r * ai_l + ai_r * ar_l,
                ar_r * br_l - ai_r * bi_l + br_r,
                ar_r * bi_l + ai_r * br_l + bi_r)

    _, _, x_re, x_im = lax.associative_scan(combine, (a_re, a_im, bu_re, bu_im), axis=1)
    y = (jnp.einsum('bsgn,gpn->bsgp', x_re, c_re.astype(f32))
         - jnp.einsum('bsgn,gpn->bsgp', x_im, c_im.astype(f32)))
    y = y.reshape(B_, S_, S5_WIDTH) + d_skip.astype(f32) * u.astype(f32)
    y = jax.nn.gelu(y)
    y = y * jax.nn.sigmoid(y @ glu_w.astype(f32) + glu_b.astype(f32))
    return y.astype(u.dtype)

def moba_attention(q, k, v):
    f32 = jnp.float32
    B_, H_, S_, hd = q.shape
    n_blk = -(-S_ // MOBA_BLOCK)
    s_pad = n_blk * MOBA_BLOCK
    pad = [(0, 0), (0, 0), (0, s_pad - S_), (0, 0)]
    q, k, v = jnp.pad(q, pad), jnp.pad(k, pad), jnp.pad(v, pad)
    k_blocks = k.reshape(B_, H_, n_blk, MOBA_BLOCK, hd)
    v_blocks = v.reshape(B_, H_, n_blk, MOBA_BLOCK, hd)
    k_mean = jnp.mean(k_blocks.astype(f32), axis=3)
    gate = jnp.einsum('bhsd,bhnd->bhsn', q.astype(f32), k_mean)
    q_blk = jnp.arange(s_pad) // MOBA_BLOCK
    fully_past = jnp.arange(n_blk)[None, :] < q_blk[:, None]
    gate = jnp.where(fully_past, gate, -jnp.inf)
    n_sel = min(MOBA_TOPK, n_blk)
    _, sel = lax.top_k(gate, n_sel)

    n_chunk = s_pad // MOBA_QCHUNK
    q_c = q.reshape(B_, H_, n_chunk, MOBA_QCHUNK, hd).transpose(2, 0, 1, 3, 4)
    sel_c = sel.reshape(B_, H_, n_chunk, MOBA_QCHUNK, n_sel).transpose(2, 0, 1, 3, 4)
    gather = jax.vmap(jax.vmap(lambda blocks, idx: blocks[idx]))
    slopes = alibi_slopes(H_)[None, :, None, None]
    scale = hd ** -0.5
    in_blk = jnp.arange(MOBA_BLOCK)
    n_s = n_sel * MOBA_BLOCK

    def chunk(args):
        c, qc, sc = args
        t = c * MOBA_QCHUNK + jnp.arange(MOBA_QCHUNK)
        own = (c * MOBA_QCHUNK) // MOBA_BLOCK
        k_sel = gather(k_blocks, sc).reshape(B_, H_, MOBA_QCHUNK, n_s, hd)
        v_sel = gather(v_blocks, sc).reshape(B_, H_, MOBA_QCHUNK, n_s, hd)
        k_own = lax.dynamic_slice_in_dim(k, own * MOBA_BLOCK, MOBA_BLOCK, axis=2)
        v_own = lax.dynamic_slice_in_dim(v, own * MOBA_BLOCK, MOBA_BLOCK, axis=2)
        s_pos_sel = (sc[..., None] * MOBA_BLOCK + in_blk).reshape(B_, H_, MOBA_QCHUNK, n_s)
        ok_sel = jnp.repeat(jnp.arange(n_sel) < own, MOBA_BLOCK)
        s_pos_own = own * MOBA_BLOCK + in_blk
        ok_own = s_pos_own[None, :] <= t[:, None]
        sc_sel = (jnp.einsum('bhqd,bhqkd->bhqk', qc, k_sel).astype(f32) * scale
                  - slopes * (t[:, None] - s_pos_sel).astype(f32))
        sc_sel = jnp.where(ok_sel, sc_sel, -jnp.inf)
        sc_own = (jnp.einsum('bhqd,bhkd->bhqk', qc, k_own).astype(f32) * scale
                  - slopes * (t[:, None] - s_pos_own[None, :]).astype(f32))
        sc_own = jnp.where(ok_own, sc_own, -jnp.inf)
        p = jax.nn.softmax(jnp.concatenate([sc_sel, sc_own], axis=-1), axis=-1).astype(v.dtype)
        return (jnp.einsum('bhqk,bhqkd->bhqd', p[..., :n_s], v_sel)
                + jnp.einsum('bhqk,bhkd->bhqd', p[..., n_s:], v_own))

    out = lax.map(chunk, (jnp.arange(n_chunk), q_c, sel_c))
    return out.transpose(1, 2, 0, 3, 4).reshape(B_, H_, s_pad, hd)[:, :, :S_]

def ab_mixer(h, w_in, conv_w, conv_b, wa, ba, wx, bx, lam, w_out):
    B_, S_, _ = h.shape
    proj = h @ w_in
    xr, gate, q, k, v = jnp.split(
        proj, [RG_WIDTH, 2 * RG_WIDTH, 2 * RG_WIDTH + SB_WIDTH, 2 * RG_WIDTH + 2 * SB_WIDTH], axis=-1)
    y_rg = rglru_branch(xr, gate, conv_w, conv_b, wa, ba, wx, bx, lam)
    heads = lambda t: t.reshape(B_, S_, SB_HEADS, SB_HEAD_DIM).transpose(0, 2, 1, 3)
    y_sb = stick_breaking_attention(heads(q), heads(k), heads(v))
    y_sb = y_sb.transpose(0, 2, 1, 3).reshape(B_, S_, SB_WIDTH).astype(y_rg.dtype)
    return jnp.concatenate([y_rg, y_sb], axis=-1) @ w_out

def cd_mixer(h, w_in, lam_re, lam_im, log_dt, b_re, b_im, c_re, c_im, d_skip, glu_w, glu_b, w_out):
    B_, S_, _ = h.shape
    proj = h @ w_in
    u, q, k, v = jnp.split(proj, [S5_WIDTH, S5_WIDTH + MOBA_WIDTH, S5_WIDTH + 2 * MOBA_WIDTH], axis=-1)
    y_s5 = s5_branch(u, lam_re, lam_im, log_dt, b_re, b_im, c_re, c_im, d_skip, glu_w, glu_b)
    heads = lambda t: t.reshape(B_, S_, MOBA_HEADS, MOBA_HEAD_DIM).transpose(0, 2, 1, 3)
    y_mb = moba_attention(heads(q), heads(k), heads(v))
    y_mb = y_mb.transpose(0, 2, 1, 3).reshape(B_, S_, MOBA_WIDTH).astype(y_s5.dtype)
    return jnp.concatenate([y_s5, y_mb], axis=-1) @ w_out

def second_inputs(seed: int = 0) -> dict:
    key = jax.random.key(seed)
    ks = iter(jax.random.split(key, 32))
    f32 = jnp.float32
    NE, NO = N_EVEN, N_ODD
    G, N, P = S5_GROUPS, S5_STATE, S5_GROUP

    def nrm(shape, scale):
        return jax.random.normal(next(ks), shape, f32) * scale

    def gain(shape):
        return 1.0 + 0.01 * jax.random.normal(next(ks), shape, f32)

    x = jax.random.normal(next(ks), (BATCH, SEQ, D_MODEL), f32)
    ab_norm = gain((NE, D_MODEL))
    ab_w_in = nrm((NE, D_MODEL, AB_IN), D_MODEL ** -0.5)
    ab_conv_w = nrm((NE, RG_CONV, 1, RG_WIDTH), RG_CONV ** -0.5)
    ab_conv_b = nrm((NE, RG_WIDTH), 0.01)
    ab_gate_a_w = nrm((NE, RG_HEADS, RG_HEAD_DIM, RG_HEAD_DIM), RG_HEAD_DIM ** -0.5)
    ab_gate_a_b = nrm((NE, RG_HEADS, RG_HEAD_DIM), 0.01)
    ab_gate_x_w = nrm((NE, RG_HEADS, RG_HEAD_DIM, RG_HEAD_DIM), RG_HEAD_DIM ** -0.5)
    ab_gate_x_b = nrm((NE, RG_HEADS, RG_HEAD_DIM), 0.01)
    a_c = jax.random.uniform(next(ks), (NE, RG_WIDTH), f32, 0.9, 0.999)
    a0 = a_c ** (1.0 / RG_C)
    ab_lambda = jnp.log(a0) - jnp.log1p(-a0)
    ab_w_out = nrm((NE, AB_MIX, D_MODEL), AB_MIX ** -0.5)

    cd_norm = gain((NO, D_MODEL))
    cd_w_in = nrm((NO, D_MODEL, CD_IN), D_MODEL ** -0.5)
    cd_lam_re = -0.5 + nrm((NO, G, N), 0.01)
    cd_lam_im = math.pi * jnp.arange(N, dtype=f32) + nrm((NO, G, N), 0.01)
    cd_log_dt = jax.random.uniform(next(ks), (NO, G), f32, math.log(1e-3), math.log(1e-1))
    cd_b_re = nrm((NO, G, N, P), (2.0 * P) ** -0.5)
    cd_b_im = nrm((NO, G, N, P), (2.0 * P) ** -0.5)
    cd_c_re = nrm((NO, G, P, N), N ** -0.5)
    cd_c_im = nrm((NO, G, P, N), N ** -0.5)
    cd_d = nrm((NO, S5_WIDTH), 1.0)
    cd_glu_w = nrm((NO, S5_WIDTH, S5_WIDTH), S5_WIDTH ** -0.5)
    cd_glu_b = nrm((NO, S5_WIDTH), 0.01)
    cd_w_out = nrm((NO, CD_MIX, D_MODEL), CD_MIX ** -0.5)

    ffn_norm = gain((DEPTH_2, D_MODEL))
    ffn_w_gate = nrm((DEPTH_2, D_MODEL, FFN_HIDDEN), D_MODEL ** -0.5)
    ffn_w_up = nrm((DEPTH_2, D_MODEL, FFN_HIDDEN), D_MODEL ** -0.5)
    ffn_w_down = nrm((DEPTH_2, FFN_HIDDEN, D_MODEL), FFN_HIDDEN ** -0.5)
    final_norm = gain((D_MODEL,))
    return {"x": x, "ab_norm": ab_norm, "ab_w_in": ab_w_in, "ab_conv_w": ab_conv_w,
            "ab_conv_b": ab_conv_b, "ab_gate_a_w": ab_gate_a_w, "ab_gate_a_b": ab_gate_a_b,
            "ab_gate_x_w": ab_gate_x_w, "ab_gate_x_b": ab_gate_x_b, "ab_lambda": ab_lambda,
            "ab_w_out": ab_w_out, "cd_norm": cd_norm, "cd_w_in": cd_w_in,
            "cd_lam_re": cd_lam_re, "cd_lam_im": cd_lam_im, "cd_log_dt": cd_log_dt,
            "cd_b_re": cd_b_re, "cd_b_im": cd_b_im, "cd_c_re": cd_c_re, "cd_c_im": cd_c_im,
            "cd_d": cd_d, "cd_glu_w": cd_glu_w, "cd_glu_b": cd_glu_b, "cd_w_out": cd_w_out,
            "ffn_norm": ffn_norm, "ffn_w_gate": ffn_w_gate, "ffn_w_up": ffn_w_up,
            "ffn_w_down": ffn_w_down, "final_norm": final_norm}

def second_block(x, ab_norm, ab_w_in, ab_conv_w, ab_conv_b, ab_gate_a_w, ab_gate_a_b,
              ab_gate_x_w, ab_gate_x_b, ab_lambda, ab_w_out, cd_norm, cd_w_in,
              cd_lam_re, cd_lam_im, cd_log_dt, cd_b_re, cd_b_im, cd_c_re, cd_c_im,
              cd_d, cd_glu_w, cd_glu_b, cd_w_out, ffn_norm, ffn_w_gate, ffn_w_up,
              ffn_w_down, final_norm):
    for layer in range(DEPTH_2):
        j = layer // 2
        if layer % 2 == 0:
            h = rms_norm(x, ab_norm[j])
            x = x + ab_mixer(h, ab_w_in[j], ab_conv_w[j], ab_conv_b[j], ab_gate_a_w[j],
                             ab_gate_a_b[j], ab_gate_x_w[j], ab_gate_x_b[j], ab_lambda[j],
                             ab_w_out[j])
        else:
            h = rms_norm(x, cd_norm[j])
            x = x + cd_mixer(h, cd_w_in[j], cd_lam_re[j], cd_lam_im[j], cd_log_dt[j],
                             cd_b_re[j], cd_b_im[j], cd_c_re[j], cd_c_im[j], cd_d[j],
                             cd_glu_w[j], cd_glu_b[j], cd_w_out[j])
        h = rms_norm(x, ffn_norm[layer])
        x = x + swiglu(h, ffn_w_gate[layer], ffn_w_up[layer], ffn_w_down[layer])
    return rms_norm(x, final_norm)


def setup_inputs(seed=0):
    out = dict(first_inputs(seed))
    for name, value in second_inputs(seed + 1).items():
        if name != "x":
            out[name + "_2"] = value
    return out


def reference(
    x, ffn1_pre_g, ffn1_post_g, ffn1_w_gate, ffn1_w_up, ffn1_w_down, mix_pre_g, mix_post_g,
    w_qkv, q_norm_g, k_norm_g, w_out, ffn2_pre_g, ffn2_post_g, ffn2_w_gate, ffn2_w_up,
    ffn2_w_down, ab_norm_2, ab_w_in_2, ab_conv_w_2, ab_conv_b_2, ab_gate_a_w_2, ab_gate_a_b_2,
    ab_gate_x_w_2, ab_gate_x_b_2, ab_lambda_2, ab_w_out_2, cd_norm_2, cd_w_in_2, cd_lam_re_2,
    cd_lam_im_2, cd_log_dt_2, cd_b_re_2, cd_b_im_2, cd_c_re_2, cd_c_im_2, cd_d_2, cd_glu_w_2,
    cd_glu_b_2, cd_w_out_2, ffn_norm_2, ffn_w_gate_2, ffn_w_up_2, ffn_w_down_2, final_norm_2,
):
    x = first_block(
        x, ffn1_pre_g, ffn1_post_g, ffn1_w_gate, ffn1_w_up, ffn1_w_down, mix_pre_g, mix_post_g,
        w_qkv, q_norm_g, k_norm_g, w_out, ffn2_pre_g, ffn2_post_g, ffn2_w_gate, ffn2_w_up,
        ffn2_w_down,
    )
    return second_block(
        x, ab_norm_2, ab_w_in_2, ab_conv_w_2, ab_conv_b_2, ab_gate_a_w_2, ab_gate_a_b_2,
        ab_gate_x_w_2, ab_gate_x_b_2, ab_lambda_2, ab_w_out_2, cd_norm_2, cd_w_in_2,
        cd_lam_re_2, cd_lam_im_2, cd_log_dt_2, cd_b_re_2, cd_b_im_2, cd_c_re_2, cd_c_im_2,
        cd_d_2, cd_glu_w_2, cd_glu_b_2, cd_w_out_2, ffn_norm_2, ffn_w_gate_2, ffn_w_up_2,
        ffn_w_down_2, final_norm_2,
    )


_drawn_inputs = setup_inputs


def setup_inputs(seed=0):
    import zlib

    import numpy as np

    out = dict(_drawn_inputs(seed))
    spreads = {}
    factors = {'ffn1_post_g': 3.761,
     'mix_post_g': 3.157,
     'q_norm_g': 5.809,
     'k_norm_g': 5.641,
     'ffn2_pre_g': 5.547,
     'ffn2_post_g': 7.597,
     'ab_norm_2': 8.0,
     'ab_conv_b_2': 4.82,
     'ab_gate_a_b_2': 29.134,
     'ab_gate_x_b_2': 24.065,
     'cd_norm_2': 124.736,
     'cd_lam_re_2': 64.0,
     'cd_lam_im_2': 37.76,
     'cd_log_dt_2': 45.064,
     'cd_b_re_2': 53.344,
     'cd_b_im_2': 51.032,
     'cd_c_re_2': 54.144,
     'cd_c_im_2': 52.552,
     'cd_glu_b_2': 200.0,
     'ffn_norm_2': 21.382,
     'final_norm_2': 192.588}
    for name, (base, spread) in spreads.items():
        noise = np.random.default_rng([zlib.crc32(name.encode()), seed]).standard_normal(out[name].shape)
        drawn = base * np.exp(spread * noise) if base else spread * noise
        out[name] = __import__('jax').numpy.asarray(drawn.astype(out[name].dtype))
    for name, factor in factors.items():
        out[name] = (out[name] * factor).astype(out[name].dtype)
    return out
```

```python
from contextlib import ExitStack
import math

import numpy as np
import concourse.bass as bass
from concourse import mybir

F32 = mybir.dt.float32
ACT = mybir.ActivationFunctionType
ALU = mybir.AluOpType
AX = mybir.AxisListType

P = 128
SEQ = 256
TT = SEQ // P
D = 1024
KC = D // P
FF = 2816
FCH = FF // P
PAIRS = FCH // 2
HD = 64
EPS = 1e-6
NEG = -1e30
SLOT = 3 * KC * 256
BLK = KC * 512
N_NORM = 7
S5_TILES = 16
TWO_PI = 2 * math.pi
C1 = 6.28125
C2 = 0.0019350051879882812
C3 = TWO_PI - C1 - C2
MAGIC = 1.5 * 2.0 ** 23
ROPE_THETA = 10000.0
GRID_W = 64

COL_GAIN = 0
COL_CONV = COL_GAIN + N_NORM * KC
COL_CONVB = COL_CONV + 16
COL_BA = COL_CONVB + 4
COL_BX = COL_BA + 4
COL_LAM = COL_BX + 4
COL_DSKIP = COL_LAM + 4
COL_GLUB = COL_DSKIP + 4
COL_LR = COL_GLUB + 4
COL_LI = COL_LR + S5_TILES
COL_LDT = COL_LI + S5_TILES
COL_SEL = COL_LDT + S5_TILES
COL_HALFPI = COL_SEL + 2
N_COLS = COL_HALFPI + 1

MIX_IN = (5, 5, 4)
MIX_BASE = (0, 7, 14)
MIX_END = (7, 14, 20)
STREAM = [("ffn", 0), ("mix", 0), ("ffn", 1), ("mix", 1), ("ffn", 2), ("mix", 2), ("ffn", 3)]


def item_base(kind, n):
    at = 0
    for k, m in STREAM:
        if (k, m) == (kind, n):
            return at
        at += PAIRS if k == "ffn" else MIX_END[m] - MIX_BASE[m]


FFN_ITEM = [item_base("ffn", n) for n in range(4)]
MIX_ITEM = [item_base("mix", n) for n in range(3)]
N_ITEMS = FFN_ITEM[3] + PAIRS


class Step:

    def __init__(self, sem):
        self.sem, self.count = sem, 0

    def mark(self, instruction):
        self.count += 1
        instruction.then_inc(self.sem, 1)

    def done(self, engine):
        engine.wait_ge(self.sem, self.count)


def build(nc, a):
    with ExitStack() as ctx:
        def sb(name, shape):
            return ctx.enter_context(nc.sbuf_tensor(name, shape, F32))

        def sem(name):
            return ctx.enter_context(nc.semaphore(name))

        x = sb("x", [P, TT, D])
        hT = sb("hT", [P, KC, SEQ])
        hn = sb("hn", [P, TT, D])
        ring = sb("ring", [P, 2, SLOT])
        ffn_s = sb("ffn_s", [P, 4, SEQ])
        act_s, sil_s = ffn_s[:, 0:2, :], ffn_s[:, 2:4, :]
        gpost = sb("gpost", [P, 2, D])
        ident = sb("ident", [P, P])
        cols = sb("cols", [P, N_COLS])
        biasB = sb("biasB", [P, TT, SEQ])
        biasM = sb("biasM", [P, 4, TT, SEQ])
        rope_in = sb("rope_in", [P, 4, TT, HD])
        qkg = sb("qkg", [P, 4, HD])
        ropeqk = sb("ropeqk", [P, 4, TT, HD])
        trow = sb("trow", [P, SEQ])
        tri = sb("tri", [P, 2, P])
        masks = sb("masks", [P, 2, 384])
        s5c = sb("s5c", [P, 5, SEQ])
        bb = sb("bb", [P, 2, 4, 2, HD])
        cc = sb("cc", [P, 3, S5_TILES, 32])
        glu = sb("glu", [P, 4, 512])
        gbd = sb("gbd", [P, 2, 4, P])
        small = sb("small", [P, 256])
        stat = sb("stat", [P, 20, 4])
        TABLES = 8704
        chw = sb("chw", [P, 8, SEQ])
        scratch = sb("scratch", [P, TABLES + 2 * S5_TILES * SEQ])
        ps = ctx.enter_context(nc.psum_tensor("ps", [P, 8 * 512], F32))

        def bank(i, n=1):
            return ps[:, i * 512:(i + n) * 512]

        at, limit = [0], [TABLES + 2 * S5_TILES * SEQ]

        def take(n):
            at[0] += n
            assert at[0] <= limit[0], at[0]
            return scratch[:, at[0] - n:at[0]]

        postw = scratch[:, 0:2 * D].rearrange("p (t n) -> p t n", t=TT)
        tabS = scratch[:, TABLES:TABLES + S5_TILES * SEQ].rearrange("p (j t) -> p j t", t=SEQ)
        tabC = scratch[:, TABLES + S5_TILES * SEQ:].rearrange("p (j t) -> p j t", t=SEQ)
        headsT = hn[:, :, :].rearrange("p t (c s) -> p (t c) s", s=SEQ)

        qT = [take(4 * SEQ).rearrange("p (c s) -> p c s", s=SEQ) for _ in range(2)]
        kTA = take(SEQ)
        kTB = take(4 * SEQ).rearrange("p (c s) -> p c s", s=SEQ)
        vA = take(TT * P).rearrange("p (t n) -> p t n", t=TT)
        vB = take(TT * 512).rearrange("p (t n) -> p t n", t=TT)
        raw = take(2 * 512).rearrange("p (r n) -> p r n", r=2)
        xn1 = take(512)
        t1 = take(512)
        t2 = take(512)
        rop = take(2 * 512).rearrange("p (r n) -> p r n", r=2)
        probs = [take(3 * 512).rearrange("p (r n) -> p r n", r=3)]
        pT = [take(2 * 512).rearrange("p (r n) -> p r n", r=2)]
        ssc = [raw]
        at[0], limit[0] = 0, TABLES
        qS = take(4 * SEQ).rearrange("p (c s) -> p c s", c=4)
        kS = take(4 * SEQ).rearrange("p (c s) -> p c s", c=4)
        vS = take(TT * 512).rearrange("p (t n) -> p t n", t=TT)
        after = at[0]
        xr = take(4 * (SEQ + 3)).rearrange("p (c s) -> p c s", c=4)
        xc = take(4 * SEQ).rearrange("p (c s) -> p c s", c=4)
        gg = ffn_s
        rgate = take(4 * SEQ).rearrange("p (c s) -> p c s", c=4)
        igate = take(4 * SEQ).rearrange("p (c s) -> p c s", c=4)
        rga = take(4 * SEQ).rearrange("p (c s) -> p c s", c=4)
        at[0] = after
        zs, lg, sp = (take(2 * 768).rearrange("p (r h s) -> p r h s", r=2, h=2) for _ in range(3))
        wz = chw[:, 0:6, :].rearrange("p a b -> p (a b)").rearrange("p (r h s) -> p r h s", r=2, h=2)
        at[0] = 0
        uT = take(4 * SEQ).rearrange("p (c s) -> p c s", c=4)
        qM = take(4 * SEQ).rearrange("p (c s) -> p c s", c=4)
        kM = take(4 * SEQ).rearrange("p (c s) -> p c s", c=4)
        vM = take(TT * 512).rearrange("p (t n) -> p t n", t=TT)
        yT = take(4 * SEQ).rearrange("p (c s) -> p c s", c=4)
        after = at[0]
        pc, pw = (chw[:, k:k + 4, :].rearrange("p (r h) s -> p r h s", r=2) for k in (0, 4))
        zz, dC, dS = (take(2 * 512).rearrange("p (r h s) -> p r h s", r=2, h=2) for _ in range(3))
        at[0] = after
        probs.append(take(3 * 512).rearrange("p (r n) -> p r n", r=3))
        pT.append(take(2 * 512).rearrange("p (r n) -> p r n", r=2))
        ssc.append(take(2 * 512).rearrange("p (r n) -> p r n", r=2))

        names = ["ss", "var", "std", "rinv", "pss", "pvar", "pstd", "prinv"]
        st = {n: small[:, 2 * k:2 * k + 2] for k, n in enumerate(names)}
        qk = {n: small[:, 16 + 8 * k:24 + 8 * k] for k, n in enumerate(["ss", "var", "std", "rinv"])}
        lam = {n: small[:, 48 + 4 * k:52 + 4 * k]
               for k, n in enumerate(["e", "den", "s", "s2", "acc", "pos", "neg8", "pos8"])}
        s5s = {n: small[:, 80 + 16 * k:96 + 16 * k] for k, n in enumerate(["dt", "mag", "th", "k", "t"])}

        def col(k, n=1):
            return cols[:, k:k + n]

        s = {n: sem(n) for n in [
            "x_loaded", "early_loaded", "s5c_loaded", "late_loaded", "w_full0", "w_full1", "gpost_loaded", "gpost_ffn2", "gpost_final", "out_stored",
            "sq_done", "var_ready", "std_ready", "hn_ready", "hT_psum", "hT_dve", "hT_act",
            "gate_ready", "up_ready", "silu_ready", "act_ready", "down_done", "ffn_tt0",
            "psq_done", "pvar_ready", "pstd_ready", "post_t", "x_ready", "final_ready",
            "proj_done", "proj_free", "raw_ready", "qkvar_ready", "qkstd_ready", "xn_ready", "t2_ready",
            "rop_ready", "ropT_psum", "ropT_evac",
            "s_ready", "max_ready", "p_ready", "pn_ready", "pt_psum", "pt_ready", "v_done", "o_ready",
            "tables_ready", "exp_dt", "lam_e", "lam_s", "s5_arg", "s5_trig", "s5_rden", "angles", "trig",
            "zeroed", "conv_done", "gates_done", "rg_act", "rg_q", "rg_sqrt", "rg_ix", "rg_done",
            "z_psum", "z_evac", "z_abs", "z_log", "sp_raw", "sp_ready", "zm_ready", "r_psum", "t_ready",
            "w_ready", "sbo_psum", "sbo_done",
            "bb_ready", "bu_done", "s5_mod", "zin_ready", "s5_scan", "s5_dem", "y_done", "y_sum",
            "y_gelu", "glu_psum", "glu_sig", "s5_done",
            "dve_step", "act_step", "pool_step"]}
        w_full = [s["w_full0"], s["w_full1"]]

        def slot_of(item):
            return item % 2

        def loaded(item):
            return 16 * (item // 2 + 1)

        def pre_x(n, t):
            return 4 * (n - 1) + 2 * (t + 1)

        def wait_unit(engine, m, j):
            if m == 0 and j < 8:
                engine.wait_ge(s["raw_ready"], j + 1)
            else:
                engine.wait_ge(s["proj_free"], (j - 7, j + 3, j + 13)[m])

        def rope_heads(r):
            return 2 if r in (2, 3) else 8

        def rope_dst(r):
            part, t = r // 2, r % 2
            q = slice(t * P, (t + 1) * P)
            if part == 1:
                return kTA[:, q].unsqueeze(1)
            return {0: qT[0], 2: qT[1], 3: kTB}[part][:, :, q]

        def head(a_, q, k, v, bias, scale, phase, o, heads_out, out_free):
            biased = bias is not None
            return dict(a=a_, q=q, k=k, v=v, bias=bias, scale=scale, o=o, heads_out=heads_out,
                        out_free=out_free,
                        exp_in=ssc[phase][:, a_ % 2, :] if biased else bank(a_ % 3),
                        exp_scale=1.0 if biased else scale,
                        probs=probs[phase][:, a_ % 3, :], pT=pT[phase][:, a_ % 2, :])

        heads1 = []
        for pair in range(8):
            for e in range(2):
                half = slice(64 * e, 64 * e + 64)
                c = pair % 4
                obank = bank(5 + pair % 2)
                dense = pair < 4
                heads1.append(head(
                    2 * pair + e, qT[0 if dense else 1][half, c, :],
                    kTA[half, :] if dense else kTB[half, c, :],
                    vA[:, :, half] if dense else vB[:, :, (2 * c + e) * HD:(2 * c + e + 1) * HD],
                    None if dense else biasB[:, :, :], HD ** -0.5, 0, obank[half, 0:SEQ],
                    (obank[:, 0:SEQ], headsT[:, pair, :]) if e else None,
                    pair - 1 if pair >= 2 else None))
        heads2 = []
        for m in range(4):
            obank = bank(5 + m % 2)[:, 0:SEQ]
            heads2.append(head(16 + m, qM[:, m, :], kM[:, m, :], vM[:, :, m * P:(m + 1) * P],
                               biasM[:, m, :, :], P ** -0.5, 1, obank, (obank, headsT[:, 4 + m, :]),
                               8 + m - 1 if m >= 2 else None))

        block = ctx.enter_context(nc.Block())

        @block.sync
        def _(sp_):
            sp_.dma_start(x[:, :, :], a["x"]).then_inc(s["x_loaded"], 16)

            def wait_release(item):
                old = item - 2
                if old < 0:
                    return
                for f in range(4):
                    if FFN_ITEM[f] <= old < FFN_ITEM[f] + PAIRS:
                        sp_.wait_ge(s["down_done"], FCH * f + 2 * (old - FFN_ITEM[f] + 1))
                for m in range(3):
                    if MIX_ITEM[m] <= old < MIX_ITEM[m] + MIX_END[m] - MIX_BASE[m]:
                        sp_.wait_ge(s["proj_done"], 2 * (MIX_BASE[m] + old - MIX_ITEM[m] + 1))

            for kind, n in STREAM:
                if kind == "ffn":
                    base = FFN_ITEM[n]
                    for p in (0, 1):
                        wait_release(base + p)
                        sl = slot_of(base + p)
                        sp_.dma_start(ring[:, sl, :], a["wffn"][PAIRS * n + p]).then_inc(w_full[sl], 16)
                    with sp_.Fori(1, PAIRS // 2) as r:
                        for h in (0, 1):
                            sp_.wait_ge(s["down_done"], r * 4 + (FCH * n + 2 * (h - 1)))
                            sl = slot_of(base + h)
                            sp_.dma_start(ring[:, sl, :], a["wffn"][r * 2 + (PAIRS * n + h)]) \
                               .then_inc(w_full[sl], 16)
                    p = PAIRS - 1
                    wait_release(base + p)
                    sl = slot_of(base + p)
                    sp_.dma_start(ring[:, sl, :], a["wffn"][PAIRS * n + p]).then_inc(w_full[sl], 16)
                else:
                    for b in range(MIX_END[n] - MIX_BASE[n]):
                        item = MIX_ITEM[n] + b
                        wait_release(item)
                        sl = slot_of(item)
                        width = BLK // 2 if (n, b) == (0, 1) else BLK
                        sp_.dma_start(ring[:, sl, 0:width], a["wmix"][MIX_BASE[n] + b, :, 0:width]) \
                           .then_inc(w_full[sl], 16)
            for t in range(TT):
                sp_.wait_ge(s["final_ready"], t + 1)
                sp_.dma_start(a["out"][:, t, :], hn[:, t, :]).then_inc(s["out_stored"], 16)
            sp_.wait_ge(s["out_stored"], 16 * TT)

        @block.tensor
        def _(pe):
            def transposes(n):
                for t in range(TT):
                    pe.wait_ge(s["hn_ready"], TT * n + t + 1)
                    if n == 0 and t == 0:
                        pe.wait_ge(s["early_loaded"], 32)
                    for c in range(KC):
                        at_ = (c % 2) * SEQ + t * P
                        i = nc.tensor.transpose(bank(4 + c // 2)[:, at_:at_ + P],
                                                hn[:, t, c * P:(c + 1) * P], ident[:, :])
                        if t == 1 and c % 2 == 1:
                            i.then_inc(s["hT_psum"], 1)

            def wait_hT(n, k):
                pe.wait_ge(s["hT_act" if k // 2 % 2 else "hT_dve"], 4 * n + k // 4 * 2 + k % 2 + 1)

            def ffn(f, n):
                base = FFN_ITEM[f]

                def gate_up(h, sl, G, first=False):
                    if not isinstance(G, int) or G >= 2:
                        pe.wait_ge(s["act_ready"], G - 1)
                    for w in range(2):
                        for k in range(KC):
                            if first and w == 0:
                                wait_hT(n, k)
                                if k == 0:
                                    wait_hT(n, 1)
                            o = w * KC * SEQ + k * SEQ + h * P
                            i = nc.tensor.matmul(bank(4 + 2 * w + h)[:, 0:SEQ],
                                                 ring[:, sl, o:o + P], hT[:, k, :],
                                                 start=k == 0, stop=k == KC - 1)
                        i.then_inc(s["gate_ready" if w == 0 else "up_ready"], 1)

                def down(h, sl, G, start=False, stop=False):
                    pe.wait_ge(s["act_ready"], G + 1)
                    for t in range(TT):
                        for half in range(2):
                            o = 2 * KC * SEQ + h * D + half * 512
                            i = nc.tensor.matmul(bank(2 * t + half), act_s[:, h, t * P:(t + 1) * P],
                                                 ring[:, sl, o:o + 512], start=start, stop=stop)
                        if stop and t == 0:
                            i.then_inc(s["ffn_tt0"], 1)
                    i.then_inc(s["down_done"], 1)

                G0 = FCH * f
                sl = slot_of(base)
                pe.wait_ge(w_full[sl], loaded(base))
                gate_up(0, sl, G0, first=True)
                gate_up(1, sl, G0 + 1)
                down(0, sl, G0, start=True)
                with pe.Fori(0, PAIRS // 2) as r:
                    for h2 in (1, 2):
                        sl = slot_of(base + h2)
                        pe.wait_ge(w_full[sl], r * 16 + loaded(base + h2))
                        G = r * 4 + (G0 + 2 * h2)
                        gate_up(0, sl, G)
                        down(1, 1 - sl, r * 4 + (G0 + 2 * h2 - 1))
                        gate_up(1, sl, r * 4 + (G0 + 2 * h2 + 1))
                        down(0, sl, G)
                down(1, slot_of(base + PAIRS - 1), G0 + FCH - 1, stop=True)

            def project(m, b, u, n, feature, width=512):
                j = 2 * b + u
                item = MIX_ITEM[m] + b
                sl = slot_of(item)
                if u == 0:
                    pe.wait_ge(w_full[sl], loaded(item))
                if j >= 4:
                    wait_unit(pe, m, j - 4)
                out = bank(j % 4)
                if feature:
                    for h in range(2):
                        for k in range(KC):
                            if j == 0 and h == 0:
                                wait_hT(n, k)
                            o = k * 512 + (2 * u + h) * P
                            i = nc.tensor.matmul(out[:, h * SEQ:(h + 1) * SEQ], ring[:, sl, o:o + P],
                                                 hT[:, k, :], start=k == 0, stop=k == KC - 1)
                else:
                    for k in range(KC):
                        if j == 0:
                            wait_hT(n, k)
                        i = nc.tensor.matmul(out[:, 0:width], hT[:, k, u * P:(u + 1) * P],
                                             ring[:, sl, k * width:(k + 1) * width],
                                             start=k == 0, stop=k == KC - 1)
                i.then_inc(s["proj_done"], 1)

            def project_out(m, ready):
                for half in range(2):
                    item = MIX_ITEM[m] + MIX_IN[m] + half
                    sl = slot_of(item)
                    pe.wait_ge(w_full[sl], loaded(item))
                    for t in range(TT):
                        for k in range(KC):
                            if half == 0 and t == 0:
                                for name, value in ready(k):
                                    pe.wait_ge(s[name], value)
                            i = nc.tensor.matmul(bank(2 * t + half), headsT[:, k, t * P:(t + 1) * P],
                                                 ring[:, sl, k * 512:(k + 1) * 512],
                                                 start=k == 0, stop=k == KC - 1)
                        i.then_inc(s["proj_done"], 1)

            def attention(heads):
                first, last = heads[0]["a"], heads[-1]["a"]
                for step in range(first, last + 4):
                    if step <= last:
                        h = heads[step - first]
                        if step >= first + 3:
                            pe.wait_ge(s["p_ready"], step - 2)
                        for t in range(TT):
                            i = nc.tensor.matmul(bank(step % 3)[:, t * SEQ:(t + 1) * SEQ],
                                                 h["q"][:, t * P:(t + 1) * P], h["k"],
                                                 start=True, stop=True)
                        i.then_inc(s["s_ready"], 1)
                    e = step - 2
                    if first <= e <= last:
                        pe.wait_ge(s["pn_ready"], e + 1)
                        if e >= first + 2:
                            pe.wait_ge(s["pt_ready"], e - 1)
                        pr = heads[e - first]["probs"]
                        for kt in range(TT):
                            for t in range(TT):
                                o = kt * SEQ + t * P
                                i = nc.tensor.transpose(bank(3 + e % 2)[:, o:o + P],
                                                        pr[:, t * SEQ + kt * P:t * SEQ + (kt + 1) * P],
                                                        ident[:, :])
                        i.then_inc(s["pt_psum"], 1)
                    e = step - 3
                    if first <= e <= last:
                        h = heads[e - first]
                        pe.wait_ge(s["pt_ready"], e + 1)
                        if h["out_free"] is not None:
                            pe.wait_ge(s["o_ready"], h["out_free"])
                        for kt in range(TT):
                            i = nc.tensor.matmul(h["o"], h["v"][:, kt, :],
                                                 h["pT"][:, kt * SEQ:(kt + 1) * SEQ],
                                                 start=kt == 0, stop=kt == TT - 1)
                        i.then_inc(s["v_done"], 1)

            transposes(0)
            ffn(0, 0)
            transposes(1)
            for j in range(10):
                project(0, j // 2, j % 2, 1, False, 256 if j // 2 == 1 else 512)
                r = j - 1
                if 0 <= r < 8:
                    pe.wait_ge(s["rop_ready"], r + 1)
                    if r >= 2:
                        pe.wait_ge(s["ropT_evac"], r - 1)
                    for c in range(rope_heads(r) // 2):
                        i = nc.tensor.transpose(bank(4 + r % 2)[:, c * P:(c + 1) * P],
                                                rop[:, r % 2, c * P:(c + 1) * P], ident[:, :])
                    i.then_inc(s["ropT_psum"], 1)
            pe.wait_ge(s["ropT_evac"], 8)
            wait_unit(pe, 0, 9)
            attention(heads1)
            project_out(0, lambda k: [("o_ready", k + 1)])
            transposes(2)
            ffn(1, 2)

            transposes(3)
            for j in range(4):
                project(1, j // 2, j % 2, 3, True)
            pe.wait_ge(s["conv_done"], 4)
            for w in range(2):
                for c in range(4):
                    i = nc.tensor.matmul(bank(4 + 2 * w, 2)[:, c * SEQ:(c + 1) * SEQ], gbd[:, w, c, :],
                                         xc[:, c, :], start=True, stop=True)
            i.then_inc(s["gates_done"], 1)
            for j in range(4, 10):
                project(1, j // 2, j % 2, 3, j // 2 != 3)
            pe.wait_ge(s["rg_done"], 4)
            wait_unit(pe, 1, 9)

            def stick_scores(b):
                if b >= 2:
                    pe.wait_ge(s["z_evac"], b - 1)
                for e in range(2):
                    r0 = slice(64 * e, 64 * e + 64)
                    z = bank(2 * (b % 2) + e)
                    nc.tensor.matmul(z[:, 0:SEQ], kS[r0, b, 0:P], qS[r0, b, :], start=True, stop=True)
                    i = nc.tensor.matmul(z[:, SEQ:384], kS[r0, b, P:SEQ], qS[r0, b, P:SEQ],
                                         start=True, stop=True)
                i.then_inc(s["z_psum"], 1)

            def stick_sums(b):
                pe.wait_ge(s["sp_ready"], b + 1)
                if b >= 1:
                    pe.wait_ge(s["t_ready"], b)
                for e in range(2):
                    R = bank(4 + e)
                    w = sp[:, b % 2, e, :]
                    nc.tensor.matmul(R[:, 0:SEQ], tri[:, 0, :], w[:, 0:SEQ], start=True, stop=False)
                    nc.tensor.matmul(R[:, P:SEQ], tri[:, 1, :], w[:, SEQ:384], start=False, stop=True)
                    i = nc.tensor.matmul(R[:, SEQ:384], tri[:, 0, :], w[:, SEQ:384], start=True, stop=True)
                i.then_inc(s["r_psum"], 1)

            def stick_values(b):
                pe.wait_ge(s["w_ready"], b + 1)
                if b >= 2:
                    pe.wait_ge(s["sbo_done"], b - 1)
                for e in range(2):
                    o = bank(6 + b % 2)[64 * e:64 * e + 64, :]
                    w = wz[:, b % 2, e, :]
                    v = vS[:, :, (2 * b + e) * HD:(2 * b + e + 1) * HD]
                    nc.tensor.matmul(o[:, 0:SEQ], v[:, 0, :], w[:, 0:SEQ], start=True, stop=False)
                    i = nc.tensor.matmul(o[:, P:SEQ], v[:, 1, :], w[:, SEQ:384], start=False, stop=True)
                i.then_inc(s["sbo_psum"], 1)

            stick_scores(0)
            stick_scores(1)
            for b in range(4):
                stick_sums(b)
                if b + 2 < 4:
                    stick_scores(b + 2)
                stick_values(b)
            project_out(1, lambda k: [("rg_done", k + 1)] if k < 4 else [("sbo_done", k - 3)])
            transposes(4)
            ffn(2, 4)

            transposes(5)
            project(2, 0, 0, 5, True)
            project(2, 0, 1, 5, True)
            wait_unit(pe, 2, 1)
            pe.wait_ge(s["bb_ready"], 4)

            def s5_in(j):
                c, q = j // 4, j % 4
                if j >= 2:
                    pe.wait_ge(s["s5_mod"], 2 * (j - 1))
                r0 = slice(32 * q, 32 * q + 32)
                for part in range(2):
                    i = nc.tensor.matmul(bank(4 + j % 2)[:, part * SEQ:(part + 1) * SEQ],
                                         bb[r0, part, c, :, :].rearrange("p g n -> p (g n)"),
                                         uT[r0, c, :], start=True, stop=True)
                i.then_inc(s["bu_done"], 1)

            def s5_out(j):
                c, q = j // 4, j % 4
                pe.wait_ge(s["s5_dem"], 2 * (j + 1))
                out = bank(6, 2)[32 * q:32 * q + 32, c * SEQ:(c + 1) * SEQ]
                r = j % 2
                terms = [(0, dC[:, r, 0, :]), (2, dS[:, r, 1, :]), (1, dS[:, r, 0, :]), (1, dC[:, r, 1, :])]
                for k, (w, z) in enumerate(terms):
                    i = nc.tensor.matmul(out, cc[:, w, j, :], z, start=k == 0, stop=k == 3)
                i.then_inc(s["y_done"], 1)

            s5_in(0)
            s5_in(1)
            for j in range(S5_TILES):
                if j % 2 == 0 and j < 12:
                    u = 2 + j // 2
                    project(2, u // 2, u % 2, 5, u // 2 != 3)
                s5_out(j)
                if j + 2 < S5_TILES:
                    s5_in(j + 2)
            wait_unit(pe, 2, 7)
            for o in range(4):
                for k in range(4):
                    if o == 0:
                        pe.wait_ge(s["y_gelu"], k + 1)
                    i = nc.tensor.matmul(bank(4 + o)[:, 0:SEQ], glu[:, k, o * P:(o + 1) * P], yT[:, k, :],
                                         start=k == 0, stop=k == 3)
                i.then_inc(s["glu_psum"], 1)
            pe.wait_ge(s["s5_done"], 4)
            attention(heads2)
            project_out(2, lambda k: [("s5_done", k + 1)] if k < 4 else [("o_ready", 8 + k - 3)])
            transposes(6)
            ffn(3, 6)

        @block.scalar
        def _(act):
            step = Step(s["act_step"])
            for name, dst in (("ident", ident[:, :]), ("cols", cols[:, :])):
                act.dma_start(dst, a[name]).then_inc(s["early_loaded"], 16)
            for k, name in enumerate(("ffn1_post_g", "mix_post_g")):
                act.dma_start(gpost[:, k, :], a[name].partition_broadcast(P)).then_inc(s["gpost_loaded"], 16)
            act.dma_start(s5c[:, :, :], a["s5c"]).then_inc(s["s5c_loaded"], 16)
            for name, dst in (("biasB", biasB[:, :, :]), ("rope_in", rope_in[:, :, :, :]),
                              ("trow", trow[:, :]), ("tri", tri[:, :, :]), ("masks", masks[:, :, :]),
                              ("biasM", biasM[:, :, :, :]), ("glu", glu[:, :, :]),
                              ("qkg", qkg[:, :, :]), ("cc", cc[:, 0:2, :, :])):
                act.dma_start(dst, a[name]).then_inc(s["late_loaded"], 16)
            act.wait_ge(s["zeroed"], 1)
            for e in range(2):
                act.dma_start(gbd[64 * e:64 * e + 64, :, :, 64 * e:64 * e + 64], a["gates"][e]) \
                   .then_inc(s["late_loaded"], 16)

            def norm(n):
                for t in range(TT):
                    if n == 0:
                        if t == 0:
                            act.wait_ge(s["x_loaded"], 16)
                    else:
                        act.wait_ge(s["x_ready"], pre_x(n, t))
                    nc.scalar.activation(postw[:, t, :], x[:, t, :], ACT.Square,
                                         accum_out=st["ss"][:, t:t + 1]).then_inc(s["sq_done"], 1)
                act.wait_ge(s["var_ready"], n + 1)
                nc.scalar.activation(st["std"], st["var"], ACT.Sqrt).then_inc(s["std_ready"], 1)

            def norm_out(n):
                for b in (1, 3):
                    act.wait_ge(s["hT_psum"], 4 * n + b + 1)
                    for h in range(2):
                        nc.scalar.activation(hT[:, 2 * b + h, :], bank(4 + b)[:, h * SEQ:(h + 1) * SEQ],
                                             ACT.Copy, scale=col(COL_GAIN + n * KC + 2 * b + h)) \
                          .then_inc(s["hT_act"], 1)

            def ffn(f):
                def silu(h, G):
                    act.wait_ge(s["gate_ready"], G + 1)
                    if not isinstance(G, int) or G >= 2:
                        act.wait_ge(s["act_ready"], G - 1)
                    nc.scalar.activation(sil_s[:, h, :], bank(4 + h)[:, 0:SEQ], ACT.Silu) \
                      .then_inc(s["silu_ready"], 1)
                for h in range(2):
                    silu(h, FCH * f + h)
                with act.Fori(1, PAIRS) as r:
                    for h in range(2):
                        silu(h, r * 2 + (FCH * f + h))

            def post(p, wait_out):
                for t in range(TT):
                    wait_out(act, t)
                    nc.scalar.activation(postw[:, t, :], bank(2 * t, 2), ACT.Square,
                                         accum_out=st["pss"][:, t:t + 1]).then_inc(s["psq_done"], 1)
                act.wait_ge(s["pvar_ready"], p + 1)
                nc.scalar.activation(st["pstd"], st["pvar"], ACT.Sqrt).then_inc(s["pstd_ready"], 1)

            def attention(heads):
                first, last = heads[0]["a"], heads[-1]["a"]
                for e in range(first, last + 4):
                    if e <= last:
                        h = heads[e - first]
                        act.wait_ge(s["max_ready"], e + 1)
                        if e >= first + 3:
                            act.wait_ge(s["pt_psum"], e - 2)
                        for t in range(TT):
                            i = nc.scalar.activation(
                                h["probs"][:, t * SEQ:(t + 1) * SEQ], h["exp_in"][:, t * SEQ:(t + 1) * SEQ],
                                ACT.Exp, bias=stat[:, h["a"], t:t + 1], scale=h["exp_scale"],
                                accum_out=stat[:, h["a"], 2 + t:3 + t])
                        i.then_inc(s["p_ready"], 1)
                    g = e - 2
                    if first <= g <= last:
                        h = heads[g - first]
                        act.wait_ge(s["pt_psum"], g + 1)
                        if g >= first + 2:
                            act.wait_ge(s["v_done"], g - 1)
                        nc.scalar.activation(h["pT"], bank(3 + g % 2), ACT.Copy).then_inc(s["pt_ready"], 1)
                    g = e - 3
                    if first <= g <= last and heads[g - first]["heads_out"] is not None:
                        act.wait_ge(s["v_done"], g + 1)
                        src, dst = heads[g - first]["heads_out"]
                        nc.scalar.activation(dst, src, ACT.Copy).then_inc(s["o_ready"], 1)

            def evacuate(unit, dst, func=ACT.Copy):
                m = 0 if unit < 10 else 1 if unit < 20 else 2
                j = unit - 2 * sum(MIX_IN[:m])
                act.wait_ge(s["proj_done"], 2 * MIX_BASE[m] + j + 1)
                nc.scalar.activation(dst, bank(j % 4), func).then_inc(s["proj_free"], 1)

            norm(0)
            act.wait_ge(s["s5c_loaded"], 16)
            act.wait_ge(s["early_loaded"], 32)
            step.mark(nc.scalar.activation(lam["e"], col(COL_LAM, 4), ACT.Abs))
            nc.scalar.activation(s5s["dt"], col(COL_LDT, S5_TILES), ACT.Exp).then_inc(s["exp_dt"], 1)
            nc.scalar.activation(s5c[:, 2, :], s5c[:, 2, :], ACT.Exp).then_inc(s["exp_dt"], 1)
            step.done(act)
            nc.scalar.activation(lam["e"], lam["e"], ACT.Exp, scale=-1.0).then_inc(s["lam_e"], 1)
            norm_out(0)
            ffn(0)
            post(0, lambda e, t: e.wait_ge(*((s["ffn_tt0"], 1) if t == 0 else (s["down_done"], FCH))))
            norm(1)
            norm_out(1)

            def rope_in_out(r):
                act.wait_ge(s["ropT_psum"], r + 1)
                n = rope_heads(r) // 2
                nc.scalar.activation(rope_dst(r), bank(4 + r % 2)[:, 0:n * P]
                                     .rearrange("p (c q) -> p c q", q=P), ACT.Copy) \
                  .then_inc(s["ropT_evac"], 1)

            for j in range(10):
                t = j % 2
                if j < 8:
                    if j >= 2:
                        act.wait_ge(s["rop_ready"], j - 1)
                    act.wait_ge(s["proj_done"], j + 1)
                    w = rope_heads(j) * HD
                    if j in (2, 3):
                        nc.scalar.activation(vA[:, t, :], bank(j)[:, P:2 * P], ACT.Copy)
                    i = nc.scalar.activation(raw[:, j % 2, 0:w], bank(j % 4)[:, 0:w], ACT.Copy)
                    i.then_inc(s["raw_ready"], 1)
                    if j < 4:
                        act.wait_ge(s["qkvar_ready"], j + 1)
                        nc.scalar.activation(qk["std"][:, 0:rope_heads(j)], qk["var"][:, 0:rope_heads(j)],
                                             ACT.Sqrt).then_inc(s["qkstd_ready"], 1)
                else:
                    evacuate(j, vB[:, t, :])
                if 0 <= j - 1 < 8:
                    rope_in_out(j - 1)
            attention(heads1)
            post(1, lambda e, t: e.wait_ge(s["proj_done"], 2 * MIX_END[0] - 1 + t))
            norm(2)
            norm_out(2)
            ffn(1)
            post(2, lambda e, t: e.wait_ge(*((s["ffn_tt0"], 2) if t == 0 else (s["down_done"], 2 * FCH))))
            norm(3)
            norm_out(3)

            for j in range(2):
                evacuate(10 + j, xr[:, 2 * j:2 * j + 2, 3:])
            act.wait_ge(s["s5_arg"], 1)
            nc.scalar.activation(chw[:, 0, :], chw[:, 0, :], ACT.Exp).then_inc(s["s5_trig"], 1)
            nc.scalar.activation(s5s["mag"], s5s["mag"], ACT.Exp).then_inc(s["s5_trig"], 1)
            nc.scalar.activation(chw[:, 2, :], chw[:, 1, :], ACT.Sin).then_inc(s["s5_trig"], 1)
            step.mark(nc.scalar.activation(chw[:, 3, :], chw[:, 1, :], ACT.Abs))
            step.done(act)
            nc.scalar.activation(chw[:, 3, :], chw[:, 3, :], ACT.Sin, bias=col(COL_HALFPI), scale=-1.0) \
              .then_inc(s["s5_trig"], 1)
            for j in range(2, 4):
                evacuate(10 + j, qS[:, 2 * (j % 2):2 * (j % 2) + 2, :])
            act.wait_ge(s["gates_done"], 1)
            for w, dst, bias in ((0, rgate, COL_BA), (1, igate, COL_BX)):
                for c in range(4):
                    step.mark(nc.scalar.activation(dst[:, c, :], bank(4 + 2 * w, 2)[:, c * SEQ:(c + 1) * SEQ],
                                                   ACT.Sigmoid, bias=col(bias + c)))
            for j in range(4, 6):
                evacuate(10 + j, kS[:, 2 * (j % 2):2 * (j % 2) + 2, :])
            step.done(act)
            act.wait_ge(s["lam_s"], 1)
            for c in range(4):
                step.mark(nc.scalar.activation(rga[:, c, :], rgate[:, c, :], ACT.Exp,
                                               scale=lam["neg8"][:, c:c + 1]))
            step.done(act)
            for c in range(4):
                nc.scalar.activation(rgate[:, c, :], rgate[:, c, :], ACT.Tanh,
                                     scale=lam["pos8"][:, c:c + 1]).then_inc(s["rg_act"], 1)
            act.wait_ge(s["rg_q"], 1)
            nc.scalar.activation(rgate[:, :, :], rgate[:, :, :], ACT.Sqrt).then_inc(s["rg_sqrt"], 1)
            for j in range(6, 8):
                evacuate(10 + j, vS[:, j % 2, :])
            act.wait_ge(s["angles"], 4)
            for jb in range(4):
                tS, tC = tabS[:, 4 * jb:4 * jb + 4, :], tabC[:, 4 * jb:4 * jb + 4, :]
                step.mark(nc.scalar.activation(tC, tS, ACT.Abs))
                step.done(act)
                nc.scalar.activation(tC, tC, ACT.Sin, bias=col(COL_HALFPI), scale=-1.0).then_inc(s["trig"], 1)
                nc.scalar.activation(tS, tS, ACT.Sin).then_inc(s["trig"], 1)
            for j in range(8, 10):
                evacuate(10 + j, gg[:, 2 * (j % 2):2 * (j % 2) + 2, :], ACT.Gelu_apprx_tanh)
            act.wait_ge(s["rg_done"], 4)

            def stick_copy(b):
                act.wait_ge(s["z_psum"], b + 1)
                if b >= 2:
                    act.wait_ge(s["zm_ready"], b - 1)
                    act.wait_ge(s["sp_raw"], b - 1)
                nc.scalar.activation(zs[:, b % 2, :, :], bank(2 * (b % 2), 2)
                                     .rearrange("p (e q) -> p e q", e=2)[:, :, 0:384],
                                     ACT.Copy, scale=HD ** -0.5).then_inc(s["z_evac"], 1)

            def stick_log(b):
                act.wait_ge(s["z_abs"], b + 1)
                step.mark(nc.scalar.activation(lg[:, b % 2, :, :], lg[:, b % 2, :, :], ACT.Exp))
                step.done(act)
                nc.scalar.activation(lg[:, b % 2, :, :], lg[:, b % 2, :, :], ACT.Ln, bias=1.0) \
                  .then_inc(s["z_log"], 1)

            stick_copy(0)
            stick_log(0)
            stick_copy(1)
            for b in range(4):
                if b + 1 < 4:
                    stick_log(b + 1)
                act.wait_ge(s["t_ready"], b + 1)
                nc.scalar.activation(wz[:, b % 2, :, :], wz[:, b % 2, :, :], ACT.Exp).then_inc(s["w_ready"], 1)
                if b + 2 < 4:
                    stick_copy(b + 2)
                act.wait_ge(s["sbo_psum"], b + 1)
                nc.scalar.activation(headsT[:, 4 + b, :], bank(6 + b % 2)[:, 0:SEQ], ACT.Copy) \
                  .then_inc(s["sbo_done"], 1)
            norm(4)
            norm_out(4)
            ffn(2)
            norm(5)
            norm_out(5)

            for j in range(8):
                t = j % 2
                dst = (uT, qM, kM)[j // 2][:, 2 * t:2 * t + 2, :] if j < 6 else vM[:, t, :]
                evacuate(20 + j, dst)
            for c in range(4):
                act.wait_ge(s["y_sum"], c + 1)
                nc.scalar.activation(yT[:, c, :], yT[:, c, :], ACT.Gelu_apprx_tanh).then_inc(s["y_gelu"], 1)
            for c in range(4):
                act.wait_ge(s["glu_psum"], c + 1)
                nc.scalar.activation(uT[:, c, :], bank(4 + c)[:, 0:SEQ], ACT.Sigmoid,
                                     bias=col(COL_GLUB + c)).then_inc(s["glu_sig"], 1)
            attention(heads2)
            norm(6)
            norm_out(6)
            ffn(3)
            norm(7)

        @block.vector
        def _(dve):
            step = Step(s["dve_step"])

            def wait_out(p, t):
                if p % 2 == 0:
                    f = p // 2
                    if t == 0:
                        dve.wait_ge(s["ffn_tt0"], f + 1)
                    else:
                        dve.wait_ge(s["down_done"], FCH * (f + 1))
                else:
                    dve.wait_ge(s["proj_done"], 2 * MIX_END[p // 2] - 1 + t)

            def norm(n):
                dve.wait_ge(s["sq_done"], TT * (n + 1))
                nc.vector.tensor_scalar(st["var"], st["ss"], 1.0 / D, EPS, ALU.mult, ALU.add) \
                  .then_inc(s["var_ready"], 1)
                dve.wait_ge(s["std_ready"], n + 1)
                step.mark(nc.vector.reciprocal(st["rinv"], st["std"]))
                step.done(dve)
                if n < N_NORM:
                    for t in range(TT):
                        nc.vector.tensor_scalar(hn[:, t, :], x[:, t, :], st["rinv"][:, t:t + 1], None,
                                                ALU.mult).then_inc(s["hn_ready"], 1)
                    for b in (0, 2):
                        dve.wait_ge(s["hT_psum"], 4 * n + b + 1)
                        for h in range(2):
                            nc.vector.tensor_scalar(hT[:, 2 * b + h, :],
                                                    bank(4 + b)[:, h * SEQ:(h + 1) * SEQ],
                                                    col(COL_GAIN + n * KC + 2 * b + h), None,
                                                    ALU.mult).then_inc(s["hT_dve"], 1)
                else:
                    dve.wait_ge(s["gpost_final"], 16)
                    for t in range(TT):
                        nc.vector.scalar_tensor_tensor(hn[:, t, :], x[:, t, :], st["rinv"][:, t:t + 1],
                                                       gpost[:, 1, :], ALU.mult, ALU.mult) \
                          .then_inc(s["final_ready"], 1)

            def ffn(f):
                def times(h, G):
                    dve.wait_ge(s["silu_ready"], G + 1)
                    dve.wait_ge(s["up_ready"], G + 1)
                    if not isinstance(G, int) or G >= 2:
                        dve.wait_ge(s["down_done"], G - 1)
                    nc.vector.tensor_tensor(act_s[:, h, :], sil_s[:, h, :], bank(6 + h)[:, 0:SEQ],
                                            ALU.mult).then_inc(s["act_ready"], 1)
                for h in range(2):
                    times(h, FCH * f + h)
                with dve.Fori(1, PAIRS) as r:
                    for h in range(2):
                        times(h, r * 2 + (FCH * f + h))

            def post_normed(p, factor):
                dve.wait_ge(s["psq_done"], TT * (p + 1))
                nc.vector.tensor_scalar(st["pvar"], st["pss"], 1.0 / D, EPS, ALU.mult, ALU.add) \
                  .then_inc(s["pvar_ready"], 1)
                dve.wait_ge(s["pstd_ready"], p + 1)
                step.mark(nc.vector.reciprocal(st["prinv"], st["pstd"]))
                step.done(dve)
                step.mark(nc.vector.tensor_scalar(st["prinv"], st["prinv"], factor, None, ALU.mult))
                step.done(dve)
                dve.wait_ge(*((s["gpost_loaded"], 32) if p < 2 else (s["gpost_ffn2"], 16)))
                for t in range(TT):
                    for half in range(2):
                        hs = slice(half * 512, (half + 1) * 512)
                        nc.vector.scalar_tensor_tensor(postw[:, t, hs], bank(2 * t + half),
                                                       st["prinv"][:, t:t + 1], gpost[:, p % 2, hs],
                                                       ALU.mult, ALU.mult).then_inc(s["post_t"], 1)

            def post_plain(p):
                for t in range(TT):
                    wait_out(p, t)
                    for half in range(2):
                        hs = slice(half * 512, (half + 1) * 512)
                        nc.vector.tensor_tensor(x[:, t, hs], x[:, t, hs], bank(2 * t + half), ALU.add) \
                          .then_inc(s["x_ready"], 1)

            def attention(heads):
                first, last = heads[0]["a"], heads[-1]["a"]
                for e in range(first, last + 2):
                    if e <= last:
                        h = heads[e - first]
                        n_ = h["a"]
                        scores = bank(e % 3)
                        dve.wait_ge(s["s_ready"], e + 1)
                        if h["bias"] is None:
                            step.mark(nc.vector.tensor_reduce(
                                stat[:, n_, 0:2], scores.rearrange("p (t k) -> p t k", t=TT), AX.X, ALU.max))
                            step.done(dve)
                            nc.vector.tensor_scalar(stat[:, n_, 0:2], stat[:, n_, 0:2], -h["scale"], None,
                                                    ALU.mult).then_inc(s["max_ready"], 1)
                        else:
                            if e >= first + 2 and heads[e - first - 2]["bias"] is not None:
                                dve.wait_ge(s["p_ready"], e - 1)
                            for t in range(TT):
                                step.mark(nc.vector.tensor_tensor_reduce(
                                    out=h["exp_in"][:, t * SEQ:(t + 1) * SEQ],
                                    in0=scores[:, t * SEQ:(t + 1) * SEQ], in1=h["bias"][:, t, :],
                                    scale=h["scale"], scalar=-3e38, op0=ALU.add, op1=ALU.max,
                                    accum_out=stat[:, n_, t:t + 1]))
                            step.done(dve)
                            nc.vector.tensor_scalar(stat[:, n_, 0:2], stat[:, n_, 0:2], -1.0, None,
                                                    ALU.mult).then_inc(s["max_ready"], 1)
                    g = e - 1
                    if first <= g <= last:
                        h = heads[g - first]
                        dve.wait_ge(s["p_ready"], g + 1)
                        step.mark(nc.vector.reciprocal(stat[:, h["a"], 2:4], stat[:, h["a"], 2:4]))
                        step.done(dve)
                        for t in range(TT):
                            pr = h["probs"][:, t * SEQ:(t + 1) * SEQ]
                            i = nc.vector.tensor_scalar(pr, pr, stat[:, h["a"], 2 + t:3 + t], None, ALU.mult)
                        i.then_inc(s["pn_ready"], 1)

            norm(0)
            dve.wait_ge(s["lam_e"], 1)
            step.mark(nc.vector.tensor_scalar(lam["den"], lam["e"], 2.0, None, ALU.add))
            step.done(dve)
            step.mark(nc.vector.reciprocal(lam["den"], lam["den"]))
            step.done(dve)
            step.mark(nc.vector.tensor_tensor(lam["s"], lam["e"], lam["den"], ALU.mult))
            step.done(dve)
            step.mark(nc.vector.tensor_tensor(lam["s2"], lam["s"], lam["s"], ALU.mult))
            step.mark(nc.vector.memset(lam["acc"], 1.0 / 17))
            for k in range(7, -1, -1):
                step.done(dve)
                step.mark(nc.vector.tensor_tensor(lam["acc"], lam["acc"], lam["s2"], ALU.mult))
                step.done(dve)
                step.mark(nc.vector.tensor_scalar(lam["acc"], lam["acc"], 1.0 / (2 * k + 1), None, ALU.add))
            step.mark(nc.vector.tensor_scalar(lam["pos"], col(COL_LAM, 4), -1.0, 0.0, ALU.mult, ALU.max))
            step.done(dve)
            step.mark(nc.vector.tensor_tensor(lam["acc"], lam["acc"], lam["s"], ALU.mult))
            step.done(dve)
            step.mark(nc.vector.scalar_tensor_tensor(lam["acc"], lam["acc"], 2.0, lam["pos"],
                                                     ALU.mult, ALU.add))
            step.done(dve)
            step.mark(nc.vector.tensor_scalar(lam["neg8"], lam["acc"], -8.0, None, ALU.mult))
            nc.vector.tensor_scalar(lam["pos8"], lam["acc"], 8.0, None, ALU.mult).then_inc(s["lam_s"], 1)
            ffn(0)
            post_normed(0, 0.5)
            norm(1)
            dve.wait_ge(s["late_loaded"], 16 * 11)
            for qk_i in range(2):
                for part in range(2):
                    g = qkg[:, 2 * qk_i + part, :].unsqueeze(1).broadcast_to([P, TT, HD])
                    nc.vector.tensor_tensor(ropeqk[:, 2 * qk_i + part, :, :], rope_in[:, part, :, :], g,
                                            ALU.mult).then_inc(s["tables_ready"], 1)
            dve.wait_ge(s["s5_arg"], 1)
            nc.vector.reciprocal(s5c[:, 2, :], chw[:, 4, :]).then_inc(s["s5_rden"], 1)

            for r in range(8):
                nh = rope_heads(r)
                w = nh * HD
                t = r % 2
                src = raw[:, r % 2, 0:w]
                dve.wait_ge(s["raw_ready"], r + 1)
                if r >= 1:
                    dve.wait_ge(s["rop_ready"], r)
                if r < 4:
                    step.mark(nc.vector.tensor_tensor(t1[:, 0:w], src, src, ALU.mult))
                    step.done(dve)
                    step.mark(nc.vector.tensor_reduce(qk["ss"][:, 0:nh],
                                                      t1[:, 0:w].rearrange("p (h d) -> p h d", d=HD),
                                                      AX.X, ALU.add))
                    step.done(dve)
                    nc.vector.tensor_scalar(qk["var"][:, 0:nh], qk["ss"][:, 0:nh], 1.0 / HD, EPS,
                                            ALU.mult, ALU.add).then_inc(s["qkvar_ready"], 1)
                    dve.wait_ge(s["qkstd_ready"], r + 1)
                    step.mark(nc.vector.reciprocal(qk["rinv"][:, 0:nh], qk["std"][:, 0:nh]))
                    step.done(dve)
                    nc.vector.tensor_tensor(xn1[:, 0:w].rearrange("p (h d) -> p h d", d=HD),
                                            src.rearrange("p (h d) -> p h d", d=HD),
                                            qk["rinv"][:, 0:nh].unsqueeze(2).broadcast_to([P, nh, HD]),
                                            ALU.mult).then_inc(s["xn_ready"], 1)
                    dve.wait_ge(s["xn_ready"], r + 1)
                    src = xn1[:, 0:w]
                cos = (ropeqk[:, 2 * (r // 2), t, :] if r < 4 else rope_in[:, 2, t, :])
                step.mark(nc.vector.tensor_tensor(t1[:, 0:w].rearrange("p (h d) -> p h d", d=HD),
                                                  src.rearrange("p (h d) -> p h d", d=HD),
                                                  cos.unsqueeze(1).broadcast_to([P, nh, HD]), ALU.mult))
                step.done(dve)
                dve.wait_ge(s["t2_ready"], 2 * (r + 1))
                if r >= 2:
                    dve.wait_ge(s["ropT_psum"], r - 1)
                nc.vector.tensor_tensor(rop[:, r % 2, 0:w], t1[:, 0:w], t2[:, 0:w], ALU.add) \
                  .then_inc(s["rop_ready"], 1)
            attention(heads1)
            post_normed(1, 1.0)
            norm(2)
            ffn(1)
            post_normed(2, 0.5)
            norm(3)

            wait_unit(dve, 1, 1)
            dve.wait_ge(s["zeroed"], 2)
            for c in range(4):
                step.mark(nc.vector.tensor_scalar(xc[:, c, :], xr[:, c, 0:SEQ], col(COL_CONV + c),
                                                  col(COL_CONVB + c), ALU.mult, ALU.add))
            for tap in range(1, 4):
                step.done(dve)
                for c in range(4):
                    i = nc.vector.scalar_tensor_tensor(xc[:, c, :], xr[:, c, tap:tap + SEQ],
                                                       col(COL_CONV + 4 * tap + c), xc[:, c, :],
                                                       ALU.mult, ALU.add)
                    if tap < 3:
                        step.mark(i)
                    else:
                        i.then_inc(s["conv_done"], 1)
            dve.wait_ge(s["rg_act"], 4)
            asq = xr[:, :, 0:SEQ]
            step.mark(nc.vector.tensor_tensor(asq, rga[:, :, :], rga[:, :, :], ALU.mult))
            step.done(dve)
            step.mark(nc.vector.scalar_tensor_tensor(rgate[:, :, :], asq, 1.0, rgate[:, :, :],
                                                     ALU.add, ALU.mult))
            step.done(dve)
            nc.vector.tensor_scalar(rgate[:, :, :], rgate[:, :, :], 1e-34, None, ALU.max) \
              .then_inc(s["rg_q"], 1)
            dve.wait_ge(s["rg_sqrt"], 1)
            dve.wait_ge(s["rg_ix"], 1)
            step.mark(nc.vector.tensor_tensor(rgate[:, :, :], rgate[:, :, :], igate[:, :, :], ALU.mult))
            step.done(dve)
            for c in range(4):
                step.mark(nc.vector.tensor_tensor_scan(xc[:, c, :], rga[:, c, :], rgate[:, c, :], 0.0,
                                                       ALU.mult, ALU.add))
            step.done(dve)
            wait_unit(dve, 1, 9)
            for c in range(4):
                nc.vector.tensor_tensor(headsT[:, c, :], xc[:, c, :], gg[:, c, :], ALU.mult) \
                  .then_inc(s["rg_done"], 1)
            dve.wait_ge(s["rg_done"], 4)

            def stick_abs(b):
                dve.wait_ge(s["z_evac"], b + 1)
                if b >= 2:
                    dve.wait_ge(s["sp_raw"], b - 1)
                nc.vector.scalar_tensor_tensor(lg[:, b % 2, :, :], zs[:, b % 2, :, :], -1.0,
                                               zs[:, b % 2, :, :], ALU.mult, ALU.min) \
                  .then_inc(s["z_abs"], 1)

            stick_abs(0)
            for b in range(4):
                if b + 1 < 4:
                    stick_abs(b + 1)
                dve.wait_ge(s["z_log"], b + 1)
                if b >= 2:
                    dve.wait_ge(s["r_psum"], b - 1)
                nc.vector.scalar_tensor_tensor(sp[:, b % 2, :, :], zs[:, b % 2, :, :], 0.0,
                                               lg[:, b % 2, :, :], ALU.max, ALU.add) \
                  .then_inc(s["sp_raw"], 1)
                dve.wait_ge(s["r_psum"], b + 1)
                dve.wait_ge(s["zm_ready"], b + 1)
                R = bank(4, 2).rearrange("p (e q) -> p e q", e=2)[:, :, 0:384]
                nc.vector.tensor_tensor(wz[:, b % 2, :, :], wz[:, b % 2, :, :], R, ALU.subtract) \
                  .then_inc(s["t_ready"], 1)
            post_plain(3)
            norm(4)
            ffn(2)
            post_plain(4)
            norm(5)

            dve.wait_ge(s["trig"], 8)

            def both(tab, j):
                return tab[:, j, :].unsqueeze(1).broadcast_to([P, 2, SEQ])

            def s5_modulate(j):
                dve.wait_ge(s["bu_done"], j + 1)
                if j >= 2:
                    dve.wait_ge(s["s5_scan"], 2 * (j - 1))
                bu = bank(4 + j % 2).rearrange("p (h s) -> p h s", h=2)
                nc.vector.tensor_tensor(pc[:, j % 2, :, :], bu, both(tabC, j), ALU.mult) \
                  .then_inc(s["s5_mod"], 1)
                nc.vector.tensor_tensor(pw[:, j % 2, :, :], bu, both(tabS, j), ALU.mult) \
                  .then_inc(s["s5_mod"], 1)

            s5_modulate(0)
            for j in range(S5_TILES):
                if j + 1 < S5_TILES:
                    s5_modulate(j + 1)
                dve.wait_ge(s["zin_ready"], 2 * (j + 1))
                if j >= 2:
                    dve.wait_ge(s["s5_dem"], 2 * (j - 1))
                for h in range(2):
                    nc.vector.tensor_tensor_scan(zz[:, j % 2, h, :],
                                                 s5s["mag"][:, j:j + 1].broadcast_to([P, SEQ]),
                                                 pc[:, j % 2, h, :], 0.0, ALU.mult, ALU.add) \
                      .then_inc(s["s5_scan"], 1)
            dve.wait_ge(s["y_done"], S5_TILES)
            for c in range(4):
                nc.vector.scalar_tensor_tensor(yT[:, c, :], uT[:, c, :], col(COL_DSKIP + c),
                                               bank(6, 2)[:, c * SEQ:(c + 1) * SEQ], ALU.mult, ALU.add) \
                  .then_inc(s["y_sum"], 1)
            for c in range(4):
                dve.wait_ge(s["glu_sig"], c + 1)
                nc.vector.tensor_tensor(headsT[:, c, :], yT[:, c, :], uT[:, c, :], ALU.mult) \
                  .then_inc(s["s5_done"], 1)
            attention(heads2)
            post_plain(5)
            norm(6)
            ffn(3)
            post_plain(6)
            norm(7)

        @block.gpsimd
        def _(pool):
            step = Step(s["pool_step"])

            def tt(out, in0, in1, op):
                step.mark(nc.gpsimd.tensor_tensor(out, in0, in1, op))
                step.done(pool)

            def ts(out, in0, s1, s2, op0, op1):
                step.mark(nc.gpsimd.tensor_scalar(out, in0, s1, s2, op0, op1))
                step.done(pool)

            def reduce_angle(ang, k, t, parts):
                ts(k, ang, 1.0 / TWO_PI, MAGIC, ALU.mult, ALU.add)
                for part in parts:
                    ts(t, k, MAGIC, -part, ALU.subtract, ALU.mult)
                    tt(ang, ang, t, ALU.add)

            def add_residual(p):
                for t in range(TT):
                    for half in range(2):
                        hs = slice(half * 512, (half + 1) * 512)
                        pool.wait_ge(s["post_t"], 4 * p + 2 * t + half + 1)
                        nc.gpsimd.tensor_tensor(x[:, t, hs], x[:, t, hs], postw[:, t, hs], ALU.add) \
                          .then_inc(s["x_ready"], 1)

            nc.gpsimd.memset(gbd[:, :, :, :], 0.0).then_inc(s["zeroed"], 1)
            pool.wait_ge(s["exp_dt"], 2)
            pool.wait_ge(s["late_loaded"], 16 * 11)
            A = [chw[:, k, :] for k in range(8)]
            lr, li, dt, br, bi = (s5c[:, k, :] for k in range(5))
            tt(A[0], lr, dt, ALU.mult)
            tt(A[1], li, dt, ALU.mult)
            reduce_angle(A[1], A[4], A[5], (C1, C2, C3))
            ts(A[1], A[1], 3.1415925, -3.1415925, ALU.min, ALU.max)
            tt(s5s["mag"], col(COL_LR, S5_TILES), s5s["dt"], ALU.mult)
            tt(s5s["th"], col(COL_LI, S5_TILES), s5s["dt"], ALU.mult)
            reduce_angle(s5s["th"], s5s["k"], s5s["t"], (C1, C2, C3))
            tt(A[4], lr, lr, ALU.mult)
            tt(A[5], li, li, ALU.mult)
            tt(A[4], A[4], A[5], ALU.add)
            nc.gpsimd.tensor_scalar(cc[:, 2, :, :], cc[:, 0, :, :], -1.0, None, ALU.mult)
            nc.gpsimd.tensor_scalar(cc[:, 1, :, :], cc[:, 1, :, :], -1.0, None, ALU.mult) \
              .then_inc(s["s5_arg"], 1)
            add_residual(0)
            pool.wait_ge(s["x_ready"], 4)
            pool.dma_start(gpost[:, 0, :], a["ffn2_post_g"].partition_broadcast(P)) \
                .then_inc(s["gpost_ffn2"], 16)

            pool.wait_ge(s["tables_ready"], 4)
            for r in range(8):
                nh = rope_heads(r)
                w = nh * HD
                t = r % 2
                if r < 4:
                    pool.wait_ge(s["xn_ready"], r + 1)
                    src, sin, groups = xn1[:, 0:w], ropeqk[:, 2 * (r // 2) + 1, t, :], 2
                else:
                    pool.wait_ge(s["raw_ready"], r + 1)
                    src, sin, groups = raw[:, r % 2, 0:w], rope_in[:, 3, t, :], 1
                if r >= 1:
                    pool.wait_ge(s["rop_ready"], r)
                J = HD // groups // 2
                for b in range(2):
                    if groups == 2:
                        cut = "p (h g b j) -> p b h g j"
                        cut1 = "p (g b j) -> p b g j"
                        o = t2[:, 0:w].rearrange(cut, g=groups, b=2, j=J)[:, b]
                        i0 = src.rearrange(cut, g=groups, b=2, j=J)[:, 1 - b]
                        i1 = sin.rearrange(cut1, g=groups, b=2)[:, b].unsqueeze(1) \
                                .broadcast_to([P, nh, groups, J])
                    else:
                        cut = "p (h b j) -> p b h j"
                        o = t2[:, 0:w].rearrange(cut, b=2, j=J)[:, b]
                        i0 = src.rearrange(cut, b=2, j=J)[:, 1 - b]
                        i1 = sin.rearrange("p (b j) -> p b j", b=2)[:, b].unsqueeze(1) \
                                .broadcast_to([P, nh, J])
                    nc.gpsimd.tensor_tensor(o, i0, i1, ALU.mult).then_inc(s["t2_ready"], 1)
            add_residual(1)
            pool.wait_ge(s["x_ready"], 8)
            pool.dma_start(gpost[:, 1, :], a["final_norm"].partition_broadcast(P)) \
                .then_inc(s["gpost_final"], 16)

            pool.wait_ge(s["s5_rden"], 1)
            for jb in range(4):
                g = slice(4 * jb, 4 * jb + 4)
                for j in range(4 * jb, 4 * jb + 4):
                    step.mark(nc.gpsimd.tensor_scalar(tabS[:, j, :], trow[:, :], s5s["th"][:, j:j + 1],
                                                      None, ALU.mult))
                step.done(pool)
                ang, k, t = tabS[:, g, :], tabC[:, g, :], chw[:, 4:8, :]
                reduce_angle(ang, k, t, (C1, C2))
                nc.gpsimd.tensor_scalar(ang, ang, 3.1415925, -3.1415925, ALU.min, ALU.max) \
                  .then_inc(s["angles"], 1)
            add_residual(2)
            pool.wait_ge(s["x_ready"], 12)
            nc.gpsimd.memset(xr[:, :, 0:3], 0.0).then_inc(s["zeroed"], 1)

            pool.wait_ge(s["s5_trig"], 4)
            pool.wait_ge(s["s5_rden"], 1)
            mag, sn, cs = A[0], A[2], A[3]
            tt(cs, mag, cs, ALU.mult)
            ts(cs, cs, 1.0, None, ALU.subtract, ALU.bypass)
            tt(sn, mag, sn, ALU.mult)
            tt(A[4], cs, lr, ALU.mult)
            tt(A[5], sn, li, ALU.mult)
            tt(A[4], A[4], A[5], ALU.add)
            tt(A[5], sn, lr, ALU.mult)
            tt(A[6], cs, li, ALU.mult)
            tt(A[5], A[5], A[6], ALU.subtract)
            tt(A[4], A[4], dt, ALU.mult)
            tt(A[5], A[5], dt, ALU.mult)
            tt(A[0], A[4], br, ALU.mult)
            tt(A[1], A[5], bi, ALU.mult)
            tt(A[0], A[0], A[1], ALU.subtract)
            tt(A[1], A[4], bi, ALU.mult)
            tt(A[2], A[5], br, ALU.mult)
            tt(A[1], A[1], A[2], ALU.add)
            for part in range(2):
                for g in range(2):
                    nc.gpsimd.tensor_scalar(bb[:, part, :, g, :],
                                            A[part].rearrange("p (c n) -> p c n", n=HD),
                                            col(COL_SEL + g), None, ALU.mult).then_inc(s["bb_ready"], 1)
            pool.wait_ge(s["rg_act"], 4)
            nc.gpsimd.tensor_tensor(igate[:, :, :], igate[:, :, :], xc[:, :, :], ALU.mult) \
              .then_inc(s["rg_ix"], 1)
            pool.wait_ge(s["rg_done"], 4)

            def stick_exponent(b):
                pool.wait_ge(s["z_evac"], b + 1)
                if b >= 2:
                    pool.wait_ge(s["sbo_psum"], b - 1)
                for e in range(2):
                    i = nc.gpsimd.tensor_tensor(wz[:, b % 2, e, :], zs[:, b % 2, e, :], masks[:, 1, :],
                                                ALU.add)
                i.then_inc(s["zm_ready"], 1)

            for b in range(4):
                stick_exponent(b)
                pool.wait_ge(s["sp_raw"], b + 1)
                for e in range(2):
                    i = nc.gpsimd.tensor_tensor(sp[:, b % 2, e, :], sp[:, b % 2, e, :], masks[:, 0, :],
                                                ALU.mult)
                i.then_inc(s["sp_ready"], 1)

            def s5_sum(j):
                pool.wait_ge(s["s5_mod"], 2 * (j + 1))
                r = j % 2
                nc.gpsimd.tensor_tensor(pc[:, r, 0, :], pc[:, r, 0, :], pw[:, r, 1, :], ALU.add) \
                  .then_inc(s["zin_ready"], 1)
                nc.gpsimd.tensor_tensor(pc[:, r, 1, :], pc[:, r, 1, :], pw[:, r, 0, :], ALU.subtract) \
                  .then_inc(s["zin_ready"], 1)

            s5_sum(0)
            for j in range(S5_TILES):
                if j + 1 < S5_TILES:
                    s5_sum(j + 1)
                pool.wait_ge(s["s5_scan"], 2 * (j + 1))
                if j >= 2:
                    pool.wait_ge(s["y_done"], j - 1)
                for dst, tab in ((dC, tabC), (dS, tabS)):
                    nc.gpsimd.tensor_tensor(dst[:, j % 2, :, :], zz[:, j % 2, :, :],
                                            tab[:, j, :].unsqueeze(1).broadcast_to([P, 2, SEQ]),
                                            ALU.mult).then_inc(s["s5_dem"], 1)


def kernel(**inputs):
    import concourse.bacc as bacc
    from concourse.bass_utils import run_bass_kernel_spmd

    w = {k: np.asarray(v) for k, v in inputs.items()}
    f32 = np.float32

    def ffn_items(gate, up, down):
        wide = [m.reshape(KC, P, PAIRS, 256).transpose(2, 1, 0, 3).reshape(PAIRS, P, KC * 256)
                for m in (gate, up)]
        low = down.reshape(PAIRS, 2, P, D).transpose(0, 2, 1, 3).reshape(PAIRS, P, 2 * D)
        return np.concatenate(wide + [low], axis=2)

    def mix_block(m):
        n = m.shape[1]
        out = np.zeros((P, BLK), m.dtype)
        out[:, :KC * n] = m.reshape(KC, P, n).transpose(1, 0, 2).reshape(P, KC * n)
        return out

    wffn = np.concatenate([
        ffn_items(w["ffn1_w_gate"][0], w["ffn1_w_up"][0], w["ffn1_w_down"][0]),
        ffn_items(w["ffn2_w_gate"][0], w["ffn2_w_up"][0], w["ffn2_w_down"][0]),
        ffn_items(w["ffn_w_gate_2"][0], w["ffn_w_up_2"][0], w["ffn_w_down_2"][0]),
        ffn_items(w["ffn_w_gate_2"][1], w["ffn_w_up_2"][1], w["ffn_w_down_2"][1])])
    pairs = [c + 4 * e for c in range(4) for e in range(2)]
    qkv, wo = w["w_qkv"][0], w["w_out"][0]
    qa = qkv[:, :512].reshape(D, 8, HD)[:, pairs].reshape(D, 512)
    wo = np.concatenate([wo[:512].reshape(8, HD, D)[pairs].reshape(512, D), wo[512:]])
    ab, cd = w["ab_w_in_2"][0], w["cd_w_in_2"][0]
    blocks = [qa, qkv[:, 512:768], qkv[:, 768:1280], qkv[:, 1280:1792], qkv[:, 1792:2304],
              wo[:, :512], wo[:, 512:]]
    blocks += [ab[:, :512], ab[:, 1024:1536], ab[:, 1536:2048], ab[:, 2048:2560], ab[:, 512:1024]]
    blocks += [w["ab_w_out_2"][0][:, :512], w["ab_w_out_2"][0][:, 512:]]
    blocks += [cd[:, k * 512:(k + 1) * 512] for k in range(4)]
    blocks += [w["cd_w_out_2"][0][:, :512], w["cd_w_out_2"][0][:, 512:]]
    wmix = np.stack([mix_block(b) for b in blocks])

    def column(v):
        return v.reshape(-1, P).T

    G, N, PG = 32, 64, 16
    lr, li, ldt = w["cd_lam_re_2"][0], w["cd_lam_im_2"][0], w["cd_log_dt_2"][0]
    ldt_n = np.broadcast_to(ldt[:, None], (G, N))
    in_quadrant = (np.arange(P) % 32) // PG
    cols = np.concatenate(
        [column(g) for g in (w["ffn1_pre_g"], w["mix_pre_g"], w["ffn2_pre_g"], w["ab_norm_2"],
                             w["ffn_norm_2"][0], w["cd_norm_2"], w["ffn_norm_2"][1])]
        + [column(w["ab_conv_w_2"]), column(w["ab_conv_b_2"]), column(w["ab_gate_a_b_2"]),
           column(w["ab_gate_x_b_2"]), column(w["ab_lambda_2"]), column(w["cd_d_2"]),
           column(w["cd_glu_b_2"]), column(lr), column(li), column(ldt_n),
           np.stack([in_quadrant == 0, in_quadrant == 1], 1).astype(f32),
           np.full((P, 1), math.pi / 2, f32)], axis=1)

    def by_channel(v):
        return np.repeat(v.reshape(4, 8, N).transpose(1, 0, 2), PG, axis=0).reshape(P, 4 * N)

    def b_by_channel(b):
        return b.reshape(4, 8, N, PG).transpose(1, 3, 0, 2).reshape(P, 4 * N)

    s5c = np.stack([by_channel(lr), by_channel(li), by_channel(ldt_n),
                    b_by_channel(w["cd_b_re_2"][0]), b_by_channel(w["cd_b_im_2"][0])], axis=1)
    cc = np.zeros((2, N, 2, S5_TILES, 2, PG), f32)
    for part, name in enumerate(("cd_c_re_2", "cd_c_im_2")):
        c = w[name][0].reshape(S5_TILES, 2, PG, N)
        for g in range(2):
            cc[g, :, part, :, g, :] = c[:, g].transpose(2, 0, 1)
    cc = cc.reshape(P, 2, S5_TILES, 32)
    gates = np.stack([w["ab_gate_a_w_2"][0], w["ab_gate_x_w_2"][0]])
    gates = gates.reshape(2, 4, 2, HD, HD).transpose(2, 3, 0, 1, 4)
    glu = w["cd_glu_w_2"][0].reshape(4, P, 512).transpose(1, 0, 2)
    qg, kg = w["q_norm_g"][0], w["k_norm_g"][0]
    swap = np.arange(HD).reshape(2, 2, 16)[:, ::-1].reshape(HD)
    qkg = np.broadcast_to(np.stack([qg, qg[swap], kg, kg[swap]]), (P, 4, HD))

    t = np.arange(SEQ)

    def angles(pos, dim):
        freqs = (ROPE_THETA ** (-np.arange(0, dim, 2, dtype=f32) / f32(dim))).astype(f32)
        return pos.astype(f32)[:, None] * freqs[None, :]

    def rope_tables(parts):
        cos = np.concatenate([np.cos(x) for x in parts for _ in range(2)], axis=1)
        sin = np.concatenate([sg * np.sin(x) for x in parts for sg in (-1, 1)], axis=1)
        return [m.reshape(TT, P, HD).transpose(1, 0, 2).astype(f32) for m in (cos, sin)]

    rope_in = np.stack(rope_tables([angles(t // GRID_W, HD // 2), angles(t % GRID_W, HD // 2)])
                       + rope_tables([angles(t, HD)]), axis=1)
    diff = t[None, :] - t[:, None]
    count = (np.abs(diff) <= 64).astype(f32)
    for dilation in (4, 16):
        span = {4: 512, 16: 2048}[dilation] // 2
        count += (diff % dilation == 0) & (np.abs(diff) <= span)
    biasB = np.where(count > 0, np.log(np.maximum(count, 1)) * HD ** 0.5, NEG).astype(f32)
    biasB = biasB.reshape(TT, P, SEQ).transpose(1, 0, 2)
    slopes = 2.0 ** (-8.0 * np.arange(1, 5) / 4)
    biasM = np.where(diff <= 0, slopes[:, None, None] * diff * P ** 0.5, NEG).astype(f32)
    biasM = biasM.reshape(4, TT, P, SEQ).transpose(2, 0, 1, 3)
    k = np.arange(P)
    tri = np.stack([k[:, None] >= k[None, :], np.ones((P, P), bool)], axis=1).astype(f32)
    past = k[:, None] < np.concatenate([t, t[:P]])[None, :]
    masks = np.stack([past, np.where(past, 0, NEG)], axis=1).astype(f32)

    data = {
        "x": w["x"][0].reshape(TT, P, D).transpose(1, 0, 2), "wffn": wffn, "wmix": wmix,
        "ident": np.eye(P, dtype=f32), "cols": cols, "ffn1_post_g": w["ffn1_post_g"][0],
        "mix_post_g": w["mix_post_g"][0], "ffn2_post_g": w["ffn2_post_g"][0],
        "final_norm": w["final_norm_2"], "s5c": s5c, "biasB": biasB, "rope_in": rope_in,
        "trow": np.broadcast_to(t.astype(f32), (P, SEQ)), "tri": tri, "masks": masks,
        "biasM": biasM, "glu": glu, "qkg": qkg, "cc": cc, "gates": gates,
    }
    nc = bacc.Bacc("TRN2", target_bir_lowering=False, num_devices=1)
    arrays, args = {}, {}
    for name, v in data.items():
        arrays["in_" + name] = np.ascontiguousarray(v)
        args[name] = nc.dram_tensor("in_" + name, v.shape, F32, kind="ExternalInput").ap()
    args["out"] = nc.dram_tensor("out_x", (P, TT, D), F32, kind="ExternalOutput").ap()
    build(nc, args)
    got = run_bass_kernel_spmd(nc, [arrays], core_ids=[0]).results[0]["out_x"]
    return np.asarray(got).reshape(P, TT, D).transpose(1, 0, 2).reshape(1, SEQ, D)
```

```python
from contextlib import ExitStack
import math

import numpy as np
import concourse.bass as bass
from concourse import mybir

F32 = mybir.dt.float32
F32R = mybir.dt.float32r
ACT = mybir.ActivationFunctionType
ALU = mybir.AluOpType
AX = mybir.AxisListType

P = 128
SEQ = 256
TT = SEQ // P
D = 1024
KC = D // P
FF = 2816
FCH = FF // P
HD = 64
EPS = 1e-6
NEG = -1e30
GU = 2 * KC * P
N_NORM = 7
S5_TILES = 16
TWO_PI = 2 * math.pi
C1 = 6.28125
C2 = 0.0019350051879882812
C3 = TWO_PI - C1 - C2
MAGIC = 1.5 * 2.0 ** 23
ROPE_THETA = 10000.0
GRID_W = 64

COL_GAIN = 0
COL_CONV = COL_GAIN + N_NORM * KC
COL_CONVB = COL_CONV + 16
COL_BA = COL_CONVB + 4
COL_BX = COL_BA + 4
COL_LAM = COL_BX + 4
COL_DSKIP = COL_LAM + 4
COL_GLUB = COL_DSKIP + 4
COL_LR = COL_GLUB + 4
COL_LI = COL_LR + S5_TILES
COL_LDT = COL_LI + S5_TILES
COL_SEL = COL_LDT + S5_TILES
COL_HALFPI = COL_SEL + 2
N_COLS = COL_HALFPI + 1

MIX_IN = (9, 10, 8)
MIX_OUT = 4
STREAM = [("ffn", 0), ("mix", 0), ("ffn", 1), ("mix", 1), ("ffn", 2), ("mix", 2), ("ffn", 3)]


def part_base(kind, n):
    at = 0
    for k, m in STREAM:
        if (k, m) == (kind, n):
            return at
        at += FCH if k == "ffn" else MIX_IN[m] + MIX_OUT
    return at


FFN_ITEM = [part_base("ffn", n) for n in range(4)]
MIX_ITEM = [part_base("mix", n) for n in range(3)]
N_ITEMS = FFN_ITEM[3] + FCH
UNITS = [sum(MIX_IN[:m]) + MIX_OUT * m for m in range(4)]


class Step:

    def __init__(self, sem):
        self.sem, self.count = sem, 0

    def mark(self, instruction):
        self.count += 1
        instruction.then_inc(self.sem, 1)

    def done(self, engine):
        engine.wait_ge(self.sem, self.count)


def build(nc, a):
    with ExitStack() as ctx:
        def sb(name, shape, dtype=F32):
            return ctx.enter_context(nc.sbuf_tensor(name, shape, dtype))

        def sem(name):
            return ctx.enter_context(nc.semaphore(name))

        x = sb("x", [P, TT, D])
        hT = [sb("hT_" + part, [P, KC, SEQ], F32R) for part in ("high", "low")]
        gu_raw = sb("gu_raw", [P, 2, GU])
        dn_raw = sb("dn_raw", [P, 2, D])
        gu = [sb("gu_" + part, [P, 2, GU], F32R) for part in ("high", "low")]
        dn = [sb("dn_" + part, [P, 2, D], F32R) for part in ("high", "low")]
        act_s = [sb("act_" + part, [P, 2, SEQ], F32R) for part in ("high", "low")]
        ffn_s = sb("ffn_s", [P, 4, SEQ])
        sil_s, prod_s = ffn_s[:, 0:2, :], ffn_s[:, 2:4, :]
        gpost = sb("gpost", [P, 2, D])
        ident = sb("ident", [P, P])
        cols = sb("cols", [P, N_COLS])
        s5in = sb("s5in", [P, 6 * SEQ])
        s5c = s5in[:, 0:5 * SEQ].rearrange("p (k n) -> p k n", k=5)
        trow = s5in[:, 5 * SEQ:]
        cc = s5in[:, :].rearrange("p (k j c) -> p k j c", k=3, c=32)
        bb = sb("bb", [P, 2, 4, 2, HD])
        small = sb("small", [P, 256])
        stat = sb("stat", [P, 20, 4])
        TABLES = 11008
        chw = sb("chw", [P, 8, SEQ])[:, :, :]
        scratch = sb("scratch", [P, TABLES + 2 * S5_TILES * SEQ])
        ps = ctx.enter_context(nc.psum_tensor("ps", [P, 8 * 512], F32))

        def bank(i, n=1):
            return ps[:, i * 512:(i + n) * 512]

        at, limit = [0], [TABLES + 2 * S5_TILES * SEQ]

        def take(n):
            at[0] += n
            assert at[0] <= limit[0], at[0]
            return scratch[:, at[0] - n:at[0]]

        postw = scratch[:, 0:2 * D].rearrange("p (t n) -> p t n", t=TT)
        tabS = scratch[:, TABLES:TABLES + S5_TILES * SEQ].rearrange("p (j t) -> p j t", t=SEQ)
        tabC = scratch[:, TABLES + S5_TILES * SEQ:].rearrange("p (j t) -> p j t", t=SEQ)
        hn = postw

        at[0] = 2 * D
        biasB = take(TT * SEQ).rearrange("p (t k) -> p t k", t=TT)
        axial = take(2 * TT * HD).rearrange("p (k t d) -> p k t d", k=2, t=TT)
        qkg = take(4 * HD).rearrange("p (k d) -> p k d", k=4)
        rope_q = take(2 * TT * 4 * HD).rearrange("p (k t h d) -> p k t h d", k=2, t=TT, h=4)
        rope_k = take(2 * TT * 2 * HD).rearrange("p (k t h d) -> p k t h d", k=2, t=TT, h=2)
        rope_b = take(2 * TT * 4 * HD).rearrange("p (k t h d) -> p k t h d", k=2, t=TT, h=4)
        qT = [take(4 * SEQ).rearrange("p (c s) -> p c s", s=SEQ) for _ in range(2)]
        kTA = take(SEQ)
        kTB = take(4 * SEQ).rearrange("p (c s) -> p c s", s=SEQ)
        vA = take(TT * P).rearrange("p (t n) -> p t n", t=TT)
        vB = take(TT * 512).rearrange("p (t n) -> p t n", t=TT)
        raw = take(2 * 512).rearrange("p (r n) -> p r n", r=2)
        xn1 = take(512)
        t1 = take(512)
        t2 = take(512)
        rop = take(2 * 512).rearrange("p (r n) -> p r n", r=2)
        pT = [take(2 * 512).rearrange("p (r n) -> p r n", r=2)]
        at[0] = 0
        probs = [take(3 * 512).rearrange("p (r n) -> p r n", r=3)]
        ssc = [raw]
        at[0], limit[0] = TABLES - 2048, TABLES
        tri = take(2 * P).rearrange("p (k m) -> p k m", k=2)
        masks = take(2 * 384).rearrange("p (k m) -> p k m", k=2)
        gbd = take(2 * 4 * P).rearrange("p (w c m) -> p w c m", w=2, c=4)
        at[0], limit[0] = 0, TABLES - 2048
        qS = take(4 * SEQ).rearrange("p (c s) -> p c s", c=4)
        kS = take(4 * SEQ).rearrange("p (c s) -> p c s", c=4)
        vS = take(TT * 512).rearrange("p (t n) -> p t n", t=TT)
        after = at[0]
        xr = take(4 * (SEQ + 3)).rearrange("p (c s) -> p c s", c=4)
        xc = take(4 * SEQ).rearrange("p (c s) -> p c s", c=4)
        gg = ffn_s
        rgate = take(4 * SEQ).rearrange("p (c s) -> p c s", c=4)
        igate = take(4 * SEQ).rearrange("p (c s) -> p c s", c=4)
        rga = take(4 * SEQ).rearrange("p (c s) -> p c s", c=4)
        at[0] = after
        zs, lg, sp = (take(2 * 768).rearrange("p (r h s) -> p r h s", r=2, h=2) for _ in range(3))
        wz = chw[:, 0:6, :].rearrange("p a b -> p (a b)").rearrange("p (r h s) -> p r h s", r=2, h=2)
        glu = scratch[:, TABLES - 2048:TABLES].rearrange("p (k m) -> p k m", k=4)
        biasM = chw.rearrange("p (m t) k -> p m t k", m=4)
        at[0] = 0
        uT = take(4 * SEQ).rearrange("p (c s) -> p c s", c=4)
        qM = take(4 * SEQ).rearrange("p (c s) -> p c s", c=4)
        kM = take(4 * SEQ).rearrange("p (c s) -> p c s", c=4)
        vM = take(TT * 512).rearrange("p (t n) -> p t n", t=TT)
        yT = take(4 * SEQ).rearrange("p (c s) -> p c s", c=4)
        after = at[0]
        pc, pw = (chw[:, k:k + 4, :].rearrange("p (r h) s -> p r h s", r=2) for k in (0, 4))
        zz, dC, dS = (take(2 * 512).rearrange("p (r h s) -> p r h s", r=2, h=2) for _ in range(3))
        at[0] = after
        probs.append(take(3 * 512).rearrange("p (r n) -> p r n", r=3))
        pT.append(take(2 * 512).rearrange("p (r n) -> p r n", r=2))
        ssc.append(take(2 * 512).rearrange("p (r n) -> p r n", r=2))

        names = ["ss", "var", "std", "rinv", "pss", "pvar", "pstd", "prinv"]
        st = {n: small[:, 2 * k:2 * k + 2] for k, n in enumerate(names)}
        qk = {n: small[:, 16 + 8 * k:24 + 8 * k] for k, n in enumerate(["ss", "var", "std", "rinv"])}
        lam = {n: small[:, 48 + 4 * k:52 + 4 * k]
               for k, n in enumerate(["e", "den", "s", "s2", "acc", "pos", "neg8", "pos8"])}
        s5s = {n: small[:, 80 + 16 * k:96 + 16 * k] for k, n in enumerate(["dt", "mag", "th", "k", "t"])}

        def col(k, n=1):
            return cols[:, k:k + n]

        s = {n: sem(n) for n in [
            "x_loaded", "early_loaded", "s5c_loaded", "late_loaded", "ab_loaded", "cd_loaded",
            "biasM_loaded", "gu_loaded0", "gu_loaded1", "dn_loaded0", "dn_loaded1", "gpost_loaded", "gpost_ffn2", "gpost_final", "out_stored",
            "sq_done", "var_ready", "std_ready", "hn_ready", "hT_psum", "hT_high", "hT_low",
            "gu_high", "gu_split", "dn_high", "dn_split",
            "gate_ready", "up_ready", "silu_ready", "prod_done", "act_high", "act_ready", "down_done",
            "ffn_tt0",
            "psq_done", "pvar_ready", "pstd_ready", "post_t", "x_ready", "final_ready",
            "proj_done", "proj_free", "raw_ready", "qkvar_ready", "qkstd_ready", "xn_ready", "t2_ready",
            "rop_ready", "ropT_psum", "ropT_evac",
            "s_ready", "max_ready", "p_ready", "pn_ready", "pt_psum", "pt_ready", "v_done", "o_high", "o_ready",
            "tables_ready", "exp_dt", "lam_e", "lam_s", "s5_arg", "s5_trig", "s5_rden", "angles", "trig",
            "zeroed", "conv_done", "gates_done", "rg_act", "rg_q", "rg_sqrt", "rg_ix", "rg_y", "rg_high", "rg_done",
            "z_psum", "z_evac", "z_abs", "z_log", "sp_raw", "sp_ready", "zm_ready", "r_psum", "t_ready",
            "w_ready", "sbo_psum", "sbo_high", "sbo_done",
            "bb_ready", "cc_ready", "bu_done", "s5_mod", "zin_ready", "s5_scan", "s5_dem", "y_done", "y_sum",
            "y_gelu", "glu_psum", "glu_sig", "s5_y", "s5_high", "s5_done",
            "dve_step", "act_step", "pool_step"]}
        gu_loaded = [s["gu_loaded0"], s["gu_loaded1"]]
        dn_loaded = [s["dn_loaded0"], s["dn_loaded1"]]

        def loaded(item):
            return 16 * (item // 2 + 1)

        def during(i, r):
            if r is None:
                return (lambda c: c + i), (lambda c: loaded(c + i))
            return (lambda c: r * 2 + (c + i)), (lambda c: r * 16 + loaded(c + i))

        PASSES = ((0, 0), (0, 1), (1, 0))

        def wait_used(engine, g):
            for f in range(4):
                if FFN_ITEM[f] <= g < FFN_ITEM[f] + FCH:
                    engine.wait_ge(s["up_ready"], FCH * f + g - FFN_ITEM[f] + 1)
            for m in range(3):
                if MIX_ITEM[m] <= g < MIX_ITEM[m] + MIX_IN[m] + MIX_OUT:
                    engine.wait_ge(s["proj_done"], UNITS[m] + g - MIX_ITEM[m] + 1)

        def pre_x(n, t):
            return 4 * (n - 1) + 2 * (t + 1)

        def wait_unit(engine, m, j):
            if m == 0 and j < 7:
                engine.wait_ge(s["raw_ready"], j + 1)
            else:
                engine.wait_ge(s["proj_free"], (j - 6, j + 3, j + 13)[m])

        def rope_heads(r):
            return 2 if r == 2 else 4

        def rope_dst(r):
            if r == 2:
                return kTA.unsqueeze(1)
            dst, u = {0: (qT[0], 0), 1: (qT[0], 1), 3: (qT[1], 0), 4: (qT[1], 1), 5: (kTB, 0),
                      6: (kTB, 1)}[r]
            return dst[:, 2 * u:2 * u + 2, :]

        def head(a_, q, k, v, bias, scale, phase, o, heads_out, out_free):
            biased = bias is not None
            return dict(a=a_, q=q, k=k, v=v, bias=bias, scale=scale, o=o, heads_out=heads_out,
                        out_free=out_free,
                        exp_in=ssc[phase][:, a_ % 2, :] if biased else bank(a_ % 3),
                        exp_scale=1.0 if biased else scale,
                        probs=probs[phase][:, a_ % 3, :], pT=pT[phase][:, a_ % 2, :])

        heads1 = []
        for pair in range(8):
            for e in range(2):
                half = slice(64 * e, 64 * e + 64)
                c = pair % 4
                obank = bank(5 + pair % 2)
                dense = pair < 4
                heads1.append(head(
                    2 * pair + e, qT[0 if dense else 1][half, c, :],
                    kTA[half, :] if dense else kTB[half, c, :],
                    vA[:, :, half] if dense else vB[:, :, (2 * c + e) * HD:(2 * c + e + 1) * HD],
                    None if dense else biasB[:, :, :], HD ** -0.5, 0, obank[half, 0:SEQ],
                    (obank[:, 0:SEQ], pair) if e else None,
                    pair - 1 if pair >= 2 else None))
        heads2 = []
        for m in range(4):
            obank = bank(5 + m % 2)[:, 0:SEQ]
            heads2.append(head(16 + m, qM[:, m, :], kM[:, m, :], vM[:, :, m * P:(m + 1) * P],
                               biasM[:, m, :, :], P ** -0.5, 1, obank, (obank, 4 + m),
                               8 + m - 1 if m >= 2 else None))

        block = ctx.enter_context(nc.Block())

        @block.sync
        def _(sp_):
            sp_.dma_start(x[:, :, :], a["x"]).then_inc(s["x_loaded"], 16)

            def load_gu(g, slot, guard=True):
                if guard:
                    sp_.wait_ge(s["gu_split"], g - 1)
                sp_.dma_start(gu_raw[:, slot, :], a["wgu"][g]).then_inc(gu_loaded[slot], 16)

            def load_dn(d, slot, guard=True):
                if guard:
                    sp_.wait_ge(s["dn_split"], d - 1)
                sp_.dma_start(dn_raw[:, slot, :], a["wdn"][d]).then_inc(dn_loaded[slot], 16)

            for g in range(4):
                if g == 2:
                    for d in range(2):
                        load_dn(d, d, guard=False)
                load_gu(g, g % 2, guard=g >= 2)
            for kind, n in STREAM:
                if kind == "ffn":
                    base, d0 = FFN_ITEM[n], FCH * n
                    load_dn(d0 + 2, d0 % 2)
                    whole = min(FCH - 2, N_ITEMS - 4 - base) // 2
                    with sp_.Fori(0, whole) as r:
                        for h in range(2):
                            load_dn(r * 2 + (d0 + h + 3), (d0 + h + 3) % 2)
                            load_gu(r * 2 + (base + h + 4), (base + h) % 2)
                    for i in range(2 * whole, FCH):
                        if i <= FCH - 2 and d0 + i + 3 < 4 * FCH:
                            load_dn(d0 + i + 3, (d0 + i + 3) % 2)
                        if base + i + 4 < N_ITEMS:
                            load_gu(base + i + 4, (base + i) % 2)
                else:
                    for g in range(MIX_ITEM[n] + 4, MIX_ITEM[n] + MIX_IN[n] + MIX_OUT + 4):
                        load_gu(g, g % 2)
            for t in range(TT):
                sp_.wait_ge(s["final_ready"], t + 1)
                sp_.dma_start(a["out"][:, t, :], hn[:, t, :]).then_inc(s["out_stored"], 16)
            sp_.wait_ge(s["out_stored"], 16 * TT)

        @block.tensor
        def _(pe):
            def transposes(n):
                for t in range(TT):
                    pe.wait_ge(s["hn_ready"], TT * n + t + 1)
                    if n == 0 and t == 0:
                        pe.wait_ge(s["early_loaded"], 32)
                    for c in range(KC):
                        at_ = (c % 2) * SEQ + t * P
                        i = nc.tensor.transpose(bank(4 + c // 2)[:, at_:at_ + P],
                                                hn[:, t, c * P:(c + 1) * P], ident[:, :])
                        if t == 1 and c % 2 == 1:
                            i.then_inc(s["hT_psum"], 1)

            def wait_hT(n, k):
                pe.wait_ge(s["hT_low"], KC * n + k + 1)

            def gate_up(h, sl, item, G, first=None):
                pe.wait_ge(s["gu_split"], item + 1)
                if not isinstance(G, int) or G >= 2:
                    pe.wait_ge(s["prod_done"], G - 1)
                for w in range(2):
                    for k in range(KC):
                        if first is not None and w == 0:
                            wait_hT(first, k)
                            if k == 0:
                                wait_hT(first, 1)
                        o = (w * KC + k) * P
                        for pw_, px in PASSES:
                            i = nc.tensor.matmul(bank(4 + 2 * w + h)[:, 0:SEQ],
                                                 gu[pw_][:, sl, o:o + P], hT[px][:, k, :],
                                                 start=(pw_, px, k) == (0, 0, 0),
                                                 stop=(pw_, px, k) == (1, 0, KC - 1))
                    i.then_inc(s["gate_ready" if w == 0 else "up_ready"], 1)

            def down(h, G, start=False, stop=False):
                pe.wait_ge(s["dn_split"], G + 1)
                pe.wait_ge(s["act_ready"], G + 1)
                for t in range(TT):
                    for px, pw_ in PASSES:
                        for half in range(2):
                            i = nc.tensor.matmul(bank(2 * t + half), act_s[px][:, h, t * P:(t + 1) * P],
                                                 dn[pw_][:, h, half * 512:half * 512 + 512],
                                                 start=start and (px, pw_) == (0, 0),
                                                 stop=stop and (px, pw_) == (1, 0))
                    if stop and t == 0:
                        i.then_inc(s["ffn_tt0"], 1)
                i.then_inc(s["down_done"], 1)

            def ffn(f, n):
                base, G0 = FFN_ITEM[f], FCH * f
                gate_up(0, base % 2, base, G0, first=n)
                gate_up(1, 1 - base % 2, base + 1, G0 + 1)
                down(0, G0, start=True)
                with pe.Fori(1, FCH // 2) as r:
                    for h in range(2):
                        gate_up(h, (base + h) % 2, r * 2 + (base + h), r * 2 + (G0 + h))
                        down(1 - h, r * 2 + (G0 + h - 1))
                down(1, G0 + FCH - 1, stop=True)

            def project(m, v, n, feature):
                item = MIX_ITEM[m] + v
                sl = item % 2
                pe.wait_ge(s["gu_split"], item + 1)
                if v >= 4:
                    wait_unit(pe, m, v - 4)
                out = bank(v % 4)
                for h in range(2):
                    for k in range(KC):
                        if v == 0 and h == 0:
                            wait_hT(n, k)
                        for pw_, px in PASSES:
                            wk = gu[pw_][:, sl, k * SEQ:(k + 1) * SEQ]
                            cut_ = slice(h * P, (h + 1) * P)
                            lhsT, rhs = ((wk[:, cut_], hT[px][:, k, :]) if feature
                                         else (hT[px][:, k, cut_], wk))
                            i = nc.tensor.matmul(out[:, h * SEQ:(h + 1) * SEQ], lhsT, rhs,
                                                 start=(pw_, px, k) == (0, 0, 0),
                                                 stop=(pw_, px, k) == (1, 0, KC - 1))
                i.then_inc(s["proj_done"], 1)

            def project_out(m, ready):
                for u in range(MIX_OUT):
                    item = MIX_ITEM[m] + MIX_IN[m] + u
                    pe.wait_ge(s["gu_split"], item + 1)
                    for t in range(TT):
                        out = bank(2 * t + u // 2)[:, (u % 2) * SEQ:(u % 2 + 1) * SEQ]
                        for k in range(KC):
                            if u == 0 and t == 0:
                                name, value = ready(k)
                                pe.wait_ge(s[name], value)
                            for pw_, px in PASSES:
                                i = nc.tensor.matmul(out, hT[px][:, k, t * P:(t + 1) * P],
                                                     gu[pw_][:, item % 2, k * SEQ:(k + 1) * SEQ],
                                                     start=(pw_, px, k) == (0, 0, 0),
                                                     stop=(pw_, px, k) == (1, 0, KC - 1))
                    i.then_inc(s["proj_done"], 1)

            def attention(heads):
                first, last = heads[0]["a"], heads[-1]["a"]
                for step in range(first, last + 4):
                    if step <= last:
                        h = heads[step - first]
                        if step >= first + 3:
                            pe.wait_ge(s["p_ready"], step - 2)
                        for t in range(TT):
                            i = nc.tensor.matmul(bank(step % 3)[:, t * SEQ:(t + 1) * SEQ],
                                                 h["q"][:, t * P:(t + 1) * P], h["k"],
                                                 start=True, stop=True)
                        i.then_inc(s["s_ready"], 1)
                    e = step - 2
                    if first <= e <= last:
                        pe.wait_ge(s["pn_ready"], e + 1)
                        if e >= first + 2:
                            pe.wait_ge(s["pt_ready"], e - 1)
                        pr = heads[e - first]["probs"]
                        for kt in range(TT):
                            for t in range(TT):
                                o = kt * SEQ + t * P
                                i = nc.tensor.transpose(bank(3 + e % 2)[:, o:o + P],
                                                        pr[:, t * SEQ + kt * P:t * SEQ + (kt + 1) * P],
                                                        ident[:, :])
                        i.then_inc(s["pt_psum"], 1)
                    e = step - 3
                    if first <= e <= last:
                        h = heads[e - first]
                        pe.wait_ge(s["pt_ready"], e + 1)
                        if h["out_free"] is not None:
                            pe.wait_ge(s["o_ready"], h["out_free"])
                        for kt in range(TT):
                            i = nc.tensor.matmul(h["o"], h["v"][:, kt, :],
                                                 h["pT"][:, kt * SEQ:(kt + 1) * SEQ],
                                                 start=kt == 0, stop=kt == TT - 1)
                        i.then_inc(s["v_done"], 1)

            transposes(0)
            ffn(0, 0)
            transposes(1)
            for v in range(9):
                project(0, v, 1, False)
                r = v - 1
                if 0 <= r < 7:
                    pe.wait_ge(s["rop_ready"], r + 1)
                    if r >= 2:
                        pe.wait_ge(s["ropT_evac"], r - 1)
                    w = rope_heads(r) * HD
                    for c in range(w // P):
                        for t in range(TT):
                            i = nc.tensor.transpose(
                                bank(4 + r % 2)[:, c * SEQ + t * P:c * SEQ + (t + 1) * P],
                                rop[:, r % 2, t * w + c * P:t * w + (c + 1) * P], ident[:, :])
                    i.then_inc(s["ropT_psum"], 1)
            pe.wait_ge(s["ropT_evac"], 7)
            wait_unit(pe, 0, 8)
            attention(heads1)
            project_out(0, lambda k: ("o_ready", k + 1))
            transposes(2)
            ffn(1, 2)

            transposes(3)
            for v in range(4):
                project(1, v, 3, True)
            pe.wait_ge(s["conv_done"], 4)
            pe.wait_ge(s["ab_loaded"], 48)
            for w in range(2):
                for c in range(4):
                    i = nc.tensor.matmul(bank(4 + 2 * w, 2)[:, c * SEQ:(c + 1) * SEQ], gbd[:, w, c, :],
                                         xc[:, c, :], start=True, stop=True)
            i.then_inc(s["gates_done"], 1)
            for v in range(4, 10):
                project(1, v, 3, v // 2 != 3)
            pe.wait_ge(s["rg_done"], 4)
            wait_unit(pe, 1, 9)

            def stick_scores(b):
                if b >= 2:
                    pe.wait_ge(s["z_evac"], b - 1)
                for e in range(2):
                    r0 = slice(64 * e, 64 * e + 64)
                    z = bank(2 * (b % 2) + e)
                    nc.tensor.matmul(z[:, 0:SEQ], kS[r0, b, 0:P], qS[r0, b, :], start=True, stop=True)
                    i = nc.tensor.matmul(z[:, SEQ:384], kS[r0, b, P:SEQ], qS[r0, b, P:SEQ],
                                         start=True, stop=True)
                i.then_inc(s["z_psum"], 1)

            def stick_sums(b):
                pe.wait_ge(s["sp_ready"], b + 1)
                if b >= 1:
                    pe.wait_ge(s["t_ready"], b)
                for e in range(2):
                    R = bank(4 + e)
                    w = sp[:, b % 2, e, :]
                    nc.tensor.matmul(R[:, 0:SEQ], tri[:, 0, :], w[:, 0:SEQ], start=True, stop=False)
                    nc.tensor.matmul(R[:, P:SEQ], tri[:, 1, :], w[:, SEQ:384], start=False, stop=True)
                    i = nc.tensor.matmul(R[:, SEQ:384], tri[:, 0, :], w[:, SEQ:384], start=True, stop=True)
                i.then_inc(s["r_psum"], 1)

            def stick_values(b):
                pe.wait_ge(s["w_ready"], b + 1)
                if b >= 2:
                    pe.wait_ge(s["sbo_done"], b - 1)
                for e in range(2):
                    o = bank(6 + b % 2)[64 * e:64 * e + 64, :]
                    w = wz[:, b % 2, e, :]
                    v = vS[:, :, (2 * b + e) * HD:(2 * b + e + 1) * HD]
                    nc.tensor.matmul(o[:, 0:SEQ], v[:, 0, :], w[:, 0:SEQ], start=True, stop=False)
                    i = nc.tensor.matmul(o[:, P:SEQ], v[:, 1, :], w[:, SEQ:384], start=False, stop=True)
                i.then_inc(s["sbo_psum"], 1)

            stick_scores(0)
            stick_scores(1)
            for b in range(4):
                stick_sums(b)
                if b + 2 < 4:
                    stick_scores(b + 2)
                stick_values(b)
            project_out(1, lambda k: ("rg_done", k + 1) if k < 4 else ("sbo_done", k - 3))
            transposes(4)
            ffn(2, 4)

            transposes(5)
            project(2, 0, 5, True)
            project(2, 1, 5, True)
            wait_unit(pe, 2, 1)
            pe.wait_ge(s["bb_ready"], 4)

            def s5_in(j):
                c, q = j // 4, j % 4
                if j >= 2:
                    pe.wait_ge(s["s5_mod"], 2 * (j - 1))
                r0 = slice(32 * q, 32 * q + 32)
                for part in range(2):
                    i = nc.tensor.matmul(bank(4 + j % 2)[:, part * SEQ:(part + 1) * SEQ],
                                         bb[r0, part, c, :, :].rearrange("p g n -> p (g n)"),
                                         uT[r0, c, :], start=True, stop=True)
                i.then_inc(s["bu_done"], 1)

            def s5_out(j):
                c, q = j // 4, j % 4
                pe.wait_ge(s["s5_dem"], 2 * (j + 1))
                out = bank(6, 2)[32 * q:32 * q + 32, c * SEQ:(c + 1) * SEQ]
                r = j % 2
                terms = [(0, dC[:, r, 0, :]), (2, dS[:, r, 1, :]), (1, dS[:, r, 0, :]), (1, dC[:, r, 1, :])]
                for k, (w, z) in enumerate(terms):
                    i = nc.tensor.matmul(out, cc[:, w, j, :], z, start=k == 0, stop=k == 3)
                i.then_inc(s["y_done"], 1)

            pe.wait_ge(s["cc_ready"], 1)
            s5_in(0)
            s5_in(1)
            for j in range(S5_TILES):
                if j % 2 == 0 and j < 12:
                    v = 2 + j // 2
                    project(2, v, 5, v // 2 != 3)
                s5_out(j)
                if j + 2 < S5_TILES:
                    s5_in(j + 2)
            wait_unit(pe, 2, 7)
            for o in range(4):
                for k in range(4):
                    if o == 0:
                        pe.wait_ge(s["y_gelu"], k + 1)
                    i = nc.tensor.matmul(bank(4 + o)[:, 0:SEQ], glu[:, k, o * P:(o + 1) * P], yT[:, k, :],
                                         start=k == 0, stop=k == 3)
                i.then_inc(s["glu_psum"], 1)
            pe.wait_ge(s["s5_done"], 4)
            attention(heads2)
            project_out(2, lambda k: ("s5_done", k + 1) if k < 4 else ("o_ready", 8 + k - 3))
            transposes(6)
            ffn(3, 6)

        @block.scalar
        def _(act):
            step = Step(s["act_step"])
            for name, dst in (("ident", ident[:, :]), ("cols", cols[:, :])):
                act.dma_start(dst, a[name]).then_inc(s["early_loaded"], 16)
            for k, name in enumerate(("ffn1_post_g", "mix_post_g")):
                act.dma_start(gpost[:, k, :], a[name].partition_broadcast(P)).then_inc(s["gpost_loaded"], 16)
            act.dma_start(s5in[:, :], a["s5in"]).then_inc(s["s5c_loaded"], 16)
            for name, dst in (("biasB", biasB[:, :, :]), ("axial", axial[:, :, :, :]),
                              ("qkg", qkg[:, :, :]), ("rope_b", rope_b[:, :, :, :, :])):
                act.dma_start(dst, a[name]).then_inc(s["late_loaded"], 16)

            def gu_high(g):
                if g >= 2:
                    wait_used(act, g - 2)
                act.wait_ge(gu_loaded[g % 2], loaded(g))
                nc.scalar.activation(gu[0][:, g % 2, :], gu_raw[:, g % 2, :], ACT.Copy) \
                  .then_inc(s["gu_high"], 1)

            def dn_high_first(f):
                act.wait_ge(dn_loaded[0], loaded(FCH * f))
                nc.scalar.activation(dn[0][:, 0, :], dn_raw[:, 0, :], ACT.Copy).then_inc(s["dn_high"], 1)

            def norm(n):
                for t in range(TT):
                    if n == 0:
                        if t == 0:
                            act.wait_ge(s["x_loaded"], 16)
                    else:
                        act.wait_ge(s["x_ready"], pre_x(n, t))
                    nc.scalar.activation(postw[:, t, :], x[:, t, :], ACT.Square,
                                         accum_out=st["ss"][:, t:t + 1]).then_inc(s["sq_done"], 1)
                act.wait_ge(s["var_ready"], n + 1)
                nc.scalar.activation(st["std"], st["var"], ACT.Sqrt).then_inc(s["std_ready"], 1)

            def norm_out(n):
                for c in range(KC):
                    act.wait_ge(s["hT_psum"], 4 * n + c // 2 + 1)
                    nc.scalar.activation(hT[0][:, c, :], bank(4 + c // 2)[:, c % 2 * SEQ:(c % 2 + 1) * SEQ],
                                         ACT.Copy, scale=col(COL_GAIN + n * KC + c)) \
                      .then_inc(s["hT_high"], 1)

            def ffn(f):
                base, G0 = FFN_ITEM[f], FCH * f

                def step_of(i, r=None):
                    plain, arrived = during(i, r)
                    h, static = i % 2, r is None
                    act.wait_ge(s["gate_ready"], plain(G0 + 1))
                    if not static or G0 + i >= 2:
                        act.wait_ge(s["prod_done"], plain(G0 - 1))
                    nc.scalar.activation(sil_s[:, h, :], bank(4 + h)[:, 0:SEQ], ACT.Silu) \
                      .then_inc(s["silu_ready"], 1)
                    if not static or i < FCH - 1:
                        act.wait_ge(dn_loaded[1 - h], arrived(G0 + 1))
                        if not static or G0 + i > 0:
                            act.wait_ge(s["down_done"], plain(G0))
                        nc.scalar.activation(dn[0][:, 1 - h, :], dn_raw[:, 1 - h, :], ACT.Copy) \
                          .then_inc(s["dn_high"], 1)
                    sl = (base + i) % 2
                    if not static or base + i + 2 < N_ITEMS:
                        act.wait_ge(gu_loaded[sl], arrived(base + 2))
                        act.wait_ge(s["up_ready"], plain(G0 + 1))
                        nc.scalar.activation(gu[0][:, sl, :], gu_raw[:, sl, :], ACT.Copy) \
                          .then_inc(s["gu_high"], 1)

                step_of(0)
                step_of(1)
                with act.Fori(1, FCH // 2 - 1) as r:
                    for i in range(2):
                        step_of(i, r)
                step_of(FCH - 2)
                step_of(FCH - 1)

            def evacuate(m, v, dst, func=ACT.Copy):
                gu_high(MIX_ITEM[m] + v + 2)
                act.wait_ge(s["proj_done"], UNITS[m] + v + 1)
                src = bank(v % 4).rearrange("p (h s) -> p h s", h=2)
                nc.scalar.activation(dst, src, func).then_inc(s["proj_free"], 1)

            def out_splits(m):
                for u in range(MIX_OUT - 1):
                    gu_high(MIX_ITEM[m] + MIX_IN[m] + u + 2)

            def next_splits(f):
                if f:
                    gu_high(FFN_ITEM[f] + 1)
                dn_high_first(f)

            def post(p, wait_out):
                for t in range(TT):
                    wait_out(act, t)
                    nc.scalar.activation(postw[:, t, :], bank(2 * t, 2), ACT.Square,
                                         accum_out=st["pss"][:, t:t + 1]).then_inc(s["psq_done"], 1)
                act.wait_ge(s["pvar_ready"], p + 1)
                nc.scalar.activation(st["pstd"], st["pvar"], ACT.Sqrt).then_inc(s["pstd_ready"], 1)

            def attention(heads):
                first, last = heads[0]["a"], heads[-1]["a"]
                for e in range(first, last + 4):
                    if e <= last:
                        h = heads[e - first]
                        act.wait_ge(s["max_ready"], e + 1)
                        if e >= first + 3:
                            act.wait_ge(s["pt_psum"], e - 2)
                        for t in range(TT):
                            i = nc.scalar.activation(
                                h["probs"][:, t * SEQ:(t + 1) * SEQ], h["exp_in"][:, t * SEQ:(t + 1) * SEQ],
                                ACT.Exp, bias=stat[:, h["a"], t:t + 1], scale=h["exp_scale"],
                                accum_out=stat[:, h["a"], 2 + t:3 + t])
                        i.then_inc(s["p_ready"], 1)
                    g = e - 2
                    if first <= g <= last:
                        h = heads[g - first]
                        act.wait_ge(s["pt_psum"], g + 1)
                        if g >= first + 2:
                            act.wait_ge(s["v_done"], g - 1)
                        nc.scalar.activation(h["pT"], bank(3 + g % 2), ACT.Copy).then_inc(s["pt_ready"], 1)
                    g = e - 3
                    if first <= g <= last and heads[g - first]["heads_out"] is not None:
                        act.wait_ge(s["v_done"], g + 1)
                        src, c = heads[g - first]["heads_out"]
                        nc.scalar.activation(hT[0][:, c, :], src, ACT.Copy).then_inc(s["o_high"], 1)

            norm(0)
            act.wait_ge(s["s5c_loaded"], 16)
            act.wait_ge(s["early_loaded"], 32)
            step.mark(nc.scalar.activation(lam["e"], col(COL_LAM, 4), ACT.Abs))
            nc.scalar.activation(s5s["dt"], col(COL_LDT, S5_TILES), ACT.Exp).then_inc(s["exp_dt"], 1)
            nc.scalar.activation(s5c[:, 2, :], s5c[:, 2, :], ACT.Exp).then_inc(s["exp_dt"], 1)
            step.done(act)
            nc.scalar.activation(lam["e"], lam["e"], ACT.Exp, scale=-1.0).then_inc(s["lam_e"], 1)
            gu_high(0)
            norm_out(0)
            gu_high(1)
            next_splits(0)
            ffn(0)
            post(0, lambda e, t: e.wait_ge(*((s["ffn_tt0"], 1) if t == 0 else (s["down_done"], FCH))))
            norm(1)
            norm_out(1)

            def rope_in_out(r):
                act.wait_ge(s["ropT_psum"], r + 1)
                n = rope_heads(r) // 2
                nc.scalar.activation(rope_dst(r), bank(4 + r % 2)[:, 0:n * SEQ]
                                     .rearrange("p (c q) -> p c q", q=SEQ), ACT.Copy) \
                  .then_inc(s["ropT_evac"], 1)

            for v in range(9):
                if v < 7:
                    gu_high(MIX_ITEM[0] + v + 2)
                    if v >= 2:
                        act.wait_ge(s["rop_ready"], v - 1)
                    act.wait_ge(s["proj_done"], v + 1)
                    w = rope_heads(v) * HD
                    src = bank(v % 4).rearrange("p (t n) -> p t n", t=TT)
                    if v == 2:
                        nc.scalar.activation(vA, src[:, :, P:2 * P], ACT.Copy)
                    nc.scalar.activation(raw[:, v % 2, 0:TT * w].rearrange("p (t n) -> p t n", t=TT),
                                         src[:, :, 0:w], ACT.Copy).then_inc(s["raw_ready"], 1)
                    if v < 3:
                        nh = TT * rope_heads(v)
                        act.wait_ge(s["qkvar_ready"], v + 1)
                        nc.scalar.activation(qk["std"][:, 0:nh], qk["var"][:, 0:nh], ACT.Sqrt) \
                          .then_inc(s["qkstd_ready"], 1)
                else:
                    evacuate(0, v, vB[:, :, (v - 7) * SEQ:(v - 6) * SEQ])
                if 0 <= v - 1 < 7:
                    rope_in_out(v - 1)
            attention(heads1)
            out_splits(0)
            post(1, lambda e, t: e.wait_ge(s["proj_done"], UNITS[1]))
            norm(2)
            for name, dst in (("tri", tri), ("masks", masks), ("gbd", gbd)):
                act.dma_start(dst, a[name]).then_inc(s["ab_loaded"], 16)
            norm_out(2)
            next_splits(1)
            ffn(1)
            post(2, lambda e, t: e.wait_ge(*((s["ffn_tt0"], 2) if t == 0 else (s["down_done"], 2 * FCH))))
            norm(3)
            norm_out(3)

            for v in range(2):
                evacuate(1, v, xr[:, 2 * v:2 * v + 2, 3:])
            act.wait_ge(s["s5_arg"], 1)
            nc.scalar.activation(chw[:, 0, :], chw[:, 0, :], ACT.Exp).then_inc(s["s5_trig"], 1)
            nc.scalar.activation(s5s["mag"], s5s["mag"], ACT.Exp).then_inc(s["s5_trig"], 1)
            nc.scalar.activation(chw[:, 2, :], chw[:, 1, :], ACT.Sin).then_inc(s["s5_trig"], 1)
            step.mark(nc.scalar.activation(chw[:, 3, :], chw[:, 1, :], ACT.Abs))
            step.done(act)
            nc.scalar.activation(chw[:, 3, :], chw[:, 3, :], ACT.Sin, bias=col(COL_HALFPI), scale=-1.0) \
              .then_inc(s["s5_trig"], 1)
            for v in range(2, 4):
                evacuate(1, v, qS[:, 2 * (v % 2):2 * (v % 2) + 2, :])
            act.wait_ge(s["gates_done"], 1)
            for w, dst, bias in ((0, rgate, COL_BA), (1, igate, COL_BX)):
                for c in range(4):
                    step.mark(nc.scalar.activation(dst[:, c, :], bank(4 + 2 * w, 2)[:, c * SEQ:(c + 1) * SEQ],
                                                   ACT.Sigmoid, bias=col(bias + c)))
            for v in range(4, 6):
                evacuate(1, v, kS[:, 2 * (v % 2):2 * (v % 2) + 2, :])
            step.done(act)
            act.wait_ge(s["lam_s"], 1)
            for c in range(4):
                step.mark(nc.scalar.activation(rga[:, c, :], rgate[:, c, :], ACT.Exp,
                                               scale=lam["neg8"][:, c:c + 1]))
            step.done(act)
            for c in range(4):
                nc.scalar.activation(rgate[:, c, :], rgate[:, c, :], ACT.Tanh,
                                     scale=lam["pos8"][:, c:c + 1]).then_inc(s["rg_act"], 1)
            act.wait_ge(s["rg_q"], 1)
            nc.scalar.activation(rgate[:, :, :], rgate[:, :, :], ACT.Sqrt).then_inc(s["rg_sqrt"], 1)
            for v in range(6, 8):
                evacuate(1, v, vS[:, :, (v % 2) * SEQ:(v % 2 + 1) * SEQ])
            act.wait_ge(s["angles"], 4)
            for jb in range(4):
                tS, tC = tabS[:, 4 * jb:4 * jb + 4, :], tabC[:, 4 * jb:4 * jb + 4, :]
                step.mark(nc.scalar.activation(tC, tS, ACT.Abs))
                step.done(act)
                nc.scalar.activation(tC, tC, ACT.Sin, bias=col(COL_HALFPI), scale=-1.0).then_inc(s["trig"], 1)
                nc.scalar.activation(tS, tS, ACT.Sin).then_inc(s["trig"], 1)
            for v in range(8, 10):
                evacuate(1, v, gg[:, 2 * (v % 2):2 * (v % 2) + 2, :], ACT.Gelu_apprx_tanh)
            for c in range(4):
                act.wait_ge(s["rg_y"], c + 1)
                nc.scalar.activation(hT[0][:, c, :], xc[:, c, :], ACT.Copy).then_inc(s["rg_high"], 1)
            act.wait_ge(s["rg_done"], 4)

            def stick_copy(b):
                act.wait_ge(s["z_psum"], b + 1)
                if b >= 2:
                    act.wait_ge(s["zm_ready"], b - 1)
                    act.wait_ge(s["sp_raw"], b - 1)
                nc.scalar.activation(zs[:, b % 2, :, :], bank(2 * (b % 2), 2)
                                     .rearrange("p (e q) -> p e q", e=2)[:, :, 0:384],
                                     ACT.Copy, scale=HD ** -0.5).then_inc(s["z_evac"], 1)

            def stick_log(b):
                act.wait_ge(s["z_abs"], b + 1)
                step.mark(nc.scalar.activation(lg[:, b % 2, :, :], lg[:, b % 2, :, :], ACT.Exp))
                step.done(act)
                nc.scalar.activation(lg[:, b % 2, :, :], lg[:, b % 2, :, :], ACT.Ln, bias=1.0) \
                  .then_inc(s["z_log"], 1)

            stick_copy(0)
            stick_log(0)
            stick_copy(1)
            for b in range(4):
                if b + 1 < 4:
                    stick_log(b + 1)
                act.wait_ge(s["t_ready"], b + 1)
                nc.scalar.activation(wz[:, b % 2, :, :], wz[:, b % 2, :, :], ACT.Exp).then_inc(s["w_ready"], 1)
                if b + 2 < 4:
                    stick_copy(b + 2)
                act.wait_ge(s["sbo_psum"], b + 1)
                nc.scalar.activation(hT[0][:, 4 + b, :], bank(6 + b % 2)[:, 0:SEQ], ACT.Copy) \
                  .then_inc(s["sbo_high"], 1)
            out_splits(1)
            norm(4)
            act.dma_start(cc[:, 0:2, :, :], a["cc"]).then_inc(s["cd_loaded"], 16)
            act.dma_start(glu, a["glu"]).then_inc(s["cd_loaded"], 16)
            norm_out(4)
            next_splits(2)
            ffn(2)
            norm(5)
            norm_out(5)

            for v in range(8):
                u = v % 2
                dst = ((uT, qM, kM)[v // 2][:, 2 * u:2 * u + 2, :] if v < 6
                       else vM[:, :, u * SEQ:(u + 1) * SEQ])
                evacuate(2, v, dst)
            act.wait_ge(s["s5_scan"], 2 * S5_TILES)
            act.dma_start(biasM, a["biasM"]).then_inc(s["biasM_loaded"], 16)
            for c in range(4):
                act.wait_ge(s["y_sum"], c + 1)
                nc.scalar.activation(yT[:, c, :], yT[:, c, :], ACT.Gelu_apprx_tanh).then_inc(s["y_gelu"], 1)
            for c in range(4):
                act.wait_ge(s["glu_psum"], c + 1)
                nc.scalar.activation(uT[:, c, :], bank(4 + c)[:, 0:SEQ], ACT.Sigmoid,
                                     bias=col(COL_GLUB + c)).then_inc(s["glu_sig"], 1)
            for c in range(4):
                act.wait_ge(s["s5_y"], c + 1)
                nc.scalar.activation(hT[0][:, c, :], yT[:, c, :], ACT.Copy).then_inc(s["s5_high"], 1)
            attention(heads2)
            out_splits(2)
            norm(6)
            norm_out(6)
            next_splits(3)
            ffn(3)
            norm(7)

        @block.vector
        def _(dve):
            step = Step(s["dve_step"])

            def wait_out(p, t):
                if p % 2 == 0:
                    f = p // 2
                    if t == 0:
                        dve.wait_ge(s["ffn_tt0"], f + 1)
                    else:
                        dve.wait_ge(s["down_done"], FCH * (f + 1))
                else:
                    dve.wait_ge(s["proj_done"], UNITS[p // 2 + 1])

            def gu_low(g):
                dve.wait_ge(s["gu_high"], g + 1)
                nc.vector.tensor_tensor(gu[1][:, g % 2, :], gu_raw[:, g % 2, :], gu[0][:, g % 2, :],
                                        ALU.subtract).then_inc(s["gu_split"], 1)

            def out_splits(m):
                for u in range(MIX_OUT - 1):
                    gu_low(MIX_ITEM[m] + MIX_IN[m] + u + 2)

            def next_splits(f):
                if f:
                    gu_low(FFN_ITEM[f] + 1)
                dve.wait_ge(s["dn_high"], FCH * f + 1)
                nc.vector.tensor_tensor(dn[1][:, 0, :], dn_raw[:, 0, :], dn[0][:, 0, :], ALU.subtract) \
                  .then_inc(s["dn_split"], 1)

            def low_of(c, src, name, value, done):
                dve.wait_ge(s[name], value)
                nc.vector.tensor_tensor(hT[1][:, c, :], src, hT[0][:, c, :], ALU.subtract) \
                  .then_inc(s[done], 1)

            def norm(n):
                dve.wait_ge(s["sq_done"], TT * (n + 1))
                nc.vector.tensor_scalar(st["var"], st["ss"], 1.0 / D, EPS, ALU.mult, ALU.add) \
                  .then_inc(s["var_ready"], 1)
                dve.wait_ge(s["std_ready"], n + 1)
                step.mark(nc.vector.reciprocal(st["rinv"], st["std"]))
                step.done(dve)
                if n < N_NORM:
                    for t in range(TT):
                        nc.vector.tensor_scalar(hn[:, t, :], x[:, t, :], st["rinv"][:, t:t + 1], None,
                                                ALU.mult).then_inc(s["hn_ready"], 1)
                    for c in range(KC):
                        dve.wait_ge(s["hT_high"], KC * n + c // 2 * 2 + 2)
                        nc.vector.scalar_tensor_tensor(
                            hT[1][:, c, :], bank(4 + c // 2)[:, c % 2 * SEQ:(c % 2 + 1) * SEQ],
                            col(COL_GAIN + n * KC + c), hT[0][:, c, :], ALU.mult, ALU.subtract) \
                          .then_inc(s["hT_low"], 1)
                else:
                    dve.wait_ge(s["gpost_final"], 16)
                    for t in range(TT):
                        nc.vector.scalar_tensor_tensor(hn[:, t, :], x[:, t, :], st["rinv"][:, t:t + 1],
                                                       gpost[:, 1, :], ALU.mult, ALU.mult) \
                          .then_inc(s["final_ready"], 1)

            def ffn(f):
                base, G0 = FFN_ITEM[f], FCH * f

                def step_of(i, r=None):
                    plain, arrived = during(i, r)
                    h, static = i % 2, r is None
                    dve.wait_ge(s["silu_ready"], plain(G0 + 1))
                    dve.wait_ge(s["up_ready"], plain(G0 + 1))
                    if not static or G0 + i >= 2:
                        dve.wait_ge(s["act_ready"], plain(G0 - 1))
                    nc.vector.tensor_tensor(prod_s[:, h, :], sil_s[:, h, :], bank(6 + h)[:, 0:SEQ],
                                            ALU.mult).then_inc(s["prod_done"], 1)
                    dve.wait_ge(s["prod_done"], plain(G0 + 1))
                    if not static or G0 + i >= 2:
                        dve.wait_ge(s["down_done"], plain(G0 - 1))
                    nc.vector.tensor_copy(act_s[0][:, h, :], prod_s[:, h, :]).then_inc(s["act_high"], 1)
                    dve.wait_ge(s["act_high"], plain(G0 + 1))
                    nc.vector.tensor_tensor(act_s[1][:, h, :], prod_s[:, h, :], act_s[0][:, h, :],
                                            ALU.subtract).then_inc(s["act_ready"], 1)
                    if not static or i < FCH - 1:
                        dve.wait_ge(s["dn_high"], plain(G0 + 2))
                        nc.vector.tensor_tensor(dn[1][:, 1 - h, :], dn_raw[:, 1 - h, :],
                                                dn[0][:, 1 - h, :], ALU.subtract) \
                          .then_inc(s["dn_split"], 1)
                    sl = (base + i) % 2
                    if not static or base + i + 2 < N_ITEMS:
                        dve.wait_ge(s["gu_high"], plain(base + 3))
                        nc.vector.tensor_tensor(gu[1][:, sl, :], gu_raw[:, sl, :], gu[0][:, sl, :],
                                                ALU.subtract).then_inc(s["gu_split"], 1)

                step_of(0)
                step_of(1)
                with dve.Fori(1, FCH // 2 - 1) as r:
                    for i in range(2):
                        step_of(i, r)
                step_of(FCH - 2)
                step_of(FCH - 1)

            def post_normed(p, factor):
                dve.wait_ge(s["psq_done"], TT * (p + 1))
                nc.vector.tensor_scalar(st["pvar"], st["pss"], 1.0 / D, EPS, ALU.mult, ALU.add) \
                  .then_inc(s["pvar_ready"], 1)
                dve.wait_ge(s["pstd_ready"], p + 1)
                step.mark(nc.vector.reciprocal(st["prinv"], st["pstd"]))
                step.done(dve)
                step.mark(nc.vector.tensor_scalar(st["prinv"], st["prinv"], factor, None, ALU.mult))
                step.done(dve)
                dve.wait_ge(*((s["gpost_loaded"], 32) if p < 2 else (s["gpost_ffn2"], 16)))
                for t in range(TT):
                    for half in range(2):
                        hs = slice(half * 512, (half + 1) * 512)
                        nc.vector.scalar_tensor_tensor(postw[:, t, hs], bank(2 * t + half),
                                                       st["prinv"][:, t:t + 1], gpost[:, p % 2, hs],
                                                       ALU.mult, ALU.mult).then_inc(s["post_t"], 1)

            def post_plain(p):
                for t in range(TT):
                    wait_out(p, t)
                    for half in range(2):
                        hs = slice(half * 512, (half + 1) * 512)
                        nc.vector.tensor_tensor(x[:, t, hs], x[:, t, hs], bank(2 * t + half), ALU.add) \
                          .then_inc(s["x_ready"], 1)

            def attention(heads):
                first, last = heads[0]["a"], heads[-1]["a"]
                for e in range(first, last + 4):
                    if e == first and heads[0]["bias"] is not None:
                        dve.wait_ge(s["biasM_loaded"], 16)
                    if e <= last:
                        h = heads[e - first]
                        n_ = h["a"]
                        scores = bank(e % 3)
                        dve.wait_ge(s["s_ready"], e + 1)
                        if h["bias"] is None:
                            step.mark(nc.vector.tensor_reduce(
                                stat[:, n_, 0:2], scores.rearrange("p (t k) -> p t k", t=TT), AX.X, ALU.max))
                            step.done(dve)
                            nc.vector.tensor_scalar(stat[:, n_, 0:2], stat[:, n_, 0:2], -h["scale"], None,
                                                    ALU.mult).then_inc(s["max_ready"], 1)
                        else:
                            if e >= first + 2 and heads[e - first - 2]["bias"] is not None:
                                dve.wait_ge(s["p_ready"], e - 1)
                            for t in range(TT):
                                step.mark(nc.vector.tensor_tensor_reduce(
                                    out=h["exp_in"][:, t * SEQ:(t + 1) * SEQ],
                                    in0=scores[:, t * SEQ:(t + 1) * SEQ], in1=h["bias"][:, t, :],
                                    scale=h["scale"], scalar=-3e38, op0=ALU.add, op1=ALU.max,
                                    accum_out=stat[:, n_, t:t + 1]))
                            step.done(dve)
                            nc.vector.tensor_scalar(stat[:, n_, 0:2], stat[:, n_, 0:2], -1.0, None,
                                                    ALU.mult).then_inc(s["max_ready"], 1)
                    g = e - 1
                    if first <= g <= last:
                        h = heads[g - first]
                        dve.wait_ge(s["p_ready"], g + 1)
                        step.mark(nc.vector.reciprocal(stat[:, h["a"], 2:4], stat[:, h["a"], 2:4]))
                        step.done(dve)
                        for t in range(TT):
                            pr = h["probs"][:, t * SEQ:(t + 1) * SEQ]
                            i = nc.vector.tensor_scalar(pr, pr, stat[:, h["a"], 2 + t:3 + t], None, ALU.mult)
                        i.then_inc(s["pn_ready"], 1)
                    g = e - 3
                    if first <= g <= last and heads[g - first]["heads_out"] is not None:
                        src, c = heads[g - first]["heads_out"]
                        done = c + 1 if first == 0 else 8 + c - 3
                        low_of(c, src, "o_high", done, "o_ready")

            norm(0)
            gu_low(0)
            gu_low(1)
            next_splits(0)
            dve.wait_ge(s["lam_e"], 1)
            step.mark(nc.vector.tensor_scalar(lam["den"], lam["e"], 2.0, None, ALU.add))
            step.done(dve)
            step.mark(nc.vector.reciprocal(lam["den"], lam["den"]))
            step.done(dve)
            step.mark(nc.vector.tensor_tensor(lam["s"], lam["e"], lam["den"], ALU.mult))
            step.done(dve)
            step.mark(nc.vector.tensor_tensor(lam["s2"], lam["s"], lam["s"], ALU.mult))
            step.mark(nc.vector.memset(lam["acc"], 1.0 / 17))
            for k in range(7, -1, -1):
                step.done(dve)
                step.mark(nc.vector.tensor_tensor(lam["acc"], lam["acc"], lam["s2"], ALU.mult))
                step.done(dve)
                step.mark(nc.vector.tensor_scalar(lam["acc"], lam["acc"], 1.0 / (2 * k + 1), None, ALU.add))
            step.mark(nc.vector.tensor_scalar(lam["pos"], col(COL_LAM, 4), -1.0, 0.0, ALU.mult, ALU.max))
            step.done(dve)
            step.mark(nc.vector.tensor_tensor(lam["acc"], lam["acc"], lam["s"], ALU.mult))
            step.done(dve)
            step.mark(nc.vector.scalar_tensor_tensor(lam["acc"], lam["acc"], 2.0, lam["pos"],
                                                     ALU.mult, ALU.add))
            step.done(dve)
            step.mark(nc.vector.tensor_scalar(lam["neg8"], lam["acc"], -8.0, None, ALU.mult))
            nc.vector.tensor_scalar(lam["pos8"], lam["acc"], 8.0, None, ALU.mult).then_inc(s["lam_s"], 1)
            ffn(0)
            post_normed(0, 0.5)
            norm(1)
            dve.wait_ge(s["late_loaded"], 64)
            for tab, g in ((rope_q, 0), (rope_k, 2)):
                for part in range(2):
                    nh = tab.shape[3]
                    for t in range(TT):
                        i = nc.vector.tensor_tensor(
                            tab[:, part, t, :, :],
                            axial[:, part, t, :].unsqueeze(1).broadcast_to([P, nh, HD]),
                            qkg[:, g + part, :].unsqueeze(1).broadcast_to([P, nh, HD]), ALU.mult)
            i.then_inc(s["tables_ready"], 1)
            dve.wait_ge(s["tables_ready"], 1)
            dve.wait_ge(s["s5_arg"], 1)
            nc.vector.reciprocal(s5c[:, 2, :], chw[:, 4, :]).then_inc(s["s5_rden"], 1)

            def flat(tab):
                return tab.rearrange("p t h d -> p (t h d)")

            for r in range(7):
                gu_low(MIX_ITEM[0] + r + 2)
                nh = TT * rope_heads(r)
                w = nh * HD
                src = raw[:, r % 2, 0:w]
                dve.wait_ge(s["raw_ready"], r + 1)
                if r >= 1:
                    dve.wait_ge(s["rop_ready"], r)
                if r < 3:
                    step.mark(nc.vector.tensor_tensor(t1[:, 0:w], src, src, ALU.mult))
                    step.done(dve)
                    step.mark(nc.vector.tensor_reduce(qk["ss"][:, 0:nh],
                                                      t1[:, 0:w].rearrange("p (h d) -> p h d", d=HD),
                                                      AX.X, ALU.add))
                    step.done(dve)
                    nc.vector.tensor_scalar(qk["var"][:, 0:nh], qk["ss"][:, 0:nh], 1.0 / HD, EPS,
                                            ALU.mult, ALU.add).then_inc(s["qkvar_ready"], 1)
                    dve.wait_ge(s["qkstd_ready"], r + 1)
                    step.mark(nc.vector.reciprocal(qk["rinv"][:, 0:nh], qk["std"][:, 0:nh]))
                    step.done(dve)
                    nc.vector.tensor_tensor(xn1[:, 0:w].rearrange("p (h d) -> p h d", d=HD),
                                            src.rearrange("p (h d) -> p h d", d=HD),
                                            qk["rinv"][:, 0:nh].unsqueeze(2).broadcast_to([P, nh, HD]),
                                            ALU.mult).then_inc(s["xn_ready"], 1)
                    dve.wait_ge(s["xn_ready"], r + 1)
                    src = xn1[:, 0:w]
                cos = flat((rope_q if r < 2 else rope_k if r == 2 else rope_b)[:, 0])
                step.mark(nc.vector.tensor_tensor(t1[:, 0:w], src, cos, ALU.mult))
                step.done(dve)
                dve.wait_ge(s["t2_ready"], 2 * (r + 1))
                if r >= 2:
                    dve.wait_ge(s["ropT_psum"], r - 1)
                nc.vector.tensor_tensor(rop[:, r % 2, 0:w], t1[:, 0:w], t2[:, 0:w], ALU.add) \
                  .then_inc(s["rop_ready"], 1)
            for v in (7, 8):
                gu_low(MIX_ITEM[0] + v + 2)
            attention(heads1)
            out_splits(0)
            post_normed(1, 1.0)
            norm(2)
            next_splits(1)
            ffn(1)
            post_normed(2, 0.5)
            norm(3)

            for v in range(2):
                gu_low(MIX_ITEM[1] + v + 2)
            wait_unit(dve, 1, 1)
            dve.wait_ge(s["zeroed"], 1)
            for c in range(4):
                step.mark(nc.vector.tensor_scalar(xc[:, c, :], xr[:, c, 0:SEQ], col(COL_CONV + c),
                                                  col(COL_CONVB + c), ALU.mult, ALU.add))
            for tap in range(1, 4):
                step.done(dve)
                for c in range(4):
                    i = nc.vector.scalar_tensor_tensor(xc[:, c, :], xr[:, c, tap:tap + SEQ],
                                                       col(COL_CONV + 4 * tap + c), xc[:, c, :],
                                                       ALU.mult, ALU.add)
                    if tap < 3:
                        step.mark(i)
                    else:
                        i.then_inc(s["conv_done"], 1)
            for v in range(2, 6):
                gu_low(MIX_ITEM[1] + v + 2)
            dve.wait_ge(s["rg_act"], 4)
            asq = xr[:, :, 0:SEQ]
            step.mark(nc.vector.tensor_tensor(asq, rga[:, :, :], rga[:, :, :], ALU.mult))
            step.done(dve)
            step.mark(nc.vector.scalar_tensor_tensor(rgate[:, :, :], asq, 1.0, rgate[:, :, :],
                                                     ALU.add, ALU.mult))
            step.done(dve)
            nc.vector.tensor_scalar(rgate[:, :, :], rgate[:, :, :], 1e-34, None, ALU.max) \
              .then_inc(s["rg_q"], 1)
            for v in range(6, 8):
                gu_low(MIX_ITEM[1] + v + 2)
            dve.wait_ge(s["rg_sqrt"], 1)
            dve.wait_ge(s["rg_ix"], 1)
            step.mark(nc.vector.tensor_tensor(rgate[:, :, :], rgate[:, :, :], igate[:, :, :], ALU.mult))
            step.done(dve)
            for c in range(4):
                step.mark(nc.vector.tensor_tensor_scan(xc[:, c, :], rga[:, c, :], rgate[:, c, :], 0.0,
                                                       ALU.mult, ALU.add))
            step.done(dve)
            for v in range(8, 10):
                gu_low(MIX_ITEM[1] + v + 2)
            wait_unit(dve, 1, 9)
            for c in range(4):
                nc.vector.tensor_tensor(xc[:, c, :], xc[:, c, :], gg[:, c, :], ALU.mult) \
                  .then_inc(s["rg_y"], 1)
            for c in range(4):
                low_of(c, xc[:, c, :], "rg_high", c + 1, "rg_done")
            dve.wait_ge(s["rg_done"], 4)

            def stick_abs(b):
                dve.wait_ge(s["z_evac"], b + 1)
                if b >= 2:
                    dve.wait_ge(s["sp_raw"], b - 1)
                nc.vector.scalar_tensor_tensor(lg[:, b % 2, :, :], zs[:, b % 2, :, :], -1.0,
                                               zs[:, b % 2, :, :], ALU.mult, ALU.min) \
                  .then_inc(s["z_abs"], 1)

            stick_abs(0)
            for b in range(4):
                if b + 1 < 4:
                    stick_abs(b + 1)
                dve.wait_ge(s["z_log"], b + 1)
                if b >= 2:
                    dve.wait_ge(s["r_psum"], b - 1)
                nc.vector.scalar_tensor_tensor(sp[:, b % 2, :, :], zs[:, b % 2, :, :], 0.0,
                                               lg[:, b % 2, :, :], ALU.max, ALU.add) \
                  .then_inc(s["sp_raw"], 1)
                dve.wait_ge(s["r_psum"], b + 1)
                dve.wait_ge(s["zm_ready"], b + 1)
                R = bank(4, 2).rearrange("p (e q) -> p e q", e=2)[:, :, 0:384]
                nc.vector.tensor_tensor(wz[:, b % 2, :, :], wz[:, b % 2, :, :], R, ALU.subtract) \
                  .then_inc(s["t_ready"], 1)
                if b:
                    low_of(3 + b, bank(6 + (b - 1) % 2)[:, 0:SEQ], "sbo_high", b, "sbo_done")
            low_of(7, bank(7)[:, 0:SEQ], "sbo_high", 4, "sbo_done")
            out_splits(1)
            post_plain(3)
            norm(4)
            next_splits(2)
            ffn(2)
            post_plain(4)
            norm(5)

            dve.wait_ge(s["trig"], 8)

            def both(tab, j):
                return tab[:, j, :].unsqueeze(1).broadcast_to([P, 2, SEQ])

            def s5_modulate(j):
                dve.wait_ge(s["bu_done"], j + 1)
                if j >= 2:
                    dve.wait_ge(s["s5_scan"], 2 * (j - 1))
                bu = bank(4 + j % 2).rearrange("p (h s) -> p h s", h=2)
                nc.vector.tensor_tensor(pc[:, j % 2, :, :], bu, both(tabC, j), ALU.mult) \
                  .then_inc(s["s5_mod"], 1)
                nc.vector.tensor_tensor(pw[:, j % 2, :, :], bu, both(tabS, j), ALU.mult) \
                  .then_inc(s["s5_mod"], 1)

            for v in range(2):
                gu_low(MIX_ITEM[2] + v + 2)
            s5_modulate(0)
            for j in range(S5_TILES):
                if j + 1 < S5_TILES:
                    s5_modulate(j + 1)
                if j % 2 == 0 and j < 12:
                    gu_low(MIX_ITEM[2] + 2 + j // 2 + 2)
                dve.wait_ge(s["zin_ready"], 2 * (j + 1))
                if j >= 2:
                    dve.wait_ge(s["s5_dem"], 2 * (j - 1))
                for h in range(2):
                    nc.vector.tensor_tensor_scan(zz[:, j % 2, h, :],
                                                 s5s["mag"][:, j:j + 1].broadcast_to([P, SEQ]),
                                                 pc[:, j % 2, h, :], 0.0, ALU.mult, ALU.add) \
                      .then_inc(s["s5_scan"], 1)
            dve.wait_ge(s["y_done"], S5_TILES)
            for c in range(4):
                nc.vector.scalar_tensor_tensor(yT[:, c, :], uT[:, c, :], col(COL_DSKIP + c),
                                               bank(6, 2)[:, c * SEQ:(c + 1) * SEQ], ALU.mult, ALU.add) \
                  .then_inc(s["y_sum"], 1)
            dve.wait_ge(s["glu_psum"], 4)
            for c in range(4):
                dve.wait_ge(s["glu_sig"], c + 1)
                nc.vector.tensor_tensor(yT[:, c, :], yT[:, c, :], uT[:, c, :], ALU.mult) \
                  .then_inc(s["s5_y"], 1)
            for c in range(4):
                low_of(c, yT[:, c, :], "s5_high", c + 1, "s5_done")
            attention(heads2)
            out_splits(2)
            post_plain(5)
            norm(6)
            next_splits(3)
            ffn(3)
            post_plain(6)
            norm(7)

        @block.gpsimd
        def _(pool):
            step = Step(s["pool_step"])

            def tt(out, in0, in1, op):
                step.mark(nc.gpsimd.tensor_tensor(out, in0, in1, op))
                step.done(pool)

            def ts(out, in0, s1, s2, op0, op1):
                step.mark(nc.gpsimd.tensor_scalar(out, in0, s1, s2, op0, op1))
                step.done(pool)

            def reduce_angle(ang, k, t, parts):
                ts(k, ang, 1.0 / TWO_PI, MAGIC, ALU.mult, ALU.add)
                for part in parts:
                    ts(t, k, MAGIC, -part, ALU.subtract, ALU.mult)
                    tt(ang, ang, t, ALU.add)

            def add_residual(p):
                for t in range(TT):
                    for half in range(2):
                        hs = slice(half * 512, (half + 1) * 512)
                        pool.wait_ge(s["post_t"], 4 * p + 2 * t + half + 1)
                        nc.gpsimd.tensor_tensor(x[:, t, hs], x[:, t, hs], postw[:, t, hs], ALU.add) \
                          .then_inc(s["x_ready"], 1)

            pool.wait_ge(s["exp_dt"], 2)
            pool.wait_ge(s["early_loaded"], 32)
            pool.wait_ge(s["s5c_loaded"], 16)
            A = [chw[:, k, :] for k in range(8)]
            lr, li, dt, br, bi = (s5c[:, k, :] for k in range(5))
            tt(A[0], lr, dt, ALU.mult)
            tt(A[1], li, dt, ALU.mult)
            reduce_angle(A[1], A[4], A[5], (C1, C2, C3))
            ts(A[1], A[1], 3.1415925, -3.1415925, ALU.min, ALU.max)
            tt(s5s["mag"], col(COL_LR, S5_TILES), s5s["dt"], ALU.mult)
            tt(s5s["th"], col(COL_LI, S5_TILES), s5s["dt"], ALU.mult)
            reduce_angle(s5s["th"], s5s["k"], s5s["t"], (C1, C2, C3))
            tt(A[4], lr, lr, ALU.mult)
            tt(A[5], li, li, ALU.mult)
            nc.gpsimd.tensor_tensor(A[4], A[4], A[5], ALU.add).then_inc(s["s5_arg"], 1)
            add_residual(0)
            pool.wait_ge(s["x_ready"], 4)
            pool.dma_start(gpost[:, 0, :], a["ffn2_post_g"].partition_broadcast(P)) \
                .then_inc(s["gpost_ffn2"], 16)

            pool.wait_ge(s["tables_ready"], 1)
            for r in range(7):
                w = TT * rope_heads(r) * HD
                if r < 3:
                    pool.wait_ge(s["xn_ready"], r + 1)
                    src, tab, cut_ = xn1[:, 0:w], rope_q if r < 2 else rope_k, "p (h b j) -> p b h j"
                    J = HD // 4
                else:
                    pool.wait_ge(s["raw_ready"], r + 1)
                    src, tab, cut_ = raw[:, r % 2, 0:w], rope_b, "p (h b j) -> p b h j"
                    J = HD // 2
                if r >= 1:
                    pool.wait_ge(s["rop_ready"], r)
                sin = tab[:, 1].rearrange("p t h d -> p (t h d)")
                for b in range(2):
                    nc.gpsimd.tensor_tensor(t2[:, 0:w].rearrange(cut_, b=2, j=J)[:, b],
                                            src.rearrange(cut_, b=2, j=J)[:, 1 - b],
                                            sin.rearrange(cut_, b=2, j=J)[:, b], ALU.mult) \
                      .then_inc(s["t2_ready"], 1)
            add_residual(1)
            pool.wait_ge(s["x_ready"], 8)
            pool.dma_start(gpost[:, 1, :], a["final_norm"].partition_broadcast(P)) \
                .then_inc(s["gpost_final"], 16)

            pool.wait_ge(s["s5_rden"], 1)
            for jb in range(4):
                g = slice(4 * jb, 4 * jb + 4)
                for j in range(4 * jb, 4 * jb + 4):
                    step.mark(nc.gpsimd.tensor_scalar(tabS[:, j, :], trow[:, :], s5s["th"][:, j:j + 1],
                                                      None, ALU.mult))
                step.done(pool)
                ang, k, t = tabS[:, g, :], tabC[:, g, :], chw[:, 4:8, :]
                reduce_angle(ang, k, t, (C1, C2))
                nc.gpsimd.tensor_scalar(ang, ang, 3.1415925, -3.1415925, ALU.min, ALU.max) \
                  .then_inc(s["angles"], 1)
            add_residual(2)
            pool.wait_ge(s["x_ready"], 12)
            nc.gpsimd.memset(xr[:, :, 0:3], 0.0).then_inc(s["zeroed"], 1)

            pool.wait_ge(s["s5_trig"], 4)
            pool.wait_ge(s["s5_rden"], 1)
            mag, sn, cs = A[0], A[2], A[3]
            tt(cs, mag, cs, ALU.mult)
            ts(cs, cs, 1.0, None, ALU.subtract, ALU.bypass)
            tt(sn, mag, sn, ALU.mult)
            tt(A[4], cs, lr, ALU.mult)
            tt(A[5], sn, li, ALU.mult)
            tt(A[4], A[4], A[5], ALU.add)
            tt(A[5], sn, lr, ALU.mult)
            tt(A[6], cs, li, ALU.mult)
            tt(A[5], A[5], A[6], ALU.subtract)
            tt(A[4], A[4], dt, ALU.mult)
            tt(A[5], A[5], dt, ALU.mult)
            tt(A[0], A[4], br, ALU.mult)
            tt(A[1], A[5], bi, ALU.mult)
            tt(A[0], A[0], A[1], ALU.subtract)
            tt(A[1], A[4], bi, ALU.mult)
            tt(A[2], A[5], br, ALU.mult)
            tt(A[1], A[1], A[2], ALU.add)
            for part in range(2):
                for g in range(2):
                    nc.gpsimd.tensor_scalar(bb[:, part, :, g, :],
                                            A[part].rearrange("p (c n) -> p c n", n=HD),
                                            col(COL_SEL + g), None, ALU.mult).then_inc(s["bb_ready"], 1)
            pool.wait_ge(s["rg_act"], 4)
            nc.gpsimd.tensor_tensor(igate[:, :, :], igate[:, :, :], xc[:, :, :], ALU.mult) \
              .then_inc(s["rg_ix"], 1)
            pool.wait_ge(s["rg_done"], 4)

            def stick_exponent(b):
                pool.wait_ge(s["z_evac"], b + 1)
                if b >= 2:
                    pool.wait_ge(s["sbo_psum"], b - 1)
                for e in range(2):
                    i = nc.gpsimd.tensor_tensor(wz[:, b % 2, e, :], zs[:, b % 2, e, :], masks[:, 1, :],
                                                ALU.add)
                i.then_inc(s["zm_ready"], 1)

            for b in range(4):
                stick_exponent(b)
                pool.wait_ge(s["sp_raw"], b + 1)
                for e in range(2):
                    i = nc.gpsimd.tensor_tensor(sp[:, b % 2, e, :], sp[:, b % 2, e, :], masks[:, 0, :],
                                                ALU.mult)
                i.then_inc(s["sp_ready"], 1)

            pool.wait_ge(s["cd_loaded"], 32)
            tt_ = nc.gpsimd.tensor_scalar
            tt_(cc[:, 2, :, :], cc[:, 0, :, :], -1.0, None, ALU.mult)
            tt_(cc[:, 1, :, :], cc[:, 1, :, :], -1.0, None, ALU.mult).then_inc(s["cc_ready"], 1)

            def s5_sum(j):
                pool.wait_ge(s["s5_mod"], 2 * (j + 1))
                r = j % 2
                nc.gpsimd.tensor_tensor(pc[:, r, 0, :], pc[:, r, 0, :], pw[:, r, 1, :], ALU.add) \
                  .then_inc(s["zin_ready"], 1)
                nc.gpsimd.tensor_tensor(pc[:, r, 1, :], pc[:, r, 1, :], pw[:, r, 0, :], ALU.subtract) \
                  .then_inc(s["zin_ready"], 1)

            s5_sum(0)
            for j in range(S5_TILES):
                if j + 1 < S5_TILES:
                    s5_sum(j + 1)
                pool.wait_ge(s["s5_scan"], 2 * (j + 1))
                if j >= 2:
                    pool.wait_ge(s["y_done"], j - 1)
                for dst, tab in ((dC, tabC), (dS, tabS)):
                    nc.gpsimd.tensor_tensor(dst[:, j % 2, :, :], zz[:, j % 2, :, :],
                                            tab[:, j, :].unsqueeze(1).broadcast_to([P, 2, SEQ]),
                                            ALU.mult).then_inc(s["s5_dem"], 1)


def kernel(**inputs):
    import concourse.bacc as bacc
    from concourse.bass_utils import run_bass_kernel_spmd

    w = {k: np.asarray(v) for k, v in inputs.items()}
    f32 = np.float32

    def by_rows(m):
        return m.reshape(-1, P, m.shape[1]).transpose(1, 0, 2)

    def ffn_gu(gate, up):
        return np.stack([by_rows(m).reshape(P, KC, FCH, P) for m in (gate, up)], axis=1) \
                 .transpose(3, 0, 1, 2, 4).reshape(FCH, P, GU)

    def mix_gu(blocks):
        wide = np.concatenate(blocks, axis=1)
        return by_rows(wide).reshape(P, KC, -1, SEQ).transpose(2, 0, 1, 3).reshape(-1, P, GU)

    pairs = [c + 4 * e for c in range(4) for e in range(2)]
    qkv, wo = w["w_qkv"][0], w["w_out"][0]
    qa = qkv[:, :512].reshape(D, 8, HD)[:, pairs].reshape(D, 512)
    wo = np.concatenate([wo[:512].reshape(8, HD, D)[pairs].reshape(512, D), wo[512:]])
    ab, cd = w["ab_w_in_2"][0], w["cd_w_in_2"][0]
    wgu = np.concatenate([
        ffn_gu(w["ffn1_w_gate"][0], w["ffn1_w_up"][0]),
        mix_gu([qa, qkv[:, 512:], wo]),
        ffn_gu(w["ffn2_w_gate"][0], w["ffn2_w_up"][0]),
        mix_gu([ab[:, :512], ab[:, 1024:], ab[:, 512:1024], w["ab_w_out_2"][0]]),
        ffn_gu(w["ffn_w_gate_2"][0], w["ffn_w_up_2"][0]),
        mix_gu([cd, w["cd_w_out_2"][0]]),
        ffn_gu(w["ffn_w_gate_2"][1], w["ffn_w_up_2"][1])])
    wdn = np.concatenate([w[n][i] for n, i in (("ffn1_w_down", 0), ("ffn2_w_down", 0),
                                               ("ffn_w_down_2", 0), ("ffn_w_down_2", 1))])
    wdn = wdn.reshape(4 * FCH, P, D)

    def column(v):
        return v.reshape(-1, P).T

    G, N, PG = 32, 64, 16
    lr, li, ldt = w["cd_lam_re_2"][0], w["cd_lam_im_2"][0], w["cd_log_dt_2"][0]
    ldt_n = np.broadcast_to(ldt[:, None], (G, N))
    in_quadrant = (np.arange(P) % 32) // PG
    cols = np.concatenate(
        [column(g) for g in (w["ffn1_pre_g"], w["mix_pre_g"], w["ffn2_pre_g"], w["ab_norm_2"],
                             w["ffn_norm_2"][0], w["cd_norm_2"], w["ffn_norm_2"][1])]
        + [column(w["ab_conv_w_2"]), column(w["ab_conv_b_2"]), column(w["ab_gate_a_b_2"]),
           column(w["ab_gate_x_b_2"]), column(w["ab_lambda_2"]), column(w["cd_d_2"]),
           column(w["cd_glu_b_2"]), column(lr), column(li), column(ldt_n),
           np.stack([in_quadrant == 0, in_quadrant == 1], 1).astype(f32),
           np.full((P, 1), math.pi / 2, f32)], axis=1)

    def by_channel(v):
        return np.repeat(v.reshape(4, 8, N).transpose(1, 0, 2), PG, axis=0).reshape(P, 4 * N)

    def b_by_channel(b):
        return b.reshape(4, 8, N, PG).transpose(1, 3, 0, 2).reshape(P, 4 * N)

    s5c = np.stack([by_channel(lr), by_channel(li), by_channel(ldt_n),
                    b_by_channel(w["cd_b_re_2"][0]), b_by_channel(w["cd_b_im_2"][0])], axis=1)
    cc = np.zeros((2, N, 2, S5_TILES, 2, PG), f32)
    for part, name in enumerate(("cd_c_re_2", "cd_c_im_2")):
        c = w[name][0].reshape(S5_TILES, 2, PG, N)
        for g in range(2):
            cc[g, :, part, :, g, :] = c[:, g].transpose(2, 0, 1)
    cc = cc.reshape(P, 2, S5_TILES, 32)
    gates = np.stack([w["ab_gate_a_w_2"][0], w["ab_gate_x_w_2"][0]])
    gates = gates.reshape(2, 4, 2, HD, HD)
    gbd = np.zeros((2, HD, 2, 4, 2, HD), f32)
    for e in range(2):
        gbd[e, :, :, :, e, :] = gates[:, :, e].transpose(2, 0, 1, 3)
    gbd = gbd.reshape(P, 2, 4, P)
    glu = w["cd_glu_w_2"][0].reshape(4, P, 512).transpose(1, 0, 2)
    qg, kg = w["q_norm_g"][0], w["k_norm_g"][0]
    swap = np.arange(HD).reshape(2, 2, 16)[:, ::-1].reshape(HD)
    qkg = np.broadcast_to(np.stack([qg, qg[swap], kg, kg[swap]]), (P, 4, HD))

    t = np.arange(SEQ)

    def angles(pos, dim):
        freqs = (ROPE_THETA ** (-np.arange(0, dim, 2, dtype=f32) / f32(dim))).astype(f32)
        return pos.astype(f32)[:, None] * freqs[None, :]

    def rope_tables(parts):
        cos = np.concatenate([np.cos(x) for x in parts for _ in range(2)], axis=1)
        sin = np.concatenate([sg * np.sin(x) for x in parts for sg in (-1, 1)], axis=1)
        return [m.reshape(TT, P, HD).transpose(1, 0, 2).astype(f32) for m in (cos, sin)]

    axial = np.stack(rope_tables([angles(t // GRID_W, HD // 2), angles(t % GRID_W, HD // 2)]), axis=1)
    rope_b = np.stack(rope_tables([angles(t, HD)]), axis=1)
    rope_b = np.repeat(rope_b[:, :, :, None, :], 4, axis=3)
    s5in = np.concatenate([s5c.reshape(P, 5 * SEQ), np.broadcast_to(t.astype(f32), (P, SEQ))], axis=1)
    diff = t[None, :] - t[:, None]
    count = (np.abs(diff) <= 64).astype(f32)
    for dilation in (4, 16):
        span = {4: 512, 16: 2048}[dilation] // 2
        count += (diff % dilation == 0) & (np.abs(diff) <= span)
    biasB = np.where(count > 0, np.log(np.maximum(count, 1)) * HD ** 0.5, NEG).astype(f32)
    biasB = biasB.reshape(TT, P, SEQ).transpose(1, 0, 2)
    slopes = 2.0 ** (-8.0 * np.arange(1, 5) / 4)
    biasM = np.where(diff <= 0, slopes[:, None, None] * diff * P ** 0.5, NEG).astype(f32)
    biasM = biasM.reshape(4, TT, P, SEQ).transpose(2, 0, 1, 3)
    k = np.arange(P)
    tri = np.stack([k[:, None] >= k[None, :], np.ones((P, P), bool)], axis=1).astype(f32)
    past = k[:, None] < np.concatenate([t, t[:P]])[None, :]
    masks = np.stack([past, np.where(past, 0, NEG)], axis=1).astype(f32)

    data = {
        "x": w["x"][0].reshape(TT, P, D).transpose(1, 0, 2), "wgu": wgu, "wdn": wdn,
        "ident": np.eye(P, dtype=f32), "cols": cols, "ffn1_post_g": w["ffn1_post_g"][0],
        "mix_post_g": w["mix_post_g"][0], "ffn2_post_g": w["ffn2_post_g"][0],
        "final_norm": w["final_norm_2"], "s5in": s5in, "biasB": biasB, "axial": axial,
        "rope_b": rope_b, "tri": tri, "masks": masks,
        "biasM": biasM, "glu": glu, "qkg": qkg, "cc": cc, "gbd": gbd,
    }
    nc = bacc.Bacc("TRN2", target_bir_lowering=False, num_devices=1)
    arrays, args = {}, {}
    for name, v in data.items():
        arrays["in_" + name] = np.ascontiguousarray(v)
        args[name] = nc.dram_tensor("in_" + name, v.shape, F32, kind="ExternalInput").ap()
    args["out"] = nc.dram_tensor("out_x", (P, TT, D), F32, kind="ExternalOutput").ap()
    build(nc, args)
    got = run_bass_kernel_spmd(nc, [arrays], core_ids=[0]).results[0]["out_x"]
    return np.asarray(got).reshape(P, TT, D).transpose(1, 0, 2).reshape(1, SEQ, D)
```

```python
from contextlib import ExitStack
import math

import numpy as np
import concourse.bass as bass
from concourse import mybir

F32 = mybir.dt.float32
F32R = mybir.dt.float32r
ACT = mybir.ActivationFunctionType
ALU = mybir.AluOpType
AX = mybir.AxisListType

P = 128
SEQ = 256
TT = SEQ // P
D = 1024
KC = D // P
FF = 2816
FCH = FF // P
HD = 64
EPS = 1e-6
NEG = -1e30
GU = 2 * KC * P
N_NORM = 7
S5_TILES = 16
TWO_PI = 2 * math.pi
C1 = 6.28125
C2 = 0.0019350051879882812
C3 = TWO_PI - C1 - C2
MAGIC = 1.5 * 2.0 ** 23
ROPE_THETA = 10000.0
GRID_W = 64

COL_GAIN = 0
COL_CONV = COL_GAIN + N_NORM * KC
COL_CONVB = COL_CONV + 16
COL_BA = COL_CONVB + 4
COL_BX = COL_BA + 4
COL_LAM = COL_BX + 4
COL_DSKIP = COL_LAM + 4
COL_GLUB = COL_DSKIP + 4
COL_LR = COL_GLUB + 4
COL_LI = COL_LR + S5_TILES
COL_LDT = COL_LI + S5_TILES
COL_SEL = COL_LDT + S5_TILES
COL_HALFPI = COL_SEL + 2
COL_EPS = COL_HALFPI + 1
N_COLS = COL_EPS + 2

MIX_IN = (9, 10, 8)
MIX_OUT = 4
STICK_BANK = (4, 6, 0, 2)
STICK_OUT = (4, 6, 5, 7)
STREAM = [("ffn", 0), ("mix", 0), ("ffn", 1), ("mix", 1), ("ffn", 2), ("mix", 2), ("ffn", 3)]


def part_base(kind, n):
    at = 0
    for k, m in STREAM:
        if (k, m) == (kind, n):
            return at
        at += FCH if k == "ffn" else MIX_IN[m] + MIX_OUT
    return at


FFN_ITEM = [part_base("ffn", n) for n in range(4)]
MIX_ITEM = [part_base("mix", n) for n in range(3)]
N_ITEMS = FFN_ITEM[3] + FCH
UNITS = [sum(MIX_IN[:m]) + MIX_OUT * m for m in range(4)]


class Step:

    def __init__(self, sem):
        self.sem, self.count = sem, 0

    def mark(self, instruction):
        self.count += 1
        instruction.then_inc(self.sem, 1)

    def done(self, engine):
        engine.wait_ge(self.sem, self.count)


def build(nc, a):
    with ExitStack() as ctx:
        def sb(name, shape, dtype=F32):
            return ctx.enter_context(nc.sbuf_tensor(name, shape, dtype))

        def sem(name):
            return ctx.enter_context(nc.semaphore(name))

        x = sb("x", [P, TT, D])
        hT = [sb("hT_" + part, [P, KC, SEQ], F32R) for part in ("high", "low")]
        gu_raw = sb("gu_raw", [P, 2, GU])
        dn_raw = sb("dn_raw", [P, 2, D])
        gu = [sb("gu_" + part, [P, 2, GU], F32R) for part in ("high", "low")]
        dn = [sb("dn_" + part, [P, 2, D], F32R) for part in ("high", "low")]
        act_s = [sb("act_" + part, [P, 2, SEQ], F32R) for part in ("high", "low")]
        ffn_s = sb("ffn_s", [P, 4, SEQ])
        sil_s, prod_s = ffn_s[:, 0:2, :], ffn_s[:, 2:4, :]
        gpost = sb("gpost", [P, 2, D])
        ident = sb("ident", [P, P])
        cols = sb("cols", [P, N_COLS])
        s5in = sb("s5in", [P, 6 * SEQ])
        s5c = s5in[:, 0:5 * SEQ].rearrange("p (k n) -> p k n", k=5)
        trow = s5in[:, 5 * SEQ:]
        cc = s5in[:, :].rearrange("p (k j c) -> p k j c", k=3, c=32)
        bb = sb("bb", [P, 2, 4, 2, HD])
        small = sb("small", [P, 256])
        stat = sb("stat", [P, 20, 4])
        TABLES = 11008
        chw = sb("chw", [P, 8, SEQ])[:, :, :]
        scratch = sb("scratch", [P, TABLES + 2 * S5_TILES * SEQ])
        ps = ctx.enter_context(nc.psum_tensor("ps", [P, 8 * 512], F32))

        def bank(i, n=1):
            return ps[:, i * 512:(i + n) * 512]

        at, limit = [0], [TABLES + 2 * S5_TILES * SEQ]

        def take(n):
            at[0] += n
            assert at[0] <= limit[0], at[0]
            return scratch[:, at[0] - n:at[0]]

        postw = scratch[:, 0:2 * D].rearrange("p (t n) -> p t n", t=TT)
        tabS = scratch[:, TABLES:TABLES + S5_TILES * SEQ].rearrange("p (j t) -> p j t", t=SEQ)
        tabC = scratch[:, TABLES + S5_TILES * SEQ:].rearrange("p (j t) -> p j t", t=SEQ)
        diag = prod_s[:, 0, :].rearrange("p (t m) -> p t m", t=TT)

        at[0] = 2 * D
        biasB = take(TT * SEQ).rearrange("p (t k) -> p t k", t=TT)
        axial = take(2 * TT * HD).rearrange("p (k t d) -> p k t d", k=2, t=TT)
        qkg = take(4 * HD).rearrange("p (k d) -> p k d", k=4)
        rope_q = take(2 * TT * 4 * HD).rearrange("p (k t h d) -> p k t h d", k=2, t=TT, h=4)
        rope_k = take(2 * TT * 2 * HD).rearrange("p (k t h d) -> p k t h d", k=2, t=TT, h=2)
        rope_b = take(2 * TT * 4 * HD).rearrange("p (k t h d) -> p k t h d", k=2, t=TT, h=4)
        qT = [take(4 * SEQ).rearrange("p (c s) -> p c s", s=SEQ) for _ in range(2)]
        kTA = take(SEQ)
        kTB = take(4 * SEQ).rearrange("p (c s) -> p c s", s=SEQ)
        vA = take(TT * P).rearrange("p (t n) -> p t n", t=TT)
        vB = take(TT * 512).rearrange("p (t n) -> p t n", t=TT)
        raw = take(2 * 512).rearrange("p (r n) -> p r n", r=2)
        xn1 = take(512)
        t1 = take(512)
        t2 = take(512)
        rop = take(2 * 512).rearrange("p (r n) -> p r n", r=2)
        pT = [take(2 * 512).rearrange("p (r n) -> p r n", r=2)]
        at[0] = 0
        probs = [take(3 * 512).rearrange("p (r n) -> p r n", r=3)]
        ssc = [raw]
        at[0], limit[0] = TABLES - 2048, TABLES
        tri = take(2 * P).rearrange("p (k m) -> p k m", k=2)
        mask = take(384)
        gbd = take(2 * 4 * P).rearrange("p (w c m) -> p w c m", w=2, c=4)
        at[0], limit[0] = 0, TABLES - 2048
        qS = take(4 * SEQ).rearrange("p (c s) -> p c s", c=4)
        kS = take(4 * SEQ).rearrange("p (c s) -> p c s", c=4)
        vS = take(TT * 512).rearrange("p (t n) -> p t n", t=TT)
        xc = take(4 * SEQ).rearrange("p (c s) -> p c s", c=4)
        after = at[0]
        xr = take(4 * (SEQ + 3)).rearrange("p (c s) -> p c s", c=4)
        gg = ffn_s
        rgate = take(4 * SEQ).rearrange("p (c s) -> p c s", c=4)
        igate = take(4 * SEQ).rearrange("p (c s) -> p c s", c=4)
        rga = take(4 * SEQ).rearrange("p (c s) -> p c s", c=4)
        at[0] = after
        zs = take(4 * 768).rearrange("p (b h s) -> p b h s", b=4, h=2)
        lg = [take(768).rearrange("p (h s) -> p h s", h=2) for _ in range(2)]
        lg += [chw[:, 3 * k:3 * k + 3, :].rearrange("p a b -> p (a b)").rearrange("p (h s) -> p h s", h=2)
               for k in range(2)]
        glu = scratch[:, TABLES - 2048:TABLES].rearrange("p (k m) -> p k m", k=4)
        biasM = chw.rearrange("p (m t) k -> p m t k", m=4)
        at[0] = 0
        uT = take(4 * SEQ).rearrange("p (c s) -> p c s", c=4)
        qM = take(4 * SEQ).rearrange("p (c s) -> p c s", c=4)
        kM = take(4 * SEQ).rearrange("p (c s) -> p c s", c=4)
        vM = take(TT * 512).rearrange("p (t n) -> p t n", t=TT)
        yT = take(4 * SEQ).rearrange("p (c s) -> p c s", c=4)
        after = at[0]
        pc, pw = (chw[:, k:k + 4, :].rearrange("p (r h) s -> p r h s", r=2) for k in (0, 4))
        zz, dC, dS = (take(2 * 512).rearrange("p (r h s) -> p r h s", r=2, h=2) for _ in range(3))
        at[0] = after
        probs.append(take(3 * 512).rearrange("p (r n) -> p r n", r=3))
        pT.append(take(2 * 512).rearrange("p (r n) -> p r n", r=2))
        ssc.append(take(2 * 512).rearrange("p (r n) -> p r n", r=2))

        st = {n: small[:, 160 + 2 * k:162 + 2 * k + 2 * (n in ("ss", "pss"))] for k, n in
              ((0, "ss"), (2, "mean0"), (3, "std"), (4, "rinv"),
               (5, "pss"), (7, "pmean0"), (8, "pstd"), (9, "prinv"), (10, "warm"))}
        qk = {n: small[:, 16 + 8 * k:24 + 8 * k] for k, n in enumerate(["ss", "var", "std", "rinv"])}
        lam = {n: small[:, 48 + 4 * k:52 + 4 * k]
               for k, n in enumerate(["e", "den", "s", "s2", "acc", "pos", "neg8", "pos8"])}
        s5s = {n: small[:, 80 + 16 * k:96 + 16 * k] for k, n in enumerate(["dt", "mag", "th", "k", "t"])}

        def col(k, n=1):
            return cols[:, k:k + n]

        s = {n: sem(n) for n in [
            "x_loaded0", "x_loaded1", "early_loaded", "s5c_loaded", "late_loaded", "ab_loaded", "cd_loaded",
            "biasM_loaded", "gu_loaded0", "gu_loaded1", "dn_loaded0", "dn_loaded1", "gpost_loaded", "gpost_ffn2", "gpost_final", "out_stored",
            "sq_done", "std_ready", "diag_ready", "hT_psum", "hT_high", "hT_low",
            "gu_high", "gu_split", "dn_high", "dn_split",
            "gate_ready", "up_ready", "silu_ready", "prod_done", "act_high", "act_ready", "down_done",
            "ffn_tt0", "mix_tt0",
            "psq_done", "pstd_ready", "gained", "x_ready", "final_ready",
            "proj_done", "proj_free", "raw_ready", "qkvar_ready", "qkstd_ready", "xn_ready", "t2_ready",
            "rop_ready", "ropT_psum", "ropT_evac",
            "s_ready", "max_ready", "p_ready", "pn_ready", "pt_psum", "pt_ready", "v_done", "o_high", "o_ready",
            "tables_ready", "exp_dt", "lam_e", "lam_den", "lam_rden", "lam_s", "s5_arg", "s5_trig", "s5_rden", "angles", "trig",
            "zeroed", "conv_done", "gates_done", "rg_act", "rg_q", "rg_sqrt", "rg_ix", "rg_y", "rg_high", "rg_done",
            "z_psum", "z_evac", "z_log", "sp_ready", "r_psum", "t_ready",
            "w_ready", "sbo_psum", "sbo_high", "sbo_done",
            "bb_ready", "cc_ready", "bu_done", "s5_mod", "zin_ready", "s5_scan", "s5_dem", "y_done", "y_sum",
            "y_gelu", "glu_psum", "glu_sig", "s5_y", "s5_high", "s5_done",
            "dve_step", "act_step", "pool_step"]}
        gu_loaded = [s["gu_loaded0"], s["gu_loaded1"]]
        dn_loaded = [s["dn_loaded0"], s["dn_loaded1"]]

        def loaded(item):
            return 16 * (item // 2 + 1)

        def during(i, r):
            if r is None:
                return (lambda c: c + i), (lambda c: loaded(c + i))
            return (lambda c: r * 2 + (c + i)), (lambda c: r * 16 + loaded(c + i))

        PASSES = ((0, 0), (0, 1), (1, 0))

        def wait_used(engine, g):
            for f in range(4):
                if FFN_ITEM[f] <= g < FFN_ITEM[f] + FCH:
                    engine.wait_ge(s["up_ready"], FCH * f + g - FFN_ITEM[f] + 1)
            for m in range(3):
                if MIX_ITEM[m] <= g < MIX_ITEM[m] + MIX_IN[m] + MIX_OUT:
                    engine.wait_ge(s["proj_done"], UNITS[m] + g - MIX_ITEM[m] + 1)

        def wait_out(engine, p, t):
            if t == 0:
                engine.wait_ge(s["mix_tt0" if p % 2 else "ffn_tt0"], p // 2 + 1)
            elif p % 2 == 0:
                engine.wait_ge(s["down_done"], FCH * (p // 2 + 1))
            else:
                engine.wait_ge(s["proj_done"], UNITS[p // 2 + 1])

        def wait_unit(engine, m, j):
            if m == 0 and j < 7:
                engine.wait_ge(s["raw_ready"], j + 1)
            else:
                engine.wait_ge(s["proj_free"], (j - 6, j + 3, j + 13)[m])

        def rope_heads(r):
            return 2 if r == 2 else 4

        def rope_dst(r):
            if r == 2:
                return kTA.unsqueeze(1)
            dst, u = {0: (qT[0], 0), 1: (qT[0], 1), 3: (qT[1], 0), 4: (qT[1], 1), 5: (kTB, 0),
                      6: (kTB, 1)}[r]
            return dst[:, 2 * u:2 * u + 2, :]

        def head(a_, q, k, v, bias, scale, phase, o, heads_out, out_free):
            biased = bias is not None
            return dict(a=a_, q=q, k=k, v=v, bias=bias, scale=scale, o=o, heads_out=heads_out,
                        out_free=out_free,
                        exp_in=ssc[phase][:, a_ % 2, :] if biased else bank(a_ % 3),
                        exp_scale=1.0 if biased else scale,
                        probs=probs[phase][:, a_ % 3, :], pT=pT[phase][:, a_ % 2, :])

        heads1 = []
        for pair in range(8):
            for e in range(2):
                half = slice(64 * e, 64 * e + 64)
                c = pair % 4
                obank = bank(5 + pair % 2)
                dense = pair < 4
                heads1.append(head(
                    2 * pair + e, qT[0 if dense else 1][half, c, :],
                    kTA[half, :] if dense else kTB[half, c, :],
                    vA[:, :, half] if dense else vB[:, :, (2 * c + e) * HD:(2 * c + e + 1) * HD],
                    None if dense else biasB[:, :, :], HD ** -0.5, 0, obank[half, 0:SEQ],
                    (obank[:, 0:SEQ], pair) if e else None,
                    pair - 1 if pair >= 2 else None))
        heads2 = []
        for m in range(4):
            obank = bank(5 + m % 2)[:, 0:SEQ]
            heads2.append(head(16 + m, qM[:, m, :], kM[:, m, :], vM[:, :, m * P:(m + 1) * P],
                               biasM[:, m, :, :], P ** -0.5, 1, obank, (obank, 4 + m),
                               8 + m - 1 if m >= 2 else None))

        block = ctx.enter_context(nc.Block())

        @block.sync
        def _(sp_):
            for t in range(TT):
                sp_.dma_start(x[:, t, :], a["x"][:, t, :]).then_inc(s["x_loaded%d" % t], 16)

            def load_gu(g, slot, guard=True):
                if guard:
                    sp_.wait_ge(s["gu_split"], g - 1)
                sp_.dma_start(gu_raw[:, slot, :], a["wgu"][g]).then_inc(gu_loaded[slot], 16)

            def load_dn(d, slot, guard=True):
                if guard:
                    sp_.wait_ge(s["dn_split"], d - 1)
                sp_.dma_start(dn_raw[:, slot, :], a["wdn"][d]).then_inc(dn_loaded[slot], 16)

            for g in range(4):
                if g == 2:
                    for d in range(2):
                        load_dn(d, d, guard=False)
                load_gu(g, g % 2, guard=g >= 2)
            for kind, n in STREAM:
                if kind == "ffn":
                    base, d0 = FFN_ITEM[n], FCH * n
                    load_dn(d0 + 2, d0 % 2)
                    whole = min(FCH - 2, N_ITEMS - 4 - base) // 2
                    with sp_.Fori(0, whole) as r:
                        for h in range(2):
                            load_dn(r * 2 + (d0 + h + 3), (d0 + h + 3) % 2)
                            load_gu(r * 2 + (base + h + 4), (base + h) % 2)
                    for i in range(2 * whole, FCH):
                        if i <= FCH - 2 and d0 + i + 3 < 4 * FCH:
                            load_dn(d0 + i + 3, (d0 + i + 3) % 2)
                        if base + i + 4 < N_ITEMS:
                            load_gu(base + i + 4, (base + i) % 2)
                else:
                    for g in range(MIX_ITEM[n] + 4, MIX_ITEM[n] + MIX_IN[n] + MIX_OUT + 4):
                        load_gu(g, g % 2)
            for q in range(2 * TT):
                t, hs = q // 2, slice(q % 2 * 512, q % 2 * 512 + 512)
                sp_.wait_ge(s["final_ready"], q + 1)
                sp_.dma_start(a["out"][:, t, hs], postw[:, t, hs]).then_inc(s["out_stored"], 16)
            sp_.wait_ge(s["out_stored"], 16 * 2 * TT)

        @block.tensor
        def _(pe):
            def transposes(n):
                for t in range(TT):
                    pe.wait_ge(s["diag_ready"], TT * n + t + 1)
                    for c in range(KC):
                        at_ = (c % 2) * SEQ + t * P
                        i = nc.tensor.matmul(bank(4 + c // 2)[:, at_:at_ + P], x[:, t, c * P:(c + 1) * P],
                                             diag[:, t, :], start=True, stop=True)
                        if t == 1 and c % 2 == 1:
                            i.then_inc(s["hT_psum"], 1)

            def wait_hT(n, k):
                pe.wait_ge(s["hT_low"], KC * n + k + 1)

            def gate_up(h, sl, item, G, first=None):
                pe.wait_ge(s["gu_split"], item + 1)
                if not isinstance(G, int) or G >= 2:
                    pe.wait_ge(s["prod_done"], G - 1)
                for w in range(2):
                    for k in range(KC):
                        if first is not None and w == 0:
                            wait_hT(first, k)
                            if k == 0:
                                wait_hT(first, 1)
                        o = (w * KC + k) * P
                        for pw_, px in PASSES:
                            i = nc.tensor.matmul(bank(4 + 2 * w + h)[:, 0:SEQ],
                                                 gu[pw_][:, sl, o:o + P], hT[px][:, k, :],
                                                 start=(pw_, px, k) == (0, 0, 0),
                                                 stop=(pw_, px, k) == (1, 0, KC - 1))
                    i.then_inc(s["gate_ready" if w == 0 else "up_ready"], 1)

            def down(h, G, start=False, stop=False):
                pe.wait_ge(s["dn_split"], G + 1)
                pe.wait_ge(s["act_ready"], G + 1)
                for t in range(TT):
                    for px, pw_ in PASSES:
                        for half in range(2):
                            i = nc.tensor.matmul(bank(2 * t + half), act_s[px][:, h, t * P:(t + 1) * P],
                                                 dn[pw_][:, h, half * 512:half * 512 + 512],
                                                 start=start and (px, pw_) == (0, 0),
                                                 stop=stop and (px, pw_) == (1, 0))
                    if stop and t == 0:
                        i.then_inc(s["ffn_tt0"], 1)
                i.then_inc(s["down_done"], 1)

            def ffn(f, n):
                base, G0 = FFN_ITEM[f], FCH * f
                gate_up(0, base % 2, base, G0, first=n)
                gate_up(1, 1 - base % 2, base + 1, G0 + 1)
                down(0, G0, start=True)
                with pe.Fori(1, FCH // 2) as r:
                    for h in range(2):
                        gate_up(h, (base + h) % 2, r * 2 + (base + h), r * 2 + (G0 + h))
                        down(1 - h, r * 2 + (G0 + h - 1))
                down(1, G0 + FCH - 1, stop=True)

            def project(m, v, n, feature):
                item = MIX_ITEM[m] + v
                sl = item % 2
                pe.wait_ge(s["gu_split"], item + 1)
                if v >= 4:
                    wait_unit(pe, m, v - 4)
                out = bank(v % 4)
                for h in range(2):
                    for k in range(KC):
                        if v == 0 and h == 0:
                            wait_hT(n, k)
                        for pw_, px in PASSES:
                            wk = gu[pw_][:, sl, k * SEQ:(k + 1) * SEQ]
                            cut_ = slice(h * P, (h + 1) * P)
                            lhsT, rhs = ((wk[:, cut_], hT[px][:, k, :]) if feature
                                         else (hT[px][:, k, cut_], wk))
                            i = nc.tensor.matmul(out[:, h * SEQ:(h + 1) * SEQ], lhsT, rhs,
                                                 start=(pw_, px, k) == (0, 0, 0),
                                                 stop=(pw_, px, k) == (1, 0, KC - 1))
                i.then_inc(s["proj_done"], 1)

            def project_out(m, ready):
                for u in range(MIX_OUT):
                    item = MIX_ITEM[m] + MIX_IN[m] + u
                    pe.wait_ge(s["gu_split"], item + 1)
                    for t in range(TT):
                        out = bank(2 * t + u // 2)[:, (u % 2) * SEQ:(u % 2 + 1) * SEQ]
                        for k in range(KC):
                            if u == 0 and t == 0:
                                name, value = ready(k)
                                pe.wait_ge(s[name], value)
                            for pw_, px in PASSES:
                                i = nc.tensor.matmul(out, hT[px][:, k, t * P:(t + 1) * P],
                                                     gu[pw_][:, item % 2, k * SEQ:(k + 1) * SEQ],
                                                     start=(pw_, px, k) == (0, 0, 0),
                                                     stop=(pw_, px, k) == (1, 0, KC - 1))
                        if u == MIX_OUT - 1 and t == 0:
                            i.then_inc(s["mix_tt0"], 1)
                    i.then_inc(s["proj_done"], 1)

            def attention(heads):
                first, last = heads[0]["a"], heads[-1]["a"]
                for step in range(first, last + 4):
                    if step <= last:
                        h = heads[step - first]
                        if step >= first + 3:
                            pe.wait_ge(s["p_ready"], step - 2)
                        for t in range(TT):
                            i = nc.tensor.matmul(bank(step % 3)[:, t * SEQ:(t + 1) * SEQ],
                                                 h["q"][:, t * P:(t + 1) * P], h["k"],
                                                 start=True, stop=True)
                        i.then_inc(s["s_ready"], 1)
                    e = step - 2
                    if first <= e <= last:
                        pe.wait_ge(s["pn_ready"], e + 1)
                        if e >= first + 2:
                            pe.wait_ge(s["pt_ready"], e - 1)
                        pr = heads[e - first]["probs"]
                        for kt in range(TT):
                            for t in range(TT):
                                o = kt * SEQ + t * P
                                i = nc.tensor.transpose(bank(3 + e % 2)[:, o:o + P],
                                                        pr[:, t * SEQ + kt * P:t * SEQ + (kt + 1) * P],
                                                        ident[:, :])
                        i.then_inc(s["pt_psum"], 1)
                    e = step - 3
                    if first <= e <= last:
                        h = heads[e - first]
                        pe.wait_ge(s["pt_ready"], e + 1)
                        if h["out_free"] is not None:
                            pe.wait_ge(s["o_ready"], h["out_free"])
                        for kt in range(TT):
                            i = nc.tensor.matmul(h["o"], h["v"][:, kt, :],
                                                 h["pT"][:, kt * SEQ:(kt + 1) * SEQ],
                                                 start=kt == 0, stop=kt == TT - 1)
                        i.then_inc(s["v_done"], 1)

            transposes(0)
            ffn(0, 0)
            transposes(1)
            for v in range(9):
                project(0, v, 1, False)
                r = v - 1
                if 0 <= r < 7:
                    pe.wait_ge(s["rop_ready"], r + 1)
                    if r >= 2:
                        pe.wait_ge(s["ropT_evac"], r - 1)
                    w = rope_heads(r) * HD
                    for c in range(w // P):
                        for t in range(TT):
                            i = nc.tensor.transpose(
                                bank(4 + r % 2)[:, c * SEQ + t * P:c * SEQ + (t + 1) * P],
                                rop[:, r % 2, t * w + c * P:t * w + (c + 1) * P], ident[:, :])
                    i.then_inc(s["ropT_psum"], 1)
            pe.wait_ge(s["ropT_evac"], 7)
            wait_unit(pe, 0, 8)
            attention(heads1)
            project_out(0, lambda k: ("o_ready", k + 1))
            transposes(2)
            ffn(1, 2)

            transposes(3)
            for v in range(4):
                project(1, v, 3, True)
            pe.wait_ge(s["conv_done"], 4)
            pe.wait_ge(s["ab_loaded"], 48)
            for w in range(2):
                for c in range(4):
                    i = nc.tensor.matmul(bank(4 + 2 * w, 2)[:, c * SEQ:(c + 1) * SEQ], gbd[:, w, c, :],
                                         xc[:, c, :], start=True, stop=True)
            i.then_inc(s["gates_done"], 1)
            for v in range(4, 9):
                project(1, v, 3, v < 8)

            def stick_scores(b):
                for e in range(2):
                    r0 = slice(64 * e, 64 * e + 64)
                    z = bank(STICK_BANK[b] + e)
                    nc.tensor.matmul(z[:, 0:SEQ], kS[r0, b, 0:P], qS[r0, b, :], start=True, stop=True)
                    i = nc.tensor.matmul(z[:, SEQ:384], kS[r0, b, P:SEQ], qS[r0, b, P:SEQ],
                                         start=True, stop=True)
                i.then_inc(s["z_psum"], 1)

            def stick_sums(b):
                pe.wait_ge(s["sp_ready"], b + 1)
                for e in range(2):
                    R = bank(STICK_BANK[b] + e)
                    w = lg[b][:, e, :]
                    nc.tensor.matmul(R[:, 0:SEQ], tri[:, 0, :], w[:, 0:SEQ], start=True, stop=False)
                    nc.tensor.matmul(R[:, P:SEQ], tri[:, 1, :], w[:, SEQ:384], start=False, stop=True)
                    i = nc.tensor.matmul(R[:, SEQ:384], tri[:, 0, :], w[:, SEQ:384], start=True, stop=True)
                i.then_inc(s["r_psum"], 1)

            def stick_values(b):
                pe.wait_ge(s["w_ready"], b + 1)
                for e in range(2):
                    o = bank(STICK_OUT[b])[64 * e:64 * e + 64, :]
                    w = zs[:, b, e, :]
                    v = vS[:, :, (2 * b + e) * HD:(2 * b + e + 1) * HD]
                    nc.tensor.matmul(o[:, 0:SEQ], v[:, 0, :], w[:, 0:SEQ], start=True, stop=False)
                    i = nc.tensor.matmul(o[:, P:SEQ], v[:, 1, :], w[:, SEQ:384], start=False, stop=True)
                i.then_inc(s["sbo_psum"], 1)

            pe.wait_ge(s["rg_act"], 4)
            wait_unit(pe, 1, 7)
            stick_scores(0)
            project(1, 9, 3, False)
            stick_scores(1)
            wait_unit(pe, 1, 9)
            stick_scores(2)
            stick_scores(3)
            stick_sums(0)
            for b in range(4):
                if b + 1 < 4:
                    stick_sums(b + 1)
                stick_values(b)
            project_out(1, lambda k: ("rg_done", k + 1) if k < 4 else ("sbo_done", k - 3))
            transposes(4)
            ffn(2, 4)

            transposes(5)
            project(2, 0, 5, True)
            project(2, 1, 5, True)
            wait_unit(pe, 2, 1)
            pe.wait_ge(s["bb_ready"], 4)

            def s5_in(j):
                c, q = j // 4, j % 4
                if j >= 2:
                    pe.wait_ge(s["s5_mod"], 2 * (j - 1))
                r0 = slice(32 * q, 32 * q + 32)
                for part in range(2):
                    i = nc.tensor.matmul(bank(4 + j % 2)[:, part * SEQ:(part + 1) * SEQ],
                                         bb[r0, part, c, :, :].rearrange("p g n -> p (g n)"),
                                         uT[r0, c, :], start=True, stop=True)
                i.then_inc(s["bu_done"], 1)

            def s5_out(j):
                c, q = j // 4, j % 4
                pe.wait_ge(s["s5_dem"], 2 * (j + 1))
                out = bank(6, 2)[32 * q:32 * q + 32, c * SEQ:(c + 1) * SEQ]
                r = j % 2
                terms = [(0, dC[:, r, 0, :]), (2, dS[:, r, 1, :]), (1, dS[:, r, 0, :]), (1, dC[:, r, 1, :])]
                for k, (w, z) in enumerate(terms):
                    i = nc.tensor.matmul(out, cc[:, w, j, :], z, start=k == 0, stop=k == 3)
                i.then_inc(s["y_done"], 1)

            pe.wait_ge(s["cc_ready"], 1)
            s5_in(0)
            s5_in(1)
            for j in range(S5_TILES):
                if j + 2 < S5_TILES:
                    s5_in(j + 2)
                if j % 2 == 0 and j < 12:
                    v = 2 + j // 2
                    project(2, v, 5, v // 2 != 3)
                s5_out(j)
            wait_unit(pe, 2, 7)
            for o in range(4):
                for k in range(4):
                    if o == 0:
                        pe.wait_ge(s["y_gelu"], k + 1)
                    i = nc.tensor.matmul(bank(4 + o)[:, 0:SEQ], glu[:, k, o * P:(o + 1) * P], yT[:, k, :],
                                         start=k == 0, stop=k == 3)
                i.then_inc(s["glu_psum"], 1)
            pe.wait_ge(s["s5_done"], 4)
            attention(heads2)
            project_out(2, lambda k: ("s5_done", k + 1) if k < 4 else ("o_ready", 8 + k - 3))
            transposes(6)
            ffn(3, 6)

        @block.scalar
        def _(act):
            step = Step(s["act_step"])
            for name, dst in (("ident", ident[:, :]), ("cols", cols[:, :])):
                act.dma_start(dst, a[name]).then_inc(s["early_loaded"], 16)

            def first_constants():
                for k, name in enumerate(("ffn1_post_g", "mix_post_g")):
                    act.dma_start(gpost[:, k, :], a[name].partition_broadcast(P)) \
                        .then_inc(s["gpost_loaded"], 16)
                act.dma_start(s5in[:, :], a["s5in"]).then_inc(s["s5c_loaded"], 16)
                for name, dst in (("biasB", biasB[:, :, :]), ("axial", axial[:, :, :, :]),
                                  ("qkg", qkg[:, :, :]), ("rope_b", rope_b[:, :, :, :, :])):
                    act.dma_start(dst, a[name]).then_inc(s["late_loaded"], 16)

            def first_exps():
                act.wait_ge(s["s5c_loaded"], 16)
                step.mark(nc.scalar.activation(lam["e"], col(COL_LAM, 4), ACT.Abs))
                nc.scalar.activation(s5s["dt"], col(COL_LDT, S5_TILES), ACT.Exp).then_inc(s["exp_dt"], 1)
                nc.scalar.activation(s5c[:, 2, :], s5c[:, 2, :], ACT.Exp).then_inc(s["exp_dt"], 1)
                step.done(act)
                nc.scalar.activation(lam["e"], lam["e"], ACT.Exp, scale=-1.0).then_inc(s["lam_e"], 1)

            def gu_high(g):
                if g >= 2:
                    wait_used(act, g - 2)
                act.wait_ge(gu_loaded[g % 2], loaded(g))
                nc.scalar.activation(gu[0][:, g % 2, :], gu_raw[:, g % 2, :], ACT.Copy) \
                  .then_inc(s["gu_high"], 1)

            def dn_high_first(f):
                act.wait_ge(dn_loaded[0], loaded(FCH * f))
                nc.scalar.activation(dn[0][:, 0, :], dn_raw[:, 0, :], ACT.Copy).then_inc(s["dn_high"], 1)

            def warm_sqrt():
                step.mark(nc.scalar.activation(st["warm"][:, 0:1], col(COL_HALFPI), ACT.Sqrt))
                step.done(act)

            def norm(n):
                for t in range(TT):
                    for half in range(2):
                        if n > 0:
                            act.wait_ge(s["x_ready"], 4 * (n - 1) + 2 * t + half + 1)
                        elif half == 0:
                            act.wait_ge(s["x_loaded%d" % t], 16)
                        hs = slice(half * 512, (half + 1) * 512)
                        k = 2 * t + half
                        nc.scalar.activation(postw[:, t, hs], x[:, t, hs], ACT.Square,
                                             accum_out=st["ss"][:, k:k + 1]).then_inc(s["sq_done"], 1)
                        act.wait_ge(s["sq_done"], 4 * n + k + 1)
                        if half == 0:
                            step.mark(nc.scalar.activation(st["mean0"][:, t:t + 1], st["ss"][:, k:k + 1],
                                                           ACT.Identity, scale=1.0 / D, bias=col(COL_EPS)))
                    step.done(act)
                    nc.scalar.activation(st["std"][:, t:t + 1], st["ss"][:, k:k + 1], ACT.Sqrt,
                                         scale=1.0 / D, bias=st["mean0"][:, t:t + 1]) \
                      .then_inc(s["std_ready"], 1)

            def norm_out(n):
                for c in range(KC):
                    act.wait_ge(s["hT_psum"], 4 * n + c // 2 + 1)
                    nc.scalar.activation(hT[0][:, c, :], bank(4 + c // 2)[:, c % 2 * SEQ:(c % 2 + 1) * SEQ],
                                         ACT.Copy, scale=col(COL_GAIN + n * KC + c)) \
                      .then_inc(s["hT_high"], 1)

            def ffn(f, side={}):
                base, G0 = FFN_ITEM[f], FCH * f

                def step_of(i, r=None):
                    plain, arrived = during(i, r)
                    h, static = i % 2, r is None
                    act.wait_ge(s["gate_ready"], plain(G0 + 1))
                    if not static or G0 + i >= 2:
                        act.wait_ge(s["prod_done"], plain(G0 - 1))
                    nc.scalar.activation(sil_s[:, h, :], bank(4 + h)[:, 0:SEQ], ACT.Silu) \
                      .then_inc(s["silu_ready"], 1)
                    if not static or i < FCH - 1:
                        act.wait_ge(dn_loaded[1 - h], arrived(G0 + 1))
                        if not static or G0 + i > 0:
                            act.wait_ge(s["down_done"], plain(G0))
                        nc.scalar.activation(dn[0][:, 1 - h, :], dn_raw[:, 1 - h, :], ACT.Copy) \
                          .then_inc(s["dn_high"], 1)
                    sl = (base + i) % 2
                    if not static or base + i + 2 < N_ITEMS:
                        act.wait_ge(gu_loaded[sl], arrived(base + 2))
                        act.wait_ge(s["up_ready"], plain(G0 + 1))
                        nc.scalar.activation(gu[0][:, sl, :], gu_raw[:, sl, :], ACT.Copy) \
                          .then_inc(s["gu_high"], 1)

                step_of(0)
                step_of(1)
                first = 2
                for i in range(2, FCH, 2):
                    if i < FCH - 2 and not (side.keys() & {i, i + 1}):
                        continue
                    if i > first:
                        with act.Fori(first // 2, i // 2) as r:
                            for h in range(2):
                                step_of(h, r)
                    for k in (i, i + 1):
                        step_of(k)
                        if k in side:
                            side[k]()
                    first = i + 2

            def evacuate(m, v, dst, func=ACT.Copy):
                gu_high(MIX_ITEM[m] + v + 2)
                act.wait_ge(s["proj_done"], UNITS[m] + v + 1)
                src = bank(v % 4).rearrange("p (h s) -> p h s", h=2)
                nc.scalar.activation(dst, src, func).then_inc(s["proj_free"], 1)

            def out_splits(m):
                for u in range(MIX_OUT - 1):
                    gu_high(MIX_ITEM[m] + MIX_IN[m] + u + 2)

            def next_splits(f):
                if f:
                    gu_high(FFN_ITEM[f] + 1)
                dn_high_first(f)

            def post(p):
                c = 1.0 if p % 2 else 4.0
                warm_sqrt()
                for t in range(TT):
                    wait_out(act, p, t)
                    for half in range(2):
                        k = 2 * t + half
                        if half == 1:
                            act.wait_ge(s["gained"], 4 * p + k)
                        nc.scalar.activation(bank(4 + k), bank(k), ACT.Square,
                                             accum_out=st["pss"][:, k:k + 1]).then_inc(s["psq_done"], 1)
                        act.wait_ge(s["psq_done"], 4 * p + k + 1)
                        if half == 0:
                            step.mark(nc.scalar.activation(
                                st["pmean0"][:, t:t + 1], st["pss"][:, k:k + 1], ACT.Identity,
                                scale=c / D, bias=col(COL_EPS + (p % 2 == 0))))
                    step.done(act)
                    nc.scalar.activation(st["pstd"][:, t:t + 1], st["pss"][:, k:k + 1], ACT.Sqrt,
                                         scale=c / D, bias=st["pmean0"][:, t:t + 1]) \
                      .then_inc(s["pstd_ready"], 1)

            def attention(heads):
                first, last = heads[0]["a"], heads[-1]["a"]
                for e in range(first, last + 4):
                    if e <= last:
                        h = heads[e - first]
                        act.wait_ge(s["max_ready"], e + 1)
                        if e >= first + 3:
                            act.wait_ge(s["pt_psum"], e - 2)
                        for t in range(TT):
                            i = nc.scalar.activation(
                                h["probs"][:, t * SEQ:(t + 1) * SEQ], h["exp_in"][:, t * SEQ:(t + 1) * SEQ],
                                ACT.Exp, bias=stat[:, h["a"], t:t + 1], scale=h["exp_scale"],
                                accum_out=stat[:, h["a"], 2 + t:3 + t])
                        i.then_inc(s["p_ready"], 1)
                    g = e - 2
                    if first <= g <= last:
                        h = heads[g - first]
                        act.wait_ge(s["pt_psum"], g + 1)
                        if g >= first + 2:
                            act.wait_ge(s["v_done"], g - 1)
                        nc.scalar.activation(h["pT"], bank(3 + g % 2), ACT.Copy).then_inc(s["pt_ready"], 1)
                    g = e - 3
                    if first <= g <= last and heads[g - first]["heads_out"] is not None:
                        act.wait_ge(s["v_done"], g + 1)
                        src, c = heads[g - first]["heads_out"]
                        nc.scalar.activation(hT[0][:, c, :], src, ACT.Copy).then_inc(s["o_high"], 1)

            act.wait_ge(s["early_loaded"], 32)
            warm_sqrt()
            norm(0)
            gu_high(0)
            norm_out(0)
            gu_high(1)
            next_splits(0)
            first_constants()
            ffn(0, {2: first_exps})
            post(0)
            norm(1)
            norm_out(1)

            def rope_in_out(r):
                act.wait_ge(s["ropT_psum"], r + 1)
                n = rope_heads(r) // 2
                nc.scalar.activation(rope_dst(r), bank(4 + r % 2)[:, 0:n * SEQ]
                                     .rearrange("p (c q) -> p c q", q=SEQ), ACT.Copy) \
                  .then_inc(s["ropT_evac"], 1)

            for v in range(9):
                if v < 7:
                    gu_high(MIX_ITEM[0] + v + 2)
                    if v >= 2:
                        act.wait_ge(s["rop_ready"], v - 1)
                    act.wait_ge(s["proj_done"], v + 1)
                    w = rope_heads(v) * HD
                    src = bank(v % 4).rearrange("p (t n) -> p t n", t=TT)
                    if v == 2:
                        nc.scalar.activation(vA, src[:, :, P:2 * P], ACT.Copy)
                    nc.scalar.activation(raw[:, v % 2, 0:TT * w].rearrange("p (t n) -> p t n", t=TT),
                                         src[:, :, 0:w], ACT.Copy).then_inc(s["raw_ready"], 1)
                    if v < 3:
                        nh = TT * rope_heads(v)
                        act.wait_ge(s["qkvar_ready"], v + 1)
                        nc.scalar.activation(qk["std"][:, 0:nh], qk["var"][:, 0:nh], ACT.Sqrt) \
                          .then_inc(s["qkstd_ready"], 1)
                else:
                    evacuate(0, v, vB[:, :, (v - 7) * SEQ:(v - 6) * SEQ])
                if 0 <= v - 1 < 7:
                    rope_in_out(v - 1)
            attention(heads1)
            out_splits(0)
            post(1)
            norm(2)
            for name, dst in (("tri", tri), ("mask", mask), ("gbd", gbd)):
                act.dma_start(dst, a[name]).then_inc(s["ab_loaded"], 16)
            norm_out(2)
            next_splits(1)

            def trig_tables(jb, half):
                tS, tC = tabS[:, 4 * jb:4 * jb + 4, :], tabC[:, 4 * jb:4 * jb + 4, :]
                if half == 0:
                    act.wait_ge(s["angles"], jb + 1)
                    step.mark(nc.scalar.activation(tC, tS, ACT.Abs))
                    step.done(act)
                    nc.scalar.activation(tC, tC, ACT.Sin, bias=col(COL_HALFPI), scale=-1.0) \
                      .then_inc(s["trig"], 1)
                else:
                    nc.scalar.activation(tS, tS, ACT.Sin).then_inc(s["trig"], 1)

            def s5_coefficients():
                act.wait_ge(s["s5_arg"], 1)
                nc.scalar.activation(chw[:, 0, :], chw[:, 0, :], ACT.Exp).then_inc(s["s5_trig"], 1)
                nc.scalar.activation(s5s["mag"], s5s["mag"], ACT.Exp).then_inc(s["s5_trig"], 1)
                nc.scalar.activation(chw[:, 2, :], chw[:, 1, :], ACT.Sin).then_inc(s["s5_trig"], 1)
                step.mark(nc.scalar.activation(chw[:, 3, :], chw[:, 1, :], ACT.Abs))
                step.done(act)
                nc.scalar.activation(chw[:, 3, :], chw[:, 3, :], ACT.Sin, bias=col(COL_HALFPI), scale=-1.0) \
                  .then_inc(s["s5_trig"], 1)

            ffn(1, {2: s5_coefficients} | {FCH - 10 + 2 * jb + half: (lambda jb=jb, half=half: trig_tables(jb, half))
                    for jb in range(4) for half in range(2)})
            post(2)
            norm(3)
            norm_out(3)

            for v in range(2):
                evacuate(1, v, xr[:, 2 * v:2 * v + 2, 3:])
            for v in range(2, 4):
                evacuate(1, v, gg[:, 2 * (v % 2):2 * (v % 2) + 2, :], ACT.Gelu_apprx_tanh)
            act.wait_ge(s["gates_done"], 1)
            for w, dst, bias in ((0, rgate, COL_BA), (1, igate, COL_BX)):
                for c in range(4):
                    step.mark(nc.scalar.activation(dst[:, c, :], bank(4 + 2 * w, 2)[:, c * SEQ:(c + 1) * SEQ],
                                                   ACT.Sigmoid, bias=col(bias + c)))
            evacuate(1, 4, qS[:, 0:2, :])
            step.done(act)
            act.wait_ge(s["lam_s"], 1)
            for c in range(4):
                step.mark(nc.scalar.activation(rga[:, c, :], rgate[:, c, :], ACT.Exp,
                                               scale=lam["neg8"][:, c:c + 1]))
            step.done(act)
            for c in range(4):
                nc.scalar.activation(rgate[:, c, :], rgate[:, c, :], ACT.Tanh,
                                     scale=lam["pos8"][:, c:c + 1]).then_inc(s["rg_act"], 1)
            evacuate(1, 5, qS[:, 2:4, :])
            act.wait_ge(s["rg_q"], 1)
            nc.scalar.activation(rgate[:, :, :], rgate[:, :, :], ACT.Sqrt).then_inc(s["rg_sqrt"], 1)
            evacuate(1, 6, kS[:, 0:2, :])
            evacuate(1, 7, kS[:, 2:4, :])
            for v in range(8, 10):
                evacuate(1, v, vS[:, :, (v % 2) * SEQ:(v % 2 + 1) * SEQ])
            for c in range(4):
                act.wait_ge(s["rg_y"], c + 1)
                nc.scalar.activation(hT[0][:, c, :], xc[:, c, :], ACT.Copy).then_inc(s["rg_high"], 1)
            act.wait_ge(s["bb_ready"], 4)
            for b in range(4):
                act.wait_ge(s["z_evac"], b + 1)
                step.mark(nc.scalar.activation(lg[b], zs[:, b, :, :], ACT.Abs))
            for b in range(4):
                if b == 0:
                    step.done(act)
                step.mark(nc.scalar.activation(lg[b], lg[b], ACT.Exp, scale=-1.0))
            step.done(act)
            for b in range(4):
                nc.scalar.activation(lg[b], lg[b], ACT.Ln, bias=1.0).then_inc(s["z_log"], 1)

            def stick_high(b):
                act.wait_ge(s["sbo_psum"], b + 1)
                nc.scalar.activation(hT[0][:, 4 + b, :], bank(STICK_OUT[b])[:, 0:SEQ], ACT.Copy) \
                  .then_inc(s["sbo_high"], 1)

            for b in range(4):
                act.wait_ge(s["t_ready"], b + 1)
                nc.scalar.activation(zs[:, b, :, :], zs[:, b, :, :], ACT.Exp).then_inc(s["w_ready"], 1)
                if b:
                    stick_high(b - 1)
            stick_high(3)
            out_splits(1)
            warm_sqrt()
            norm(4)
            act.dma_start(cc[:, 0:2, :, :], a["cc"]).then_inc(s["cd_loaded"], 16)
            act.dma_start(glu, a["glu"]).then_inc(s["cd_loaded"], 16)
            norm_out(4)
            next_splits(2)
            ffn(2)
            warm_sqrt()
            norm(5)
            norm_out(5)

            for v in range(8):
                u = v % 2
                dst = ((uT, qM, kM)[v // 2][:, 2 * u:2 * u + 2, :] if v < 6
                       else vM[:, :, u * SEQ:(u + 1) * SEQ])
                evacuate(2, v, dst)
            act.wait_ge(s["s5_scan"], 2 * S5_TILES)
            act.dma_start(biasM, a["biasM"]).then_inc(s["biasM_loaded"], 16)
            for c in range(4):
                act.wait_ge(s["y_sum"], c + 1)
                nc.scalar.activation(yT[:, c, :], yT[:, c, :], ACT.Gelu_apprx_tanh).then_inc(s["y_gelu"], 1)
            for c in range(4):
                act.wait_ge(s["glu_psum"], c + 1)
                nc.scalar.activation(uT[:, c, :], bank(4 + c)[:, 0:SEQ], ACT.Sigmoid,
                                     bias=col(COL_GLUB + c)).then_inc(s["glu_sig"], 1)
            for c in range(4):
                act.wait_ge(s["s5_y"], c + 1)
                nc.scalar.activation(hT[0][:, c, :], yT[:, c, :], ACT.Copy).then_inc(s["s5_high"], 1)
            attention(heads2)
            out_splits(2)
            warm_sqrt()
            norm(6)
            norm_out(6)
            next_splits(3)
            ffn(3)
            warm_sqrt()
            norm(7)

        @block.vector
        def _(dve):
            step = Step(s["dve_step"])

            def gu_low(g):
                dve.wait_ge(s["gu_high"], g + 1)
                nc.vector.tensor_tensor(gu[1][:, g % 2, :], gu_raw[:, g % 2, :], gu[0][:, g % 2, :],
                                        ALU.subtract).then_inc(s["gu_split"], 1)

            def out_splits(m):
                for u in range(MIX_OUT - 1):
                    gu_low(MIX_ITEM[m] + MIX_IN[m] + u + 2)

            def next_splits(f):
                if f:
                    gu_low(FFN_ITEM[f] + 1)
                dve.wait_ge(s["dn_high"], FCH * f + 1)
                nc.vector.tensor_tensor(dn[1][:, 0, :], dn_raw[:, 0, :], dn[0][:, 0, :], ALU.subtract) \
                  .then_inc(s["dn_split"], 1)

            def low_of(c, src, name, value, done):
                dve.wait_ge(s[name], value)
                nc.vector.tensor_tensor(hT[1][:, c, :], src, hT[0][:, c, :], ALU.subtract) \
                  .then_inc(s[done], 1)

            def norm_tile(n, t):
                dve.wait_ge(s["std_ready"], TT * n + t + 1)
                rinv = st["rinv"][:, t:t + 1]
                step.mark(nc.vector.reciprocal(rinv, st["std"][:, t:t + 1]))
                step.done(dve)
                nc.vector.tensor_scalar(diag[:, t, :], ident[:, :], rinv, None, ALU.mult) \
                  .then_inc(s["diag_ready"], 1)

            def norm_low(n):
                for c in range(KC):
                    dve.wait_ge(s["hT_high"], KC * n + c // 2 * 2 + 2)
                    nc.vector.scalar_tensor_tensor(
                        hT[1][:, c, :], bank(4 + c // 2)[:, c % 2 * SEQ:(c % 2 + 1) * SEQ],
                        col(COL_GAIN + n * KC + c), hT[0][:, c, :], ALU.mult, ALU.subtract) \
                      .then_inc(s["hT_low"], 1)

            def norm_final():
                dve.wait_ge(s["gpost_final"], 16)
                for t in range(TT):
                    dve.wait_ge(s["std_ready"], TT * N_NORM + t + 1)
                    rinv = st["rinv"][:, t:t + 1]
                    step.mark(nc.vector.reciprocal(rinv, st["std"][:, t:t + 1]))
                    step.done(dve)
                    for half in range(2):
                        hs = slice(half * 512, (half + 1) * 512)
                        nc.vector.scalar_tensor_tensor(postw[:, t, hs], x[:, t, hs], rinv,
                                                       gpost[:, 1, hs], ALU.mult, ALU.mult) \
                          .then_inc(s["final_ready"], 1)

            def ffn(f, side={}):
                base, G0 = FFN_ITEM[f], FCH * f

                def step_of(i, r=None):
                    plain, arrived = during(i, r)
                    h, static = i % 2, r is None
                    dve.wait_ge(s["silu_ready"], plain(G0 + 1))
                    dve.wait_ge(s["up_ready"], plain(G0 + 1))
                    if not static or G0 + i >= 2:
                        dve.wait_ge(s["act_ready"], plain(G0 - 1))
                    nc.vector.tensor_tensor(prod_s[:, h, :], sil_s[:, h, :], bank(6 + h)[:, 0:SEQ],
                                            ALU.mult).then_inc(s["prod_done"], 1)
                    dve.wait_ge(s["prod_done"], plain(G0 + 1))
                    if not static or G0 + i >= 2:
                        dve.wait_ge(s["down_done"], plain(G0 - 1))
                    nc.vector.tensor_copy(act_s[0][:, h, :], prod_s[:, h, :]).then_inc(s["act_high"], 1)
                    dve.wait_ge(s["act_high"], plain(G0 + 1))
                    nc.vector.tensor_tensor(act_s[1][:, h, :], prod_s[:, h, :], act_s[0][:, h, :],
                                            ALU.subtract).then_inc(s["act_ready"], 1)
                    if not static or i < FCH - 1:
                        dve.wait_ge(s["dn_high"], plain(G0 + 2))
                        nc.vector.tensor_tensor(dn[1][:, 1 - h, :], dn_raw[:, 1 - h, :],
                                                dn[0][:, 1 - h, :], ALU.subtract) \
                          .then_inc(s["dn_split"], 1)
                    sl = (base + i) % 2
                    if not static or base + i + 2 < N_ITEMS:
                        dve.wait_ge(s["gu_high"], plain(base + 3))
                        nc.vector.tensor_tensor(gu[1][:, sl, :], gu_raw[:, sl, :], gu[0][:, sl, :],
                                                ALU.subtract).then_inc(s["gu_split"], 1)

                step_of(0)
                step_of(1)
                first = 2
                for i in range(2, FCH, 2):
                    if i < FCH - 2 and not (side.keys() & {i, i + 1}):
                        continue
                    if i > first:
                        with dve.Fori(first // 2, i // 2) as r:
                            for h in range(2):
                                step_of(h, r)
                    for k in (i, i + 1):
                        step_of(k)
                        if k in side:
                            side[k]()
                    first = i + 2

            def post_normed(p):
                dve.wait_ge(*((s["gpost_loaded"], 32) if p < 2 else (s["gpost_ffn2"], 16)))
                halves = [slice(0, 512), slice(512, 1024)]
                for t in range(TT):
                    wait_out(dve, p, t)
                    for half in (1, 0):
                        hs = halves[half]
                        if half == 0:
                            dve.wait_ge(s["psq_done"], 4 * p + 2 * t + 1)
                        nc.vector.tensor_tensor(postw[:, t, hs], bank(2 * t + half), gpost[:, p % 2, hs],
                                                ALU.mult).then_inc(s["gained"], 1)
                for t in range(TT):
                    dve.wait_ge(s["pstd_ready"], TT * p + t + 1)
                    rinv = st["prinv"][:, t:t + 1]
                    step.mark(nc.vector.reciprocal(rinv, st["pstd"][:, t:t + 1]))
                    dve.wait_ge(s["gained"], 4 * p + 2 * t + 2)
                    step.done(dve)
                    for half in range(2):
                        hs = halves[half]
                        nc.vector.scalar_tensor_tensor(x[:, t, hs], postw[:, t, hs], rinv, x[:, t, hs],
                                                       ALU.mult, ALU.add).then_inc(s["x_ready"], 1)
                        if (t, half) == (1, 0):
                            norm_tile(p + 1, 0)
                norm_tile(p + 1, 1)

            def post_plain(p):
                for t in range(TT):
                    wait_out(dve, p, t)
                    for half in range(2):
                        hs = slice(half * 512, (half + 1) * 512)
                        nc.vector.tensor_tensor(x[:, t, hs], x[:, t, hs], bank(2 * t + half), ALU.add) \
                          .then_inc(s["x_ready"], 1)
                        if (t, half) == (1, 0) and p + 1 < N_NORM:
                            norm_tile(p + 1, 0)
                if p + 1 < N_NORM:
                    norm_tile(p + 1, 1)

            def attention(heads):
                first, last = heads[0]["a"], heads[-1]["a"]
                for e in range(first, last + 4):
                    if e == first and heads[0]["bias"] is not None:
                        dve.wait_ge(s["biasM_loaded"], 16)
                    if e <= last:
                        h = heads[e - first]
                        n_ = h["a"]
                        scores = bank(e % 3)
                        dve.wait_ge(s["s_ready"], e + 1)
                        if h["bias"] is None:
                            step.mark(nc.vector.tensor_reduce(
                                stat[:, n_, 0:2], scores.rearrange("p (t k) -> p t k", t=TT), AX.X, ALU.max))
                            step.done(dve)
                            nc.vector.tensor_scalar(stat[:, n_, 0:2], stat[:, n_, 0:2], -h["scale"], None,
                                                    ALU.mult).then_inc(s["max_ready"], 1)
                        else:
                            if e >= first + 2 and heads[e - first - 2]["bias"] is not None:
                                dve.wait_ge(s["p_ready"], e - 1)
                            for t in range(TT):
                                step.mark(nc.vector.tensor_tensor_reduce(
                                    out=h["exp_in"][:, t * SEQ:(t + 1) * SEQ],
                                    in0=scores[:, t * SEQ:(t + 1) * SEQ], in1=h["bias"][:, t, :],
                                    scale=h["scale"], scalar=-3e38, op0=ALU.add, op1=ALU.max,
                                    accum_out=stat[:, n_, t:t + 1]))
                            step.done(dve)
                            nc.vector.tensor_scalar(stat[:, n_, 0:2], stat[:, n_, 0:2], -1.0, None,
                                                    ALU.mult).then_inc(s["max_ready"], 1)
                    g = e - 1
                    if first <= g <= last:
                        h = heads[g - first]
                        dve.wait_ge(s["p_ready"], g + 1)
                        step.mark(nc.vector.reciprocal(stat[:, h["a"], 2:4], stat[:, h["a"], 2:4]))
                        step.done(dve)
                        for t in range(TT):
                            pr = h["probs"][:, t * SEQ:(t + 1) * SEQ]
                            i = nc.vector.tensor_scalar(pr, pr, stat[:, h["a"], 2 + t:3 + t], None, ALU.mult)
                        i.then_inc(s["pn_ready"], 1)
                    g = e - 3
                    if first <= g <= last and heads[g - first]["heads_out"] is not None:
                        src, c = heads[g - first]["heads_out"]
                        done = c + 1 if first == 0 else 8 + c - 3
                        low_of(c, src, "o_high", done, "o_ready")

            dve.wait_ge(s["early_loaded"], 32)
            for t in range(TT):
                norm_tile(0, t)
            gu_low(0)
            norm_low(0)
            gu_low(1)
            next_splits(0)
            ffn(0)
            post_normed(0)
            norm_low(1)
            dve.wait_ge(s["late_loaded"], 64)
            for tab, g in ((rope_q, 0), (rope_k, 2)):
                for part in range(2):
                    nh = tab.shape[3]
                    for t in range(TT):
                        i = nc.vector.tensor_tensor(
                            tab[:, part, t, :, :],
                            axial[:, part, t, :].unsqueeze(1).broadcast_to([P, nh, HD]),
                            qkg[:, g + part, :].unsqueeze(1).broadcast_to([P, nh, HD]), ALU.mult)
            i.then_inc(s["tables_ready"], 1)
            dve.wait_ge(s["tables_ready"], 1)
            dve.wait_ge(s["lam_den"], 1)
            nc.vector.reciprocal(lam["den"], lam["den"]).then_inc(s["lam_rden"], 1)
            dve.wait_ge(s["s5_arg"], 1)
            nc.vector.reciprocal(s5c[:, 2, :], chw[:, 4, :]).then_inc(s["s5_rden"], 1)

            def flat(tab):
                return tab.rearrange("p t h d -> p (t h d)")

            for r in range(7):
                gu_low(MIX_ITEM[0] + r + 2)
                nh = TT * rope_heads(r)
                w = nh * HD
                src = raw[:, r % 2, 0:w]
                dve.wait_ge(s["raw_ready"], r + 1)
                if r >= 1:
                    dve.wait_ge(s["rop_ready"], r)
                if r < 3:
                    step.mark(nc.vector.tensor_tensor(t1[:, 0:w], src, src, ALU.mult))
                    step.done(dve)
                    step.mark(nc.vector.tensor_reduce(qk["ss"][:, 0:nh],
                                                      t1[:, 0:w].rearrange("p (h d) -> p h d", d=HD),
                                                      AX.X, ALU.add))
                    step.done(dve)
                    nc.vector.tensor_scalar(qk["var"][:, 0:nh], qk["ss"][:, 0:nh], 1.0 / HD, EPS,
                                            ALU.mult, ALU.add).then_inc(s["qkvar_ready"], 1)
                    dve.wait_ge(s["qkstd_ready"], r + 1)
                    step.mark(nc.vector.reciprocal(qk["rinv"][:, 0:nh], qk["std"][:, 0:nh]))
                    step.done(dve)
                    nc.vector.tensor_tensor(xn1[:, 0:w].rearrange("p (h d) -> p h d", d=HD),
                                            src.rearrange("p (h d) -> p h d", d=HD),
                                            qk["rinv"][:, 0:nh].unsqueeze(2).broadcast_to([P, nh, HD]),
                                            ALU.mult).then_inc(s["xn_ready"], 1)
                    dve.wait_ge(s["xn_ready"], r + 1)
                    src = xn1[:, 0:w]
                cos = flat((rope_q if r < 2 else rope_k if r == 2 else rope_b)[:, 0])
                step.mark(nc.vector.tensor_tensor(t1[:, 0:w], src, cos, ALU.mult))
                step.done(dve)
                dve.wait_ge(s["t2_ready"], 2 * (r + 1))
                if r >= 2:
                    dve.wait_ge(s["ropT_psum"], r - 1)
                nc.vector.tensor_tensor(rop[:, r % 2, 0:w], t1[:, 0:w], t2[:, 0:w], ALU.add) \
                  .then_inc(s["rop_ready"], 1)
            for v in (7, 8):
                gu_low(MIX_ITEM[0] + v + 2)
            attention(heads1)
            out_splits(0)
            post_normed(1)
            norm_low(2)
            next_splits(1)
            ffn(1)
            post_normed(2)
            norm_low(3)

            for v in range(2):
                gu_low(MIX_ITEM[1] + v + 2)
            wait_unit(dve, 1, 1)
            dve.wait_ge(s["zeroed"], 1)
            for c in range(4):
                step.mark(nc.vector.tensor_scalar(xc[:, c, :], xr[:, c, 0:SEQ], col(COL_CONV + c),
                                                  col(COL_CONVB + c), ALU.mult, ALU.add))
            for tap in range(1, 4):
                step.done(dve)
                for c in range(4):
                    i = nc.vector.scalar_tensor_tensor(xc[:, c, :], xr[:, c, tap:tap + SEQ],
                                                       col(COL_CONV + 4 * tap + c), xc[:, c, :],
                                                       ALU.mult, ALU.add)
                    if tap < 3:
                        step.mark(i)
                    else:
                        i.then_inc(s["conv_done"], 1)
            for v in range(2, 5):
                gu_low(MIX_ITEM[1] + v + 2)
            dve.wait_ge(s["rg_act"], 4)
            asq = xr[:, :, 0:SEQ]
            step.mark(nc.vector.tensor_tensor(asq, rga[:, :, :], rga[:, :, :], ALU.mult))
            step.done(dve)
            step.mark(nc.vector.scalar_tensor_tensor(rgate[:, :, :], asq, 1.0, rgate[:, :, :],
                                                     ALU.add, ALU.mult))
            step.done(dve)
            nc.vector.tensor_scalar(rgate[:, :, :], rgate[:, :, :], 1e-34, None, ALU.max) \
              .then_inc(s["rg_q"], 1)
            gu_low(MIX_ITEM[1] + 5 + 2)
            dve.wait_ge(s["rg_sqrt"], 1)
            dve.wait_ge(s["rg_ix"], 1)
            step.mark(nc.vector.tensor_tensor(rgate[:, :, :], rgate[:, :, :], igate[:, :, :], ALU.mult))
            step.done(dve)
            for c in range(4):
                step.mark(nc.vector.tensor_tensor_scan(xc[:, c, :], rga[:, c, :], rgate[:, c, :], 0.0,
                                                       ALU.mult, ALU.add))
            gu_low(MIX_ITEM[1] + 6 + 2)
            step.done(dve)
            wait_unit(dve, 1, 3)
            for c in range(4):
                nc.vector.tensor_tensor(xc[:, c, :], xc[:, c, :], gg[:, c, :], ALU.mult) \
                  .then_inc(s["rg_y"], 1)
            gu_low(MIX_ITEM[1] + 7 + 2)
            dve.wait_ge(s["rg_y"], 4)
            dve.wait_ge(s["ab_loaded"], 48)

            def both_banks(b):
                return bank(STICK_BANK[b], 2).rearrange("p (e q) -> p e q", e=2)[:, :, 0:384]

            def stick_mask(b):
                dve.wait_ge(s["z_psum"], b + 1)
                nc.vector.scalar_tensor_tensor(zs[:, b, :, :], both_banks(b), HD ** -0.5,
                                               mask.unsqueeze(1).broadcast_to([P, 2, 384]),
                                               ALU.mult, ALU.add).then_inc(s["z_evac"], 1)

            gu_low(MIX_ITEM[1] + 8 + 2)
            stick_mask(0)
            gu_low(MIX_ITEM[1] + 9 + 2)
            for b in range(1, 4):
                stick_mask(b)
            for c in range(4):
                low_of(c, xc[:, c, :], "rg_high", c + 1, "rg_done")
            for b in range(4):
                dve.wait_ge(s["z_log"], b + 1)
                nc.vector.scalar_tensor_tensor(lg[b], zs[:, b, :, :], 0.0, lg[b], ALU.max, ALU.add) \
                  .then_inc(s["sp_ready"], 1)
            for b in range(4):
                dve.wait_ge(s["r_psum"], b + 1)
                nc.vector.tensor_tensor(zs[:, b, :, :], zs[:, b, :, :], both_banks(b), ALU.subtract) \
                  .then_inc(s["t_ready"], 1)
                if b >= 2:
                    low_of(2 + b, bank(STICK_OUT[b - 2])[:, 0:SEQ], "sbo_high", b - 1, "sbo_done")
            for b in range(2, 4):
                low_of(4 + b, bank(STICK_OUT[b])[:, 0:SEQ], "sbo_high", b + 1, "sbo_done")
            out_splits(1)
            post_plain(3)
            norm_low(4)
            next_splits(2)
            ffn(2)
            post_plain(4)
            norm_low(5)

            dve.wait_ge(s["trig"], 8)

            def both(tab, j):
                return tab[:, j, :].unsqueeze(1).broadcast_to([P, 2, SEQ])

            def s5_modulate(j):
                dve.wait_ge(s["bu_done"], j + 1)
                if j >= 2:
                    dve.wait_ge(s["s5_scan"], 2 * (j - 1))
                bu = bank(4 + j % 2).rearrange("p (h s) -> p h s", h=2)
                nc.vector.tensor_tensor(pc[:, j % 2, :, :], bu, both(tabC, j), ALU.mult) \
                  .then_inc(s["s5_mod"], 1)
                nc.vector.tensor_tensor(pw[:, j % 2, :, :], bu, both(tabS, j), ALU.mult) \
                  .then_inc(s["s5_mod"], 1)

            for v in range(2):
                gu_low(MIX_ITEM[2] + v + 2)
            s5_modulate(0)
            for j in range(S5_TILES):
                if j + 1 < S5_TILES:
                    s5_modulate(j + 1)
                dve.wait_ge(s["zin_ready"], 2 * (j + 1))
                if j >= 2:
                    dve.wait_ge(s["s5_dem"], 2 * (j - 1))
                for h in range(2):
                    nc.vector.tensor_tensor_scan(zz[:, j % 2, h, :],
                                                 s5s["mag"][:, j:j + 1].broadcast_to([P, SEQ]),
                                                 pc[:, j % 2, h, :], 0.0, ALU.mult, ALU.add) \
                      .then_inc(s["s5_scan"], 1)
                if j % 2 == 0 and 2 <= j < 14:
                    gu_low(MIX_ITEM[2] + j // 2 + 3)
            dve.wait_ge(s["y_done"], S5_TILES)
            for c in range(4):
                nc.vector.scalar_tensor_tensor(yT[:, c, :], uT[:, c, :], col(COL_DSKIP + c),
                                               bank(6, 2)[:, c * SEQ:(c + 1) * SEQ], ALU.mult, ALU.add) \
                  .then_inc(s["y_sum"], 1)
            dve.wait_ge(s["glu_psum"], 4)
            for c in range(4):
                dve.wait_ge(s["glu_sig"], c + 1)
                nc.vector.tensor_tensor(yT[:, c, :], yT[:, c, :], uT[:, c, :], ALU.mult) \
                  .then_inc(s["s5_y"], 1)
            for c in range(4):
                low_of(c, yT[:, c, :], "s5_high", c + 1, "s5_done")
            attention(heads2)
            out_splits(2)
            post_plain(5)
            norm_low(6)
            next_splits(3)
            ffn(3)
            post_plain(6)
            norm_final()

        @block.gpsimd
        def _(pool):
            step = Step(s["pool_step"])

            def tt(out, in0, in1, op):
                step.mark(nc.gpsimd.tensor_tensor(out, in0, in1, op))
                step.done(pool)

            def ts(out, in0, s1, s2, op0, op1):
                step.mark(nc.gpsimd.tensor_scalar(out, in0, s1, s2, op0, op1))
                step.done(pool)

            def reduce_angle(ang, k, t, parts):
                ts(k, ang, 1.0 / TWO_PI, MAGIC, ALU.mult, ALU.add)
                for part in parts:
                    ts(t, k, MAGIC, -part, ALU.subtract, ALU.mult)
                    tt(ang, ang, t, ALU.add)

            pool.wait_ge(s["exp_dt"], 2)
            pool.wait_ge(s["early_loaded"], 32)
            pool.wait_ge(s["s5c_loaded"], 16)
            A = [chw[:, k, :] for k in range(8)]
            lr, li, dt, br, bi = (s5c[:, k, :] for k in range(5))
            tt(A[0], lr, dt, ALU.mult)
            tt(A[1], li, dt, ALU.mult)
            reduce_angle(A[1], A[4], A[5], (C1, C2, C3))
            ts(A[1], A[1], 3.1415925, -3.1415925, ALU.min, ALU.max)
            tt(s5s["mag"], col(COL_LR, S5_TILES), s5s["dt"], ALU.mult)
            tt(s5s["th"], col(COL_LI, S5_TILES), s5s["dt"], ALU.mult)
            reduce_angle(s5s["th"], s5s["k"], s5s["t"], (C1, C2, C3))
            tt(A[4], lr, lr, ALU.mult)
            tt(A[5], li, li, ALU.mult)
            nc.gpsimd.tensor_tensor(A[4], A[4], A[5], ALU.add).then_inc(s["s5_arg"], 1)
            pool.wait_ge(s["lam_e"], 1)
            nc.gpsimd.tensor_scalar(lam["den"], lam["e"], 2.0, None, ALU.add, ALU.bypass) \
              .then_inc(s["lam_den"], 1)
            pool.wait_ge(s["x_ready"], 4)
            pool.dma_start(gpost[:, 0, :], a["ffn2_post_g"].partition_broadcast(P)) \
                .then_inc(s["gpost_ffn2"], 16)

            pool.wait_ge(s["tables_ready"], 1)
            for r in range(7):
                w = TT * rope_heads(r) * HD
                if r < 3:
                    pool.wait_ge(s["xn_ready"], r + 1)
                    src, tab, cut_ = xn1[:, 0:w], rope_q if r < 2 else rope_k, "p (h b j) -> p b h j"
                    J = HD // 4
                else:
                    pool.wait_ge(s["raw_ready"], r + 1)
                    src, tab, cut_ = raw[:, r % 2, 0:w], rope_b, "p (h b j) -> p b h j"
                    J = HD // 2
                if r >= 1:
                    pool.wait_ge(s["rop_ready"], r)
                sin = tab[:, 1].rearrange("p t h d -> p (t h d)")
                for b in range(2):
                    nc.gpsimd.tensor_tensor(t2[:, 0:w].rearrange(cut_, b=2, j=J)[:, b],
                                            src.rearrange(cut_, b=2, j=J)[:, 1 - b],
                                            sin.rearrange(cut_, b=2, j=J)[:, b], ALU.mult) \
                      .then_inc(s["t2_ready"], 1)
            pool.wait_ge(s["x_ready"], 8)
            pool.dma_start(gpost[:, 1, :], a["final_norm"].partition_broadcast(P)) \
                .then_inc(s["gpost_final"], 16)

            pool.wait_ge(s["lam_rden"], 1)
            tt(lam["s"], lam["e"], lam["den"], ALU.mult)
            tt(lam["s2"], lam["s"], lam["s"], ALU.mult)
            ts(lam["acc"], lam["s2"], 1.0 / 17, 1.0 / 15, ALU.mult, ALU.add)
            for k in range(6, -1, -1):
                tt(lam["acc"], lam["acc"], lam["s2"], ALU.mult)
                ts(lam["acc"], lam["acc"], 1.0 / (2 * k + 1), None, ALU.add, ALU.bypass)
            tt(lam["acc"], lam["acc"], lam["s"], ALU.mult)
            ts(lam["pos"], col(COL_LAM, 4), -1.0, 0.0, ALU.mult, ALU.max)
            ts(lam["acc"], lam["acc"], 2.0, None, ALU.mult, ALU.bypass)
            tt(lam["acc"], lam["acc"], lam["pos"], ALU.add)
            ts(lam["neg8"], lam["acc"], -8.0, None, ALU.mult, ALU.bypass)
            nc.gpsimd.tensor_scalar(lam["pos8"], lam["acc"], 8.0, None, ALU.mult, ALU.bypass) \
              .then_inc(s["lam_s"], 1)

            pool.wait_ge(s["s5_rden"], 1)
            for jb in range(4):
                g = slice(4 * jb, 4 * jb + 4)
                for j in range(4 * jb, 4 * jb + 4):
                    step.mark(nc.gpsimd.tensor_scalar(tabS[:, j, :], trow[:, :], s5s["th"][:, j:j + 1],
                                                      None, ALU.mult))
                step.done(pool)
                ang, k, t = tabS[:, g, :], tabC[:, g, :], chw[:, 4:8, :]
                reduce_angle(ang, k, t, (C1, C2))
                nc.gpsimd.tensor_scalar(ang, ang, 3.1415925, -3.1415925, ALU.min, ALU.max) \
                  .then_inc(s["angles"], 1)
            pool.wait_ge(s["s5_trig"], 4)
            pool.wait_ge(s["s5_rden"], 1)
            mag, sn, cs = A[0], A[2], A[3]
            tt(cs, mag, cs, ALU.mult)
            ts(cs, cs, 1.0, None, ALU.subtract, ALU.bypass)
            tt(sn, mag, sn, ALU.mult)
            tt(A[4], cs, lr, ALU.mult)
            tt(A[5], sn, li, ALU.mult)
            tt(A[4], A[4], A[5], ALU.add)
            tt(A[5], sn, lr, ALU.mult)
            tt(A[6], cs, li, ALU.mult)
            tt(A[5], A[5], A[6], ALU.subtract)
            tt(A[4], A[4], dt, ALU.mult)
            tt(A[5], A[5], dt, ALU.mult)
            tt(A[0], A[4], br, ALU.mult)
            tt(A[1], A[5], bi, ALU.mult)
            tt(A[0], A[0], A[1], ALU.subtract)
            tt(A[1], A[4], bi, ALU.mult)
            tt(A[2], A[5], br, ALU.mult)
            tt(A[1], A[1], A[2], ALU.add)
            for part in range(2):
                for g in range(2):
                    nc.gpsimd.tensor_scalar(bb[:, part, :, g, :],
                                            A[part].rearrange("p (c n) -> p c n", n=HD),
                                            col(COL_SEL + g), None, ALU.mult).then_inc(s["bb_ready"], 1)
            pool.wait_ge(s["x_ready"], 12)
            nc.gpsimd.memset(xr[:, :, 0:3], 0.0).then_inc(s["zeroed"], 1)
            pool.wait_ge(s["rg_act"], 4)
            nc.gpsimd.tensor_tensor(igate[:, :, :], igate[:, :, :], xc[:, :, :], ALU.mult) \
              .then_inc(s["rg_ix"], 1)
            pool.wait_ge(s["cd_loaded"], 32)
            tt_ = nc.gpsimd.tensor_scalar
            tt_(cc[:, 2, :, :], cc[:, 0, :, :], -1.0, None, ALU.mult)
            tt_(cc[:, 1, :, :], cc[:, 1, :, :], -1.0, None, ALU.mult).then_inc(s["cc_ready"], 1)

            def s5_sum(j):
                pool.wait_ge(s["s5_mod"], 2 * (j + 1))
                r = j % 2
                nc.gpsimd.tensor_tensor(pc[:, r, 0, :], pc[:, r, 0, :], pw[:, r, 1, :], ALU.add) \
                  .then_inc(s["zin_ready"], 1)
                nc.gpsimd.tensor_tensor(pc[:, r, 1, :], pc[:, r, 1, :], pw[:, r, 0, :], ALU.subtract) \
                  .then_inc(s["zin_ready"], 1)

            s5_sum(0)
            for j in range(S5_TILES):
                if j + 1 < S5_TILES:
                    s5_sum(j + 1)
                pool.wait_ge(s["s5_scan"], 2 * (j + 1))
                if j >= 2:
                    pool.wait_ge(s["y_done"], j - 1)
                for dst, tab in ((dC, tabC), (dS, tabS)):
                    nc.gpsimd.tensor_tensor(dst[:, j % 2, :, :], zz[:, j % 2, :, :],
                                            tab[:, j, :].unsqueeze(1).broadcast_to([P, 2, SEQ]),
                                            ALU.mult).then_inc(s["s5_dem"], 1)


def kernel(**inputs):
    import concourse.bacc as bacc
    from concourse.bass_utils import run_bass_kernel_spmd

    w = {k: np.asarray(v) for k, v in inputs.items()}
    f32 = np.float32

    def by_rows(m):
        return m.reshape(-1, P, m.shape[1]).transpose(1, 0, 2)

    def ffn_gu(gate, up):
        return np.stack([by_rows(m).reshape(P, KC, FCH, P) for m in (gate, up)], axis=1) \
                 .transpose(3, 0, 1, 2, 4).reshape(FCH, P, GU)

    def mix_gu(blocks):
        wide = np.concatenate(blocks, axis=1)
        return by_rows(wide).reshape(P, KC, -1, SEQ).transpose(2, 0, 1, 3).reshape(-1, P, GU)

    pairs = [c + 4 * e for c in range(4) for e in range(2)]
    qkv, wo = w["w_qkv"][0], w["w_out"][0]
    qa = qkv[:, :512].reshape(D, 8, HD)[:, pairs].reshape(D, 512)
    wo = np.concatenate([wo[:512].reshape(8, HD, D)[pairs].reshape(512, D), wo[512:]])
    ab, cd = w["ab_w_in_2"][0], w["cd_w_in_2"][0]
    wgu = np.concatenate([
        ffn_gu(w["ffn1_w_gate"][0], w["ffn1_w_up"][0]),
        mix_gu([qa, qkv[:, 512:], wo]),
        ffn_gu(w["ffn2_w_gate"][0], w["ffn2_w_up"][0]),
        mix_gu([ab, w["ab_w_out_2"][0]]),
        ffn_gu(w["ffn_w_gate_2"][0], w["ffn_w_up_2"][0]),
        mix_gu([cd, w["cd_w_out_2"][0]]),
        ffn_gu(w["ffn_w_gate_2"][1], w["ffn_w_up_2"][1])])
    wdn = np.concatenate([w[n][i] for n, i in (("ffn1_w_down", 0), ("ffn2_w_down", 0),
                                               ("ffn_w_down_2", 0), ("ffn_w_down_2", 1))])
    wdn = wdn.reshape(4 * FCH, P, D)

    def column(v):
        return v.reshape(-1, P).T

    G, N, PG = 32, 64, 16
    lr, li, ldt = w["cd_lam_re_2"][0], w["cd_lam_im_2"][0], w["cd_log_dt_2"][0]
    ldt_n = np.broadcast_to(ldt[:, None], (G, N))
    in_quadrant = (np.arange(P) % 32) // PG
    cols = np.concatenate(
        [column(g) for g in (w["ffn1_pre_g"], w["mix_pre_g"], w["ffn2_pre_g"], w["ab_norm_2"],
                             w["ffn_norm_2"][0], w["cd_norm_2"], w["ffn_norm_2"][1])]
        + [column(w["ab_conv_w_2"]), column(w["ab_conv_b_2"]), column(w["ab_gate_a_b_2"]),
           column(w["ab_gate_x_b_2"]), column(w["ab_lambda_2"]), column(w["cd_d_2"]),
           column(w["cd_glu_b_2"]), column(lr), column(li), column(ldt_n),
           np.stack([in_quadrant == 0, in_quadrant == 1], 1).astype(f32),
           np.full((P, 1), math.pi / 2, f32), np.full((P, 1), EPS, f32),
           np.full((P, 1), 4 * EPS, f32)], axis=1)

    def by_channel(v):
        return np.repeat(v.reshape(4, 8, N).transpose(1, 0, 2), PG, axis=0).reshape(P, 4 * N)

    def b_by_channel(b):
        return b.reshape(4, 8, N, PG).transpose(1, 3, 0, 2).reshape(P, 4 * N)

    s5c = np.stack([by_channel(lr), by_channel(li), by_channel(ldt_n),
                    b_by_channel(w["cd_b_re_2"][0]), b_by_channel(w["cd_b_im_2"][0])], axis=1)
    cc = np.zeros((2, N, 2, S5_TILES, 2, PG), f32)
    for part, name in enumerate(("cd_c_re_2", "cd_c_im_2")):
        c = w[name][0].reshape(S5_TILES, 2, PG, N)
        for g in range(2):
            cc[g, :, part, :, g, :] = c[:, g].transpose(2, 0, 1)
    cc = cc.reshape(P, 2, S5_TILES, 32)
    gates = np.stack([w["ab_gate_a_w_2"][0], w["ab_gate_x_w_2"][0]])
    gates = gates.reshape(2, 4, 2, HD, HD)
    gbd = np.zeros((2, HD, 2, 4, 2, HD), f32)
    for e in range(2):
        gbd[e, :, :, :, e, :] = gates[:, :, e].transpose(2, 0, 1, 3)
    gbd = gbd.reshape(P, 2, 4, P)
    glu = w["cd_glu_w_2"][0].reshape(4, P, 512).transpose(1, 0, 2)
    qg, kg = w["q_norm_g"][0], w["k_norm_g"][0]
    swap = np.arange(HD).reshape(2, 2, 16)[:, ::-1].reshape(HD)
    qkg = np.broadcast_to(np.stack([qg, qg[swap], kg, kg[swap]]), (P, 4, HD))

    t = np.arange(SEQ)

    def angles(pos, dim):
        freqs = (ROPE_THETA ** (-np.arange(0, dim, 2, dtype=f32) / f32(dim))).astype(f32)
        return pos.astype(f32)[:, None] * freqs[None, :]

    def rope_tables(parts):
        cos = np.concatenate([np.cos(x) for x in parts for _ in range(2)], axis=1)
        sin = np.concatenate([sg * np.sin(x) for x in parts for sg in (-1, 1)], axis=1)
        return [m.reshape(TT, P, HD).transpose(1, 0, 2).astype(f32) for m in (cos, sin)]

    axial = np.stack(rope_tables([angles(t // GRID_W, HD // 2), angles(t % GRID_W, HD // 2)]), axis=1)
    rope_b = np.stack(rope_tables([angles(t, HD)]), axis=1)
    rope_b = np.repeat(rope_b[:, :, :, None, :], 4, axis=3)
    s5in = np.concatenate([s5c.reshape(P, 5 * SEQ), np.broadcast_to(t.astype(f32), (P, SEQ))], axis=1)
    diff = t[None, :] - t[:, None]
    count = (np.abs(diff) <= 64).astype(f32)
    for dilation in (4, 16):
        span = {4: 512, 16: 2048}[dilation] // 2
        count += (diff % dilation == 0) & (np.abs(diff) <= span)
    biasB = np.where(count > 0, np.log(np.maximum(count, 1)) * HD ** 0.5, NEG).astype(f32)
    biasB = biasB.reshape(TT, P, SEQ).transpose(1, 0, 2)
    slopes = 2.0 ** (-8.0 * np.arange(1, 5) / 4)
    biasM = np.where(diff <= 0, slopes[:, None, None] * diff * P ** 0.5, NEG).astype(f32)
    biasM = biasM.reshape(4, TT, P, SEQ).transpose(2, 0, 1, 3)
    k = np.arange(P)
    tri = np.stack([k[:, None] >= k[None, :], np.ones((P, P), bool)], axis=1).astype(f32)
    past = k[:, None] < np.concatenate([t, t[:P]])[None, :]
    mask = np.where(past, 0, NEG).astype(f32)

    data = {
        "x": w["x"][0].reshape(TT, P, D).transpose(1, 0, 2), "wgu": wgu, "wdn": wdn,
        "ident": np.eye(P, dtype=f32), "cols": cols, "ffn1_post_g": w["ffn1_post_g"][0],
        "mix_post_g": w["mix_post_g"][0], "ffn2_post_g": w["ffn2_post_g"][0],
        "final_norm": w["final_norm_2"], "s5in": s5in, "biasB": biasB, "axial": axial,
        "rope_b": rope_b, "tri": tri, "mask": mask,
        "biasM": biasM, "glu": glu, "qkg": qkg, "cc": cc, "gbd": gbd,
    }
    nc = bacc.Bacc("TRN2", target_bir_lowering=False, num_devices=1)
    arrays, args = {}, {}
    for name, v in data.items():
        arrays["in_" + name] = np.ascontiguousarray(v)
        args[name] = nc.dram_tensor("in_" + name, v.shape, F32, kind="ExternalInput").ap()
    args["out"] = nc.dram_tensor("out_x", (P, TT, D), F32, kind="ExternalOutput").ap()
    build(nc, args)
    got = run_bass_kernel_spmd(nc, [arrays], core_ids=[0]).results[0]["out_x"]
    return np.asarray(got).reshape(P, TT, D).transpose(1, 0, 2).reshape(1, SEQ, D)
```
